# Optimizing a Trainium2 kernel written in Bass

```python
import math
import jax, jax.numpy as jnp
from jax import lax
import numpy as np

D_MODEL = 1024
BATCH = 1
SEQ = 512
DEPTH = 1

N_HEADS = 16
N_KV_HEADS = 2
GROUP = N_HEADS // N_KV_HEADS
HEAD_DIM = 64
WINDOW = 128
BLOCK = 128
ATTN_SCALE = 1.0 / math.sqrt(HEAD_DIM)
NEG_INF = -1e30
POOL_WINDOWS = (2, 4, 8, 16)
N_POOL_GROUPS = len(POOL_WINDOWS)
POOL_GROUP = 128
POOL_W = N_POOL_GROUPS * POOL_GROUP
Q_W = N_HEADS * HEAD_DIM
KV_W = N_KV_HEADS * HEAD_DIM
IN_W = Q_W + 2 * KV_W + POOL_W + 2 * D_MODEL
SPLITS = (Q_W, Q_W + KV_W, Q_W + 2 * KV_W, Q_W + 2 * KV_W + POOL_W, Q_W + 2 * KV_W + POOL_W + D_MODEL)
PEER_HEADS = 8
N_KEYS = 128
N_EXPERTS = N_KEYS * N_KEYS
D_KEY = 256
D_HALF = D_KEY // 2
PEER_TOPK = 16
PEER_CHUNK = 128
EPS = 1e-5


def rmsnorm(x, g):
    xf = x.astype(jnp.float32)
    y = xf * lax.rsqrt(jnp.mean(xf * xf, axis=-1, keepdims=True) + EPS)
    return (y * g.astype(jnp.float32)).astype(x.dtype)

def sliding_window_attention(q, k, v, sinks):
    b, s = q.shape[0], q.shape[1]
    nblk = s // BLOCK
    kp = jnp.pad(k, ((0, 0), (BLOCK, 0), (0, 0), (0, 0)))
    vp = jnp.pad(v, ((0, 0), (BLOCK, 0), (0, 0), (0, 0)))
    qb = q.reshape(b, nblk, BLOCK, N_KV_HEADS, GROUP, HEAD_DIM).swapaxes(0, 1)
    sink = sinks.astype(jnp.float32).reshape(1, N_KV_HEADS, GROUP, 1, 1)

    def one_block(args):
        i, qi = args
        start = i * BLOCK
        kb = lax.dynamic_slice_in_dim(kp, start, 2 * BLOCK, axis=1)
        vb = lax.dynamic_slice_in_dim(vp, start, 2 * BLOCK, axis=1)
        sc = jnp.einsum('bqhgd,bkhd->bhgqk', qi, kb).astype(jnp.float32) * ATTN_SCALE
        qpos = start + jnp.arange(BLOCK)
        kpos = start - BLOCK + jnp.arange(2 * BLOCK)
        rel = qpos[:, None] - kpos[None, :]
        mask = (rel >= 0) & (rel < WINDOW) & (kpos[None, :] >= 0)
        sc = jnp.where(mask, sc, NEG_INF)
        sc = jnp.concatenate([sc, jnp.broadcast_to(sink, sc.shape[:-1] + (1,))], axis=-1)
        p = jax.nn.softmax(sc, axis=-1)[..., :-1]
        return jnp.einsum('bhgqk,bkhd->bqhgd', p.astype(vb.dtype), vb)

    o = lax.map(one_block, (jnp.arange(nblk), qb))
    return o.swapaxes(0, 1).reshape(b, s, Q_W)

def multiscale_pool(p, w_grp, scale):
    b, s = p.shape[0], p.shape[1]
    pf = p.astype(jnp.float32).reshape(b, s, N_POOL_GROUPS, POOL_GROUP)
    c = jnp.cumsum(pf, axis=1)
    t1 = jnp.arange(1, s + 1, dtype=jnp.float32)
    outs = []
    for j, w in enumerate(POOL_WINDOWS):
        cj = c[:, :, j]
        lag = jnp.pad(cj, ((0, 0), (w, 0), (0, 0)))[:, :s]
        cnt = jnp.minimum(t1, float(w))[None, :, None]
        outs.append((cj - lag) / cnt - pf[:, :, j])
    pooled = jnp.stack(outs, axis=2).astype(p.dtype)
    y = jnp.einsum('bsgc,gcd->bsgd', pooled, w_grp).reshape(b, s, POOL_W)
    return y * scale

def peer(xn, w_query, sub_keys, u_tab, v_tab):
    b, s, d = xn.shape
    xt = xn.reshape((b * s) // PEER_CHUNK, PEER_CHUNK, d)

    def chunk(xc):
        c = xc.shape[0]
        q = (xc @ w_query).reshape(c, PEER_HEADS, 2, D_HALF)
        sc = jnp.einsum('chpd,hpkd->chpk', q, sub_keys).astype(jnp.float32)
        sv, si = lax.top_k(sc, PEER_TOPK)
        cand = (sv[:, :, 0, :, None] + sv[:, :, 1, None, :]).reshape(c, PEER_HEADS, PEER_TOPK * PEER_TOPK)
        cidx = (si[:, :, 0, :, None] * N_KEYS + si[:, :, 1, None, :]).reshape(c, PEER_HEADS, PEER_TOPK * PEER_TOPK)
        fv, fi = lax.top_k(cand, PEER_TOPK)
        idx = jnp.take_along_axis(cidx, fi, axis=-1)
        g = jax.nn.softmax(fv, axis=-1)
        u = u_tab[idx]
        a = jax.nn.gelu(jnp.einsum('chkd,cd->chk', u, xc).astype(jnp.float32), approximate=False)
        vv = v_tab[idx]
        return jnp.einsum('chk,chkd->cd', (g * a).astype(vv.dtype), vv)

    return lax.map(chunk, xt).reshape(b, s, d)

def first_inputs(seed: int = 0) -> dict:
    key = jax.random.key(seed)
    ks = jax.random.split(key, 16)
    f32 = jnp.float32
    L = DEPTH
    nrm = lambda k, shape, std: jax.random.normal(k, shape, f32) * std
    return {
        'x': jax.random.normal(ks[0], (BATCH, SEQ, D_MODEL), f32),
        'ln_mix_g': 1.0 + nrm(ks[1], (L, D_MODEL), 0.05),
        'w_in': nrm(ks[2], (L, D_MODEL, IN_W), D_MODEL ** -0.5),
        'b_in': nrm(ks[3], (L, IN_W), 0.02),
        'attn_sinks': nrm(ks[4], (L, N_HEADS), 0.5),
        'w_attn_up': nrm(ks[5], (L, Q_W, D_MODEL), Q_W ** -0.5),
        'w_pool_grp': nrm(ks[6], (L, N_POOL_GROUPS, POOL_GROUP, POOL_GROUP), POOL_GROUP ** -0.5),
        'pool_scale': 1.0 + nrm(ks[7], (L, POOL_W), 0.1),
        'w_pool_up': nrm(ks[8], (L, POOL_W, D_MODEL), POOL_W ** -0.5),
        'w_o': nrm(ks[9], (L, D_MODEL, D_MODEL), D_MODEL ** -0.5),
        'ln_ffn_g': 1.0 + nrm(ks[10], (L, D_MODEL), 0.05),
        'w_query': nrm(ks[11], (L, D_MODEL, PEER_HEADS * D_KEY), D_MODEL ** -0.5),
        'sub_keys': nrm(ks[12], (L, PEER_HEADS, 2, N_KEYS, D_HALF), D_HALF ** -0.5),
        'u_experts': nrm(ks[13], (L, N_EXPERTS, D_MODEL), D_MODEL ** -0.5),
        'v_experts': nrm(ks[14], (L, N_EXPERTS, D_MODEL), PEER_HEADS ** -0.5),
        'ln_final_g': 1.0 + nrm(ks[15], (D_MODEL,), 0.05),
    }

def first_block(x, ln_mix_g, w_in, b_in, attn_sinks, w_attn_up, w_pool_grp, pool_scale, w_pool_up, w_o,
              ln_ffn_g, w_query, sub_keys, u_experts, v_experts, ln_final_g):
    b, s, _ = x.shape
    h = x
    for l in range(DEPTH):
        xn = rmsnorm(h, ln_mix_g[l])
        z = xn @ w_in[l] + b_in[l]
        q, k, v, pz, ga, gp = jnp.split(z, SPLITS, axis=-1)
        q = q.reshape(b, s, N_KV_HEADS, GROUP, HEAD_DIM)
        k = k.reshape(b, s, N_KV_HEADS, HEAD_DIM)
        v = v.reshape(b, s, N_KV_HEADS, HEAD_DIM)
        y_a = sliding_window_attention(q, k, v, attn_sinks[l]) @ w_attn_up[l]
        y_p = multiscale_pool(pz, w_pool_grp[l], pool_scale[l]) @ w_pool_up[l]
        merged = jax.nn.sigmoid(ga) * y_a + jax.nn.sigmoid(gp) * y_p
        h = h + merged @ w_o[l]
        h = h + peer(rmsnorm(h, ln_ffn_g[l]), w_query[l], sub_keys[l], u_experts[l], v_experts[l])
    return rmsnorm(h, ln_final_g)


MIX_WIDTH = D_MODEL
RWKV_WIDTH = MIX_WIDTH // 2
RWKV_HEAD_DIM = 64
RWKV_HEADS = RWKV_WIDTH // RWKV_HEAD_DIM
RWKV_DECAY_LORA = 64
RWKV_AAA_LORA = 64
RWKV_GATE_LORA = 128
RWKV_GN_EPS = 64e-5
GLA_WIDTH = MIX_WIDTH - RWKV_WIDTH
GLA_HEADS = 4
GLA_DV = GLA_WIDTH // GLA_HEADS
GLA_DK = GLA_DV // 2
GLA_KEY_WIDTH = GLA_HEADS * GLA_DK
GLA_GATE_LORA = 16
GLA_GATE_TEMP = 16.0
GLA_CHUNK = 64
CONV_WIDTH = 3
PLE_DIM = 256
D_FF = -(-8 * D_MODEL // (3 * 256)) * 256
NORM_EPS = 1e-6

RWKV_SPLITS = (RWKV_WIDTH, 2 * RWKV_WIDTH, 3 * RWKV_WIDTH,
               3 * RWKV_WIDTH + 2 * RWKV_DECAY_LORA,
               3 * RWKV_WIDTH + 2 * RWKV_DECAY_LORA + RWKV_AAA_LORA)
RWKV_IN_WIDTH = RWKV_SPLITS[-1] + RWKV_GATE_LORA
GLA_SPLITS = (2 * GLA_KEY_WIDTH + GLA_WIDTH, 2 * GLA_KEY_WIDTH + 2 * GLA_WIDTH)
GLA_IN_WIDTH = GLA_SPLITS[-1] + 2 * GLA_GATE_LORA
IN_WIDTH = RWKV_IN_WIDTH + GLA_IN_WIDTH


def rms_norm(x, w, eps=NORM_EPS):
    xf = x.astype(jnp.float32)
    y = xf * lax.rsqrt(jnp.mean(xf * xf, axis=-1, keepdims=True) + eps)
    return (y * w.astype(jnp.float32)).astype(x.dtype)

def centred_shift(z):
    zp = jnp.pad(z, ((0, 0), (1, 1), (0, 0)))
    return 0.5 * (zp[:, :-2] + zp[:, 2:])

def centred_dwconv(z, w):
    pad = (w.shape[0] - 1) // 2
    return lax.conv_general_dilated(z, w.astype(z.dtype), window_strides=(1,),
                                    padding=[(pad, pad)],
                                    dimension_numbers=('NWC', 'WIO', 'NWC'),
                                    feature_group_count=z.shape[-1])

def rwkv7_scan(r, decay, k, v, kk, b, reverse):
    B, T, H, N = r.shape
    xs = tuple(jnp.moveaxis(t, 1, 0) for t in (r, decay, k, v, kk, b))

    def step(S, inp):
        r_t, w_t, k_t, v_t, kk_t, b_t = inp
        sa = jnp.einsum('bhij,bhj->bhi', S, -kk_t)
        S = (S * w_t[:, :, None, :] + sa[..., None] * b_t[:, :, None, :]
             + v_t[..., None] * k_t[:, :, None, :])
        return S, jnp.einsum('bhij,bhj->bhi', S, r_t)

    S0 = jnp.zeros((B, H, N, N), r.dtype)
    _, y = lax.scan(step, S0, xs, reverse=reverse)
    return jnp.moveaxis(y, 0, 1)

def rwkv7_mixer(z, w0, w_up, a0, a_up, g_up, k_k, k_a, r_k, ln_w, ln_b, out_dtype):
    B, T, _ = z.shape
    z = z.astype(jnp.float32)
    r, k, v, w_lo, a_lo, g_lo = jnp.split(z, RWKV_SPLITS, axis=-1)
    w_lo = w_lo.reshape(B, T, 2, RWKV_DECAY_LORA)
    w_log = -jax.nn.softplus(-(w0 + jnp.einsum('btdr,drc->btdc', jnp.tanh(w_lo), w_up))) - 0.5
    decay = jnp.exp(-jnp.exp(w_log))
    a = jax.nn.sigmoid(a0 + a_lo @ a_up)
    g = jax.nn.sigmoid(g_lo) @ g_up

    def heads(t):
        return t.reshape(B, T, RWKV_HEADS, RWKV_HEAD_DIM)

    kk = heads(k * k_k)
    kk = kk * lax.rsqrt(jnp.maximum(jnp.sum(kk * kk, axis=-1, keepdims=True), 1e-24))
    k = k * (1.0 + (a - 1.0) * k_a)
    r_h, k_h, v_h, a_h = heads(r), heads(k), heads(v), heads(a)
    b_h = kk * a_h
    y = (rwkv7_scan(r_h, heads(decay[:, :, 0]), k_h, v_h, kk, b_h, False)
         + rwkv7_scan(r_h, heads(decay[:, :, 1]), k_h, v_h, kk, b_h, True))
    mu = jnp.mean(y, axis=-1, keepdims=True)
    var = jnp.mean(jnp.square(y - mu), axis=-1, keepdims=True)
    y = heads(((y - mu) * lax.rsqrt(var + RWKV_GN_EPS)).reshape(B, T, RWKV_WIDTH) * ln_w + ln_b)
    bonus = jnp.sum(r_h * k_h * r_k, axis=-1, keepdims=True) * v_h
    y = (y + bonus).reshape(B, T, RWKV_WIDTH)
    return (y * g).astype(out_dtype)

def gla_chunked(q, k, v, log_a):
    B, H, T, DK = q.shape
    DV = v.shape[-1]
    nc = T // GLA_CHUNK

    def to_chunks(t):
        return t.reshape(B, H, nc, GLA_CHUNK, t.shape[-1]).transpose(2, 0, 1, 3, 4)

    qc, kc, vc = to_chunks(q), to_chunks(k), to_chunks(v)
    bc = jnp.cumsum(to_chunks(log_a), axis=-2)
    mask = jnp.tril(jnp.ones((GLA_CHUNK, GLA_CHUNK), dtype=bool))[:, :, None]

    def step(S, inp):
        q_c, k_c, v_c, b_c = inp
        o_inter = jnp.einsum('bhcd,bhde->bhce', q_c * jnp.exp(b_c), S)
        diff = b_c[:, :, :, None, :] - b_c[:, :, None, :, :]
        dmat = jnp.exp(jnp.where(mask, diff, -jnp.inf))
        scores = jnp.einsum('bhid,bhjd,bhijd->bhij', q_c, k_c, dmat)
        o_intra = jnp.einsum('bhij,bhje->bhie', scores, v_c)
        b_last = b_c[:, :, -1:, :]
        S = (S * jnp.exp(b_last[:, :, 0, :])[..., None]
             + jnp.einsum('bhcd,bhce->bhde', k_c * jnp.exp(b_last - b_c), v_c))
        return S, o_inter + o_intra

    S0 = jnp.zeros((B, H, DK, DV), q.dtype)
    _, o = lax.scan(step, S0, (qc, kc, vc, bc))
    return o.transpose(1, 2, 0, 3, 4).reshape(B, H, T, DV)

def gla_mixer(z, conv_w, a_up, a_b, norm_w, out_dtype):
    B, T, _ = z.shape
    z = z.astype(jnp.float32)
    qkv, g, a_lo = jnp.split(z, GLA_SPLITS, axis=-1)
    qkv = jax.nn.silu(centred_dwconv(qkv, conv_w))
    q, k, v = jnp.split(qkv, (GLA_KEY_WIDTH, 2 * GLA_KEY_WIDTH), axis=-1)
    a_lo = a_lo.reshape(B, T, 2, GLA_GATE_LORA)
    log_a = jax.nn.log_sigmoid(jnp.einsum('btdr,drc->btdc', a_lo, a_up) + a_b) / GLA_GATE_TEMP

    def heads(t, d):
        return t.reshape(B, T, GLA_HEADS, d).transpose(0, 2, 1, 3)

    def flip(t):
        return jnp.flip(t, axis=2)

    q_h = heads(q, GLA_DK) * GLA_DK ** -0.5
    k_h = heads(k, GLA_DK)
    v_h = heads(v, GLA_DV)
    o_f = gla_chunked(q_h, k_h, v_h, heads(log_a[:, :, 0], GLA_DK))
    o_b = flip(gla_chunked(flip(q_h), flip(k_h), flip(v_h), flip(heads(log_a[:, :, 1], GLA_DK))))
    o = (o_f + o_b).transpose(0, 2, 1, 3)
    o = rms_norm(o, norm_w) * jax.nn.silu(g.reshape(B, T, GLA_HEADS, GLA_DV))
    return o.reshape(B, T, GLA_WIDTH).astype(out_dtype)

def second_inputs(seed: int = 0) -> dict:
    key = jax.random.key(seed)
    ks = jax.random.split(key, 32)
    L = DEPTH
    f32 = jnp.float32

    def nrm(k, shape, scale):
        return jax.random.normal(k, shape, f32) * scale

    def gain(k, shape):
        return 1.0 + 0.05 * jax.random.normal(k, shape, f32)

    return {
        'x': jax.random.normal(ks[0], (BATCH, SEQ, D_MODEL), f32),
        'p': jax.random.normal(ks[1], (DEPTH, BATCH, SEQ, PLE_DIM), f32),
        'norm_mix_pre': gain(ks[2], (L, D_MODEL)),
        'norm_mix_post': gain(ks[3], (L, D_MODEL)),
        'norm_ffn_pre': gain(ks[4], (L, D_MODEL)),
        'norm_ffn_post': gain(ks[5], (L, D_MODEL)),
        'norm_ple': gain(ks[6], (L, D_MODEL)),
        'w_in': nrm(ks[7], (L, D_MODEL, IN_WIDTH), D_MODEL ** -0.5),
        'rwkv_mu': jax.random.uniform(ks[8], (L, RWKV_IN_WIDTH), f32),
        'rwkv_w0': jax.random.uniform(ks[9], (L, 2, RWKV_WIDTH), f32, -6.0, -1.0),
        'rwkv_w_up': nrm(ks[10], (L, 2, RWKV_DECAY_LORA, RWKV_WIDTH), RWKV_DECAY_LORA ** -0.5),
        'rwkv_a0': nrm(ks[11], (L, RWKV_WIDTH), 0.3),
        'rwkv_a_up': nrm(ks[12], (L, RWKV_AAA_LORA, RWKV_WIDTH), 0.5 * RWKV_AAA_LORA ** -0.5),
        'rwkv_g_up': nrm(ks[13], (L, RWKV_GATE_LORA, RWKV_WIDTH), RWKV_GATE_LORA ** -0.5),
        'rwkv_k_k': 0.85 + 0.05 * jax.random.normal(ks[14], (L, RWKV_WIDTH), f32),
        'rwkv_k_a': gain(ks[15], (L, RWKV_WIDTH)),
        'rwkv_r_k': nrm(ks[16], (L, RWKV_HEADS, RWKV_HEAD_DIM), 0.1),
        'rwkv_ln_w': gain(ks[17], (L, RWKV_WIDTH)),
        'rwkv_ln_b': nrm(ks[18], (L, RWKV_WIDTH), 0.02),
        'gla_conv': nrm(ks[19], (L, CONV_WIDTH, 1, 2 * GLA_KEY_WIDTH + GLA_WIDTH), CONV_WIDTH ** -0.5),
        'gla_a_up': nrm(ks[20], (L, 2, GLA_GATE_LORA, GLA_KEY_WIDTH), GLA_GATE_LORA ** -0.5),
        'gla_a_b': 2.0 + 0.5 * jax.random.normal(ks[21], (L, 2, GLA_KEY_WIDTH), f32),
        'gla_norm': gain(ks[22], (L, GLA_DV)),
        'w_out': nrm(ks[23], (L, MIX_WIDTH, D_MODEL), MIX_WIDTH ** -0.5),
        'ffn_gate': nrm(ks[24], (L, D_MODEL, D_FF), D_MODEL ** -0.5),
        'ffn_up': nrm(ks[25], (L, D_MODEL, D_FF), D_MODEL ** -0.5),
        'ffn_down': nrm(ks[26], (L, D_FF, D_MODEL), D_FF ** -0.5),
        'ple_proj': nrm(ks[27], (L, PLE_DIM, D_MODEL), PLE_DIM ** -0.5),
        'ple_gate': nrm(ks[28], (L, D_MODEL, D_MODEL), D_MODEL ** -0.5),
        'ple_gate_b': nrm(ks[29], (L, D_MODEL), 0.02),
    }

def second_block(x, p, norm_mix_pre, norm_mix_post, norm_ffn_pre, norm_ffn_post, norm_ple,
              w_in, rwkv_mu, rwkv_w0, rwkv_w_up, rwkv_a0, rwkv_a_up, rwkv_g_up,
              rwkv_k_k, rwkv_k_a, rwkv_r_k, rwkv_ln_w, rwkv_ln_b,
              gla_conv, gla_a_up, gla_a_b, gla_norm, w_out,
              ffn_gate, ffn_up, ffn_down, ple_proj, ple_gate, ple_gate_b):
    h = x
    for i in range(DEPTH):
        xn = rms_norm(h, norm_mix_pre[i])
        z = xn @ w_in[i]
        z_rwkv, z_gla = z[..., :RWKV_IN_WIDTH], z[..., RWKV_IN_WIDTH:]
        z_rwkv = z_rwkv + rwkv_mu[i] * (centred_shift(z_rwkv) - z_rwkv)
        y_rwkv = rwkv7_mixer(z_rwkv, rwkv_w0[i], rwkv_w_up[i], rwkv_a0[i], rwkv_a_up[i],
                             rwkv_g_up[i], rwkv_k_k[i], rwkv_k_a[i], rwkv_r_k[i],
                             rwkv_ln_w[i], rwkv_ln_b[i], h.dtype)
        y_gla = gla_mixer(z_gla, gla_conv[i], gla_a_up[i], gla_a_b[i], gla_norm[i], h.dtype)
        y = jnp.concatenate([y_rwkv, y_gla], axis=-1) @ w_out[i]
        h = h + rms_norm(y, norm_mix_post[i])
        hn = rms_norm(h, norm_ffn_pre[i])
        f = (jax.nn.silu(hn @ ffn_gate[i]) * (hn @ ffn_up[i])) @ ffn_down[i]
        h = h + rms_norm(f, norm_ffn_post[i])
        e = p[i] @ ple_proj[i]
        gate = jax.nn.sigmoid(h @ ple_gate[i] + ple_gate_b[i])
        h = h + rms_norm(gate * e, norm_ple[i])
    return h


def setup_inputs(seed=0):
    out = dict(first_inputs(seed))
    for name, value in second_inputs(seed + 1).items():
        if name != "x":
            out[name + "_2"] = value
    return out


def reference(
    x, ln_mix_g, w_in, b_in, attn_sinks, w_attn_up, w_pool_grp, pool_scale, w_pool_up, w_o,
    ln_ffn_g, w_query, sub_keys, u_experts, v_experts, ln_final_g, p_2, norm_mix_pre_2,
    norm_mix_post_2, norm_ffn_pre_2, norm_ffn_post_2, norm_ple_2, w_in_2, rwkv_mu_2, rwkv_w0_2,
    rwkv_w_up_2, rwkv_a0_2, rwkv_a_up_2, rwkv_g_up_2, rwkv_k_k_2, rwkv_k_a_2, rwkv_r_k_2,
    rwkv_ln_w_2, rwkv_ln_b_2, gla_conv_2, gla_a_up_2, gla_a_b_2, gla_norm_2, w_out_2,
    ffn_gate_2, ffn_up_2, ffn_down_2, ple_proj_2, ple_gate_2, ple_gate_b_2,
):
    x = first_block(
        x, ln_mix_g, w_in, b_in, attn_sinks, w_attn_up, w_pool_grp, pool_scale, w_pool_up, w_o,
        ln_ffn_g, w_query, sub_keys, u_experts, v_experts, ln_final_g,
    )
    return second_block(
        x, p_2, norm_mix_pre_2, norm_mix_post_2, norm_ffn_pre_2, norm_ffn_post_2, norm_ple_2,
        w_in_2, rwkv_mu_2, rwkv_w0_2, rwkv_w_up_2, rwkv_a0_2, rwkv_a_up_2, rwkv_g_up_2,
        rwkv_k_k_2, rwkv_k_a_2, rwkv_r_k_2, rwkv_ln_w_2, rwkv_ln_b_2, gla_conv_2, gla_a_up_2,
        gla_a_b_2, gla_norm_2, w_out_2, ffn_gate_2, ffn_up_2, ffn_down_2, ple_proj_2,
        ple_gate_2, ple_gate_b_2,
    )


_drawn_inputs = setup_inputs


def setup_inputs(seed=0):
    import zlib

    import numpy as np

    out = dict(_drawn_inputs(seed))
    spreads = {}
    factors = {'attn_sinks': 7.405, 'rwkv_ln_b_2': 6.218, 'gla_a_up_2': 3.82, 'ple_gate_b_2': 8.0}
    for name, (base, spread) in spreads.items():
        noise = np.random.default_rng([zlib.crc32(name.encode()), seed]).standard_normal(out[name].shape)
        drawn = base * np.exp(spread * noise) if base else spread * noise
        out[name] = __import__('jax').numpy.asarray(drawn.astype(out[name].dtype))
    for name, factor in factors.items():
        out[name] = (out[name] * factor).astype(out[name].dtype)
    return out
```

```python
from contextlib import ExitStack

import numpy as np

import concourse.bass as bass
from concourse import mybir

F32 = mybir.dt.float32
U32 = mybir.dt.uint32
ALU = mybir.AluOpType
ACT = mybir.ActivationFunctionType
AXX = mybir.AxisListType.X

P = 128
T = 512
D = 1024
DC = D // P
BANK = 4

NH, NKV, HD = 16, 2, 64
QC = NH * HD // P
NB = T // P
SCALE = HD ** -0.5
NEG = -1e30
PW = (2, 4, 8, 16)
PH = 8
NK = 128
TK = 16
NE = NK * NK
TB = 64
NTB = T // TB
GI = 16
NG = NK // GI

C = 64
NCH = T // C
RC = 4
GP = 2
FFC = 2816 // P


class Count:

    def __init__(self, sem, base=0, per=0, i=0):
        self.sem, self.start, self.n, self.per, self.i = sem, base, 0, per, i

    def inc(self, ins):
        ins.then_inc(self.sem, 1)
        self.n += 1

    def at(self):
        return self.start + self.n + (self.i * self.per if self.per else 0)

    def wait(self, eng):
        eng.wait_ge(self.sem, self.at())


class Dense:

    def __init__(self, ctx, nc, ps):
        self.ring = ctx.enter_context(nc.sbuf_tensor("weight_ring", [P, BANK, DC * P], F32))
        self.acc = [ps[:, k, :] for k in range(BANK)]
        self.ready = [ctx.enter_context(nc.semaphore(f"weight_slot_loaded{k}")) for k in range(BANK)]
        self.used = ctx.enter_context(nc.semaphore("weight_slot_used"))
        self.free = [ctx.enter_context(nc.semaphore(f"accumulator_read{k}")) for k in range(BANK)]
        self.slots = 0
        self.units = 0

    def open(self, act):
        for k in range(BANK):
            act.sem_inc(self.free[k], 1)

    def load(self, sp, w, turns, per=1):
        kt = w.shape[2]

        def slot(i, n):
            sp.dma_start(self.ring[:, n % BANK, 0:kt], w[i * BANK * per + n]).then_inc(self.ready[n % BANK], 16)

        first = 0
        if self.slots == 0:
            for n in range(BANK * per):
                if n >= BANK:
                    sp.wait_ge(self.used, n - BANK + 1)
                slot(0, n)
            first = 1
        if turns > first:
            with sp.Fori(first, turns) as i:
                for n in range(BANK * per):
                    sp.wait_ge(self.used, i * (BANK * per) + (self.slots + n - BANK + 1))
                    slot(i, n)

    def slot_wait(self, pe, i, n, per=1):
        pe.wait_ge(self.ready[n % BANK], i * (16 * per) + 16 * (self.slots // BANK + n // BANK + 1))

    def free_wait(self, pe, i, k):
        pe.wait_ge(self.free[k], i + (self.units // BANK + 1))

    def multiply(self, pe, turns, rhs, kts):
        per = len(kts)
        with pe.Fori(0, turns) as i:
            for k in range(BANK):
                self.free_wait(pe, i, k)
                done = 0
                for j, kt in enumerate(kts):
                    n = k * per + j
                    self.slot_wait(pe, i, n, per)
                    for t in range(kt):
                        mm = pe.matmul(self.acc[k], self.ring[:, n % BANK, t * P:(t + 1) * P], rhs(done),
                                       start=(done == 0), stop=(done == sum(kts) - 1))
                        done += 1
                    mm.then_inc(self.used, 1)

    def full_wait(self, eng, i, k, per=1):
        eng.wait_ge(self.used, i * (BANK * per) + (self.slots + (k + 1) * per))

    def read_value(self, i, k):
        return i + (self.units // BANK + 2)

    def close(self, turns, per=1):
        self.slots += turns * BANK * per
        self.units += turns * BANK


class Norm:

    def __init__(self, ctx, nc, ps, ones):
        def sem(n):
            return ctx.enter_context(nc.semaphore(n))

        self.sq, self.sum, self.rstd_ok, self.out = sem("norm_squares"), sem("norm_summed"), sem("norm_rstd"), sem("norm_out")
        self.added = sem("norm_added")
        self.adds = 0
        self.rstd = ctx.enter_context(nc.sbuf_tensor("norm_rstd_tile", [P, T], F32))
        self.ps, self.ones, self.n = ps[:, 4, :], ones, 0

    def squares(self, act, src, dst):
        for k in range(DC):
            act.activation(dst[:, k, :], src[:, k, :], ACT.Square).then_inc(self.sq, 1)

    def sums(self, pe, sq):
        for k in range(DC):
            pe.wait_ge(self.sq, DC * self.n + k + 1)
            mm = pe.matmul(self.ps, self.ones, sq[:, k, :], start=(k == 0), stop=(k == DC - 1))
        mm.then_inc(self.sum, 1)

    def roots(self, act, eps):
        act.wait_ge(self.sum, self.n + 1)
        act.activation(self.rstd[:, :], self.ps, ACT.Ln, bias=eps, scale=1.0 / D).then_inc(self.rstd_ok, 1)
        act.wait_ge(self.rstd_ok, 2 * self.n + 1)
        act.activation(self.rstd[:, :], self.rstd[:, :], ACT.Exp, scale=-0.5).then_inc(self.rstd_ok, 1)

    def scale(self, dve, src, dst, gain, add=None):
        dve.wait_ge(self.rstd_ok, 2 * self.n + 2)
        for k in range(DC):
            dve.scalar_tensor_tensor(out=dst[:, k, :], in0=src[:, k, :], scalar=gain[:, k:k + 1],
                                     in1=self.rstd[:, :], op0=ALU.mult, op1=ALU.mult).then_inc(self.out, 1)
        if add is not None:
            for k in range(DC):
                dve.wait_ge(self.out, DC * self.n + k + 1)
                dve.tensor_tensor(add[:, k, :], add[:, k, :], dst[:, k, :], ALU.add).then_inc(self.added, 1)

    def out_wait(self, eng, k=DC - 1):
        eng.wait_ge(self.out, DC * self.n + k + 1)

    def added_wait(self, eng, k=DC - 1):
        eng.wait_ge(self.added, DC * self.adds + k + 1)

    def close(self, add=False):
        self.n += 1
        self.adds += add


def layout_params(a):
    def col(v):
        return np.asarray(v, np.float32).reshape(-1, P).T

    b = np.asarray(a["b_in"])[0]
    qw, kw = NH * HD, NKV * HD
    o_pool = qw + 2 * kw
    o_ga = o_pool + len(PW) * P
    bk = b[qw:qw + kw].reshape(NKV, HD)
    mu = np.zeros((15 * P,), np.float32)
    rmu = np.asarray(a["rwkv_mu_2"])[0]
    mu[0:13 * P + 64] = rmu[0:13 * P + 64]
    mu[14 * P:15 * P] = rmu[13 * P + 64:]
    conv = np.asarray(a["gla_conv_2"])[0, :, 0, :]
    parts = [
        ("g_mix", col(a["ln_mix_g"][0])), ("b_q", col(b[0:qw])),
        ("b_k", np.concatenate([np.concatenate([bk[v], bk[v]])[:, None] for v in range(NKV)], 1)),
        ("b_v", np.broadcast_to(b[qw + kw:o_pool][None, :], (P, kw))),
        ("b_pool", col(b[o_pool:o_ga])), ("b_ga", col(b[o_ga:o_ga + D])), ("b_gp", col(b[o_ga + D:])),
        ("sinks", np.broadcast_to(np.asarray(a["attn_sinks"])[0][None, :], (P, NH))),
        ("pool_scale", col(a["pool_scale"][0])), ("g_ffn", col(a["ln_ffn_g"][0])),
        ("g_final", col(a["ln_final_g"])),
        ("g_mix_pre", col(a["norm_mix_pre_2"][0])), ("g_mix_post", col(a["norm_mix_post_2"][0])),
        ("g_ffn_pre", col(a["norm_ffn_pre_2"][0])), ("g_ffn_post", col(a["norm_ffn_post_2"][0])),
        ("g_ple", col(a["norm_ple_2"][0])), ("mu", col(mu)),
        ("w0", col(np.asarray(a["rwkv_w0_2"])[0].reshape(-1))), ("a0", col(a["rwkv_a0_2"][0])),
        ("k_k", col(a["rwkv_k_k_2"][0])), ("k_a", col(a["rwkv_k_a_2"][0])),
        ("r_k", col(np.asarray(a["rwkv_r_k_2"])[0].reshape(-1))),
        ("ln_w", col(a["rwkv_ln_w_2"][0])), ("ln_b", col(a["rwkv_ln_b_2"][0])),
        ("conv0", col(conv[0])), ("conv1", col(conv[1])), ("conv2", col(conv[2])),
        ("a_b", col(np.asarray(a["gla_a_b_2"])[0].reshape(-1))), ("gla_norm", col(a["gla_norm_2"][0])),
        ("b_ple", col(a["ple_gate_b_2"][0])),
        ("eps5", np.full((P, 1), 1e-5, np.float32)), ("eps6", np.full((P, 1), 1e-6, np.float32)),
        ("eps_gn", np.full((P, 1), 64e-5, np.float32)), ("tiny", np.full((P, 1), 1e-24, np.float32)),
    ]
    where, at = {}, 0
    for name, v in parts:
        where[name] = (at, v.shape[1])
        at += v.shape[1]
    return where, np.ascontiguousarray(np.concatenate([v for _, v in parts], 1))


def tiles(w):
    w = np.asarray(w)
    k, n = w.shape
    return np.ascontiguousarray(w.reshape(k // P, P, n // P, P).transpose(2, 1, 0, 3).reshape(n // P, P, k))


def layout_constants():
    q, k = np.arange(P)[:, None], np.arange(2 * P)[None, :]
    rel = q - (k - P)
    ok = (rel >= 0) & (rel < P)
    mask = np.where(ok, 0.0, NEG).astype(np.float32)
    mask0 = np.where(ok & (k >= P), 0.0, NEG).astype(np.float32)
    t1 = np.arange(1, T + 1, dtype=np.float32)
    inv = np.concatenate([np.broadcast_to((1.0 / np.minimum(t1, float(w)))[None, :], (P, T)) for w in PW], 1)
    ident = np.eye(P, dtype=np.float32)
    iota = np.broadcast_to(np.arange(P, dtype=np.float32)[None, :], (P, P))
    ones = np.ones((P, P), np.float32)
    half = np.kron(np.eye(2), np.ones((64, 64))).astype(np.float32)
    s, t = (np.arange(P) % C)[:, None], np.arange(C)[None, :]
    upper = (s < t).astype(np.float32)
    upper_eq = (s <= t).astype(np.float32)
    levels = []
    m = 1
    while m < C:
        levels.append(((s // (2 * m) == t // (2 * m)) & (s % (2 * m) < m) & (t % (2 * m) >= m)).astype(np.float32))
        m *= 2
    eye2 = (s == t).astype(np.float32)
    start = np.broadcast_to((np.arange(T) % C != 0).astype(np.float32)[None, :], (P, T))
    parts = [("mask", np.concatenate([mask0, mask, mask, mask], 1)), ("inv_count", inv), ("ident", ident),
             ("iota", iota), ("ones", ones), ("half", half), ("upper", upper), ("upper_eq", upper_eq),
             ("eye2", eye2), ("levels", np.concatenate(levels, 1)), ("chunk_start", start)]
    where, at = {}, 0
    for name, v in parts:
        where[name] = (at, v.shape[1])
        at += v.shape[1]
    return where, np.ascontiguousarray(np.concatenate([v for _, v in parts], 1).astype(np.float32))


class Kernel:

    def __init__(self, nc):
        self.nc, self.spent = nc, []

    def semaphore(self, name):
        self.spent.append(self.nc.alloc_semaphore(name))
        return self.spent[-1]

    def clear_semaphores(self):
        self.nc.clear_and_free_semaphores(self.spent)
        self.nc.all_engine_barrier()
        self.spent = []


def first_mixer(nc, k, dram):
    dense, norm, par, h, ps, consts = k.dense, k.norm, k.par, k.h, k.ps, k.consts
    with ExitStack() as ctx:
        def sb(name, shape, dt=F32):
            return ctx.enter_context(nc.sbuf_tensor(name, shape, dt))

        sem = k.semaphore

        q = sb("q_then_attention_out", [P, QC, T])
        xn = sb("xn_then_merged", [P, DC, T])
        ga = sb("gate_attention", [P, DC, T])
        gp = sb("gate_pool", [P, DC, T])
        zp = sb("pool_in", [P, len(PW), 16 + T])
        keys = sb("keys_by_kv_and_half", [P, NKV, 2, P + T])
        vals = sb("values_by_token", [P, NB + 1, NKV * HD])
        yp = sb("pooled", [P, len(PW), T])
        cm = sb("mask_by_block", [P, NB, 2 * P])

        zeroed = sem("pool_engine_zeroed")
        with nc.Block() as block:
            @block.sync
            def _(sp):
                sp.dma_start(h[:, :, :], dram["x"]).then_inc(k.boot, 16)
                sp.dma_start(par.tile, dram["params"]).then_inc(k.boot, 16)
                sp.dma_start(consts.tile, dram["consts"][:, consts.first:]).then_inc(k.boot, 16)
                sp.dma_start(cm[:, :, :], dram["consts"][:, 0:NB * 2 * P].rearrange("p (b n) -> p b n", b=NB)).then_inc(k.boot, 16)
                dense.load(sp, dram["w_z"], 8)

            @block.gpsimd
            def _(pool):
                pool.memset(keys[:, :, :, :], 0.0).then_inc(zeroed, 1)
                pool.memset(vals[:, 0, :], 0.0).then_inc(zeroed, 1)
                pool.memset(zp[:, :, 0:16], 0.0).then_inc(zeroed, 1)

            @block.scalar
            def _(act):
                dense.open(act)
                act.wait_ge(k.boot, 64)
                norm.squares(act, h, xn)
                norm.roots(act, par("eps5"))

                def gemm_out(first, turns, dst, bias, func):
                    with act.Fori(first, first + turns) as i:
                        for n in range(BANK):
                            dense.full_wait(act, i, n)
                            act.activation(dst(i * BANK + (n - first * BANK)), dense.acc[n], func,
                                           bias=bias[:, bass.ds(i * BANK + (n - first * BANK), 1)]).then_inc(dense.free[n], 1)

                gemm_out(0, 2, lambda m: q[:, m, :], par("b_q"), ACT.Identity)
                gemm_out(2, 2, lambda m: ga[:, m, :], par("b_ga"), ACT.Sigmoid)
                gemm_out(4, 2, lambda m: gp[:, m, :], par("b_gp"), ACT.Sigmoid)
                act.wait_ge(zeroed, 3)
                for n in range(BANK):
                    dense.full_wait(act, 6, n)
                    act.activation(zp[:, n, 16:], dense.acc[n], ACT.Identity,
                                   bias=par("b_pool")[:, n:n + 1]).then_inc(dense.free[n], 1)
                for v in range(NKV):
                    dense.full_wait(act, 7, v)
                    act.activation(keys[0:HD, v, 0, P:], dense.acc[v][0:HD, :], ACT.Identity,
                                   bias=par("b_k")[0:HD, v:v + 1])
                    act.activation(keys[HD:P, v, 1, P:], dense.acc[v][HD:P, :], ACT.Identity,
                                   bias=par("b_k")[HD:P, v:v + 1]).then_inc(dense.free[v], 1)
                act.sem_inc(dense.free[3], 1)

            @block.vector
            def _(dve):
                dve.wait_ge(k.boot, 64)
                norm.scale(dve, h, xn, par("g_mix"))
                dense.full_wait(dve, 7, 2)
                dve.tensor_tensor(vals[:, 1:, :], dense.acc[2].rearrange("p (b n) -> p b n", b=NB),
                                  par("b_v")[:, None, :].to_broadcast([P, NB, P]), ALU.add).then_inc(dense.free[2], 1)

            @block.tensor
            def _(pe):
                pe.wait_ge(k.boot, 64)
                norm.sums(pe, xn)
                norm.out_wait(pe)
                dense.multiply(pe, 7, lambda t: xn[:, t, :], [DC])
                for v in range(NKV):
                    dense.free_wait(pe, 7, v)
                    dense.slot_wait(pe, 7, v)
                    for t in range(DC):
                        mm = pe.matmul(dense.acc[v], dense.ring[:, v, t * P:(t + 1) * P], xn[:, t, :],
                                       start=(t == 0), stop=(t == DC - 1))
                    mm.then_inc(dense.used, 1)
                dense.free_wait(pe, 7, 2)
                dense.slot_wait(pe, 7, 2)
                for b in range(NB):
                    for t in range(DC):
                        mm = pe.matmul(dense.acc[2][:, b * P:(b + 1) * P], xn[:, t, b * P:(b + 1) * P],
                                       dense.ring[:, 2, t * P:(t + 1) * P], start=(t == 0), stop=(t == DC - 1))
                mm.then_inc(dense.used, 1)
        norm.close()
        group_w = dense.ring[:, 3, :]
        group_slot = dense.slots // BANK + 8
        dense.close(8)

        attention(nc, k, q, keys, vals, cm, zp, yp)

        yps = sb("pool_groups_out", [P, len(PW), T])
        group_done, group_out, merge_a, merge_p, merged = (sem(n) for n in (
            "pool_group_product", "pool_group_scaled", "attention_gated", "pool_gated", "merged"))
        dense_a, dense_p, dense_o = 2, 2, 2
        base = (dense.slots, dense.units)
        with nc.Block() as block:
            @block.sync
            def _(sp):
                dense.slots, dense.units = base
                for name, turns in (("w_attn_up", 2), ("w_pool_up", 2), ("w_o", 2)):
                    dense.load(sp, dram[name], turns)
                    dense.close(turns)

            @block.scalar
            def _(act):
                for g in range(len(PW)):
                    act.wait_ge(group_done, g + 1)
                    act.activation(yps[:, g, :], ps[:, 4 + g, :], ACT.Copy,
                                   scale=par("pool_scale")[:, g:g + 1]).then_inc(group_out, 1)

            @block.vector
            def _(dve):
                dense.slots, dense.units = base

                def gate(dst, g, turns, done):
                    with dve.Fori(0, turns) as i:
                        for n in range(BANK):
                            dense.full_wait(dve, i, n)
                            dve.tensor_tensor(dst[:, i * BANK + n, :], dense.acc[n], g[:, i * BANK + n, :],
                                              ALU.mult).then_inc(dense.free[n], 1)
                    dense.close(turns)

                gate(xn, ga, dense_a, merge_a)
                gate(gp, gp, dense_p, merge_p)
                for n in range(BANK):
                    dve.wait_ge(dense.free[n], dense.units // BANK + 1)
                for m in range(DC):
                    dve.tensor_tensor(xn[:, m, :], xn[:, m, :], gp[:, m, :], ALU.add).then_inc(merged, 1)
                with dve.Fori(0, dense_o) as i:
                    for n in range(BANK):
                        dense.full_wait(dve, i, n)
                        dve.tensor_tensor(h[:, i * BANK + n, :], dense.acc[n], h[:, i * BANK + n, :],
                                          ALU.add).then_inc(dense.free[n], 1)
                dense.close(dense_o)

            @block.tensor
            def _(pe):
                dense.slots, dense.units = base
                pe.wait_ge(dense.ready[3], 16 * group_slot)
                for g in range(len(PW)):
                    mm = pe.matmul(ps[:, 4 + g, :], group_w[:, g * P:(g + 1) * P], yp[:, g, :], start=True, stop=True)
                    mm.then_inc(group_done, 1)
                pe.wait_ge(group_done, len(PW))
                pe.sem_inc(dense.used, 1)
                dense.multiply(pe, 2, lambda t: q[:, t, :], [DC])
                dense.close(2)
                pe.wait_ge(group_out, len(PW))
                dense.multiply(pe, 2, lambda t: yps[:, t, :], [len(PW)])
                dense.close(2)
                pe.wait_ge(merged, DC)
                dense.multiply(pe, 2, lambda t: xn[:, t, :], [DC])
                dense.close(2)


def attention(nc, k, q, keys, vals, masks, zp, yp):
    ps, par, consts = k.ps, k.par, k.consts
    with ExitStack() as ctx:
        def sb(name, shape, dt=F32):
            return ctx.enter_context(nc.sbuf_tensor(name, shape, dt))

        sem = k.semaphore

        qs = sb("query_block", [P, QC, P])
        vs = sb("value_blocks", [P, 2, NKV, 2, P])
        s = sb("scores", [P, 2, 2, 2 * P])
        e = sb("probabilities", [P, 2, 2, 2 * P])
        pt = sb("probabilities_transposed", [P, 4 * P])
        mx, nm, su, es, den, rc = (sb(n, [P, NH]) for n in (
            "row_max", "negated_max", "row_sum", "sink_exp", "denominator", "reciprocal"))
        nsink = sb("negated_sinks", [P, NH])
        inv = sb("inverse_counts", [P, len(PW), T])
        w1, w2 = (sb(n, [P, len(PW), 16 + T]) for n in ("window_sums_a", "window_sums_b"))
        inv_in, zeroed, staged, scored, scaled, chain, negmax, exps, probs, turned, copied, mixed, out, pooled = (
            sem(n) for n in ("inverse_counts_loaded", "value_blocks_zeroed", "query_block_staged", "scores_product",
                             "scores_scaled", "attention_vector_chain", "negated_max_ready", "exps_done", "probs_ready",
                             "probs_transposed", "transposed_copied", "value_product", "attention_out", "pool_chain"))
        with nc.Block() as block:
            @block.sync
            def _(sp):
                sp.dma_start(inv[:, :, :], k.dram["inv_count"]).then_inc(inv_in, 16)

            @block.gpsimd
            def _(pool):
                pool.memset(vs[:, :, :, :, :], 0.0).then_inc(zeroed, 1)
                pool.wait_ge(zeroed, 1)
                with pool.Fori(0, NB) as b:
                    pool.tensor_copy(qs[:, :, :], q[:, :, bass.ds(b * P, P)]).then_inc(staged, 1)
                    for half in range(2):
                        pool.tensor_copy(vs[:, :, :, half, half * HD:(half + 1) * HD],
                                         vals[:, bass.ds(b, 2), :].rearrange("p b (v n) -> p b v n", v=NKV)).then_inc(staged, 1)
                    pool.wait_ge(mixed, b * QC + QC)
                pool.memset(w1[:, :, 0:16], 0.0).then_inc(pooled, 1)
                pool.memset(w2[:, :, 0:16], 0.0).then_inc(pooled, 1)
                src = zp
                for n, dst in enumerate((w1, w2, w1, w2)):
                    lag = PW[n] // 2
                    pool.wait_ge(pooled, 2 + n)
                    pool.tensor_tensor(dst[:, n:, 16:], src[:, n:, 16:], src[:, n:, 16 - lag:16 + T - lag],
                                       ALU.add).then_inc(pooled, 1)
                    src = dst
                pool.wait_ge(pooled, 6)
                pool.wait_ge(inv_in, 16)
                for g in range(len(PW)):
                    pool.tensor_tensor(yp[:, g, :], (w1, w2)[g % 2][:, g, 16:], inv[:, g, :], ALU.mult).then_inc(pooled, 1)
                for g in range(len(PW)):
                    pool.wait_ge(pooled, 7 + g)
                    pool.tensor_tensor(yp[:, g, :], yp[:, g, :], zp[:, g, 16:], ALU.subtract).then_inc(pooled, 1)

            @block.tensor
            def _(pe):
                with pe.Fori(0, NB) as b:
                    pe.wait_ge(staged, b * 3 + 3)

                    def scores(c):
                        if c >= 2:
                            pe.wait_ge(scaled, b * QC + (c - 1))
                        for half in range(2):
                            mm = pe.matmul(ps[:, c % 2, half * 2 * P:(half + 1) * 2 * P], qs[:, c, :],
                                           keys[:, c * NKV // QC, half, bass.ds(b * P, 2 * P)], start=True, stop=True)
                        mm.then_inc(scored, 1)

                    scores(0)
                    for c in range(QC):
                        if c + 1 < QC:
                            scores(c + 1)
                        pe.wait_ge(probs, b * QC + (c + 1))
                        if c:
                            pe.wait_ge(copied, b * QC + c)
                        for half in range(2):
                            for kb in range(2):
                                n = half * 2 + kb
                                mm = pe.transpose(ps[:, 2, n * P:(n + 1) * P], e[:, c % 2, half, kb * P:(kb + 1) * P],
                                                  consts("ident"))
                        mm.then_inc(turned, 1)
                        pe.wait_ge(copied, b * QC + (c + 1))
                        if c:
                            pe.wait_ge(out, b * QC + c)
                        for half in range(2):
                            for kb in range(2):
                                n = half * 2 + kb
                                mm = pe.matmul(ps[:, 3, 0:P], vs[:, kb, c * NKV // QC, half, :], pt[:, n * P:(n + 1) * P],
                                               start=(n == 0), stop=(n == 3))
                        mm.then_inc(mixed, 1)
                    pe.wait_ge(out, b * QC + QC)

            @block.vector
            def _(dve):
                sinks = par("sinks")
                dve.tensor_scalar(nsink[:, :], sinks, -1.0, None, ALU.mult).then_inc(chain, 1)
                per = 3 * QC
                with dve.Fori(0, NB) as b:
                    link = Count(chain, 1, per, b)

                    def scale_and_max(c):
                        dve.wait_ge(scored, b * QC + (c + 1))
                        dve.scalar_tensor_tensor(
                            out=s[:, c % 2, :, :], in0=ps[:, c % 2, :].rearrange("p (g n) -> p g n", g=2), scalar=SCALE,
                            in1=masks[:, bass.ds(b, 1), :].to_broadcast([P, 2, 2 * P]),
                            op0=ALU.mult, op1=ALU.add).then_inc(scaled, 1)
                        dve.wait_ge(scaled, b * QC + (c + 1))
                        link.inc(dve.tensor_reduce(mx[:, 2 * c:2 * c + 2], s[:, c % 2, :, :], AXX, ALU.max))
                        link.wait(dve)
                        dve.scalar_tensor_tensor(out=nm[:, 2 * c:2 * c + 2], in0=mx[:, 2 * c:2 * c + 2], scalar=-1.0,
                                                 in1=nsink[:, 2 * c:2 * c + 2], op0=ALU.mult,
                                                 op1=ALU.min).then_inc(negmax, 1)

                    def normalise(c):
                        dve.wait_ge(exps, b * (4 * QC) + 4 * (c + 1))
                        r = slice(2 * c, 2 * c + 2)
                        link.inc(dve.tensor_tensor(den[:, r], su[:, r], es[:, r], ALU.add))
                        link.wait(dve)
                        link.inc(dve.reciprocal(rc[:, r], den[:, r]))
                        link.wait(dve)
                        dve.tensor_tensor(e[:, c % 2, :, :], e[:, c % 2, :, :],
                                          rc[:, r, None].to_broadcast([P, 2, 2 * P]), ALU.mult).then_inc(probs, 1)

                    scale_and_max(0)
                    for c in range(1, QC):
                        scale_and_max(c)
                        normalise(c - 1)
                    normalise(QC - 1)

            @block.scalar
            def _(act):
                with act.Fori(0, NB) as b:
                    def exp(c):
                        act.wait_ge(negmax, b * QC + (c + 1))
                        for half in range(2):
                            j = 2 * c + half
                            act.activation(e[:, c % 2, half, :], s[:, c % 2, half, :], ACT.Exp, bias=nm[:, j:j + 1],
                                           accum_out=su[:, j:j + 1]).then_inc(exps, 1)
                            act.activation(es[:, j:j + 1], par("sinks")[:, j:j + 1], ACT.Exp,
                                           bias=nm[:, j:j + 1]).then_inc(exps, 1)

                    def copy_out(c):
                        act.wait_ge(turned, b * QC + (c + 1))
                        act.activation(pt[:, :], ps[:, 2, :], ACT.Copy).then_inc(copied, 1)
                        act.wait_ge(mixed, b * QC + (c + 1))
                        act.activation(q[:, c, bass.ds(b * P, P)], ps[:, 3, 0:P], ACT.Copy).then_inc(out, 1)

                    exp(0)
                    for c in range(1, QC):
                        exp(c)
                        copy_out(c - 1)
                    copy_out(QC - 1)


def experts(nc, k, dram):
    dense, norm, par, h, ps, consts = k.dense, k.norm, k.par, k.h, k.ps, k.consts
    with ExitStack() as ctx:
        xn = ctx.enter_context(nc.sbuf_tensor("expert_in", [P, DC, T], F32))
        with ExitStack() as ctx_sel:
            sel = ctx_sel.enter_context(nc.sbuf_tensor("choices", [P, 3, T], F32))
            choose(nc, k, dram, xn, sel)
            build_table(nc, k, dram, sel)
        apply_experts(nc, k, dram, xn)


def choose(nc, k, dram, xn, sel):
    dense, norm, par, h, ps, consts = k.dense, k.norm, k.par, k.h, k.ps, k.consts
    M = 2 * PH
    with ExitStack() as ctx:
        def sb(name, shape, dt=F32):
            return ctx.enter_context(nc.sbuf_tensor(name, shape, dt))

        sem = k.semaphore

        qy = sb("expert_queries", [P, M, T])
        turns = M // BANK
        with nc.Block() as block:
            @block.sync
            def _(sp):
                dense.load(sp, dram["w_query"], turns)

            @block.scalar
            def _(act):
                norm.squares(act, h, xn)
                norm.roots(act, par("eps5"))
                with act.Fori(0, turns) as i:
                    for n in range(BANK):
                        dense.full_wait(act, i, n)
                        act.activation(qy[:, i * BANK + n, :], dense.acc[n], ACT.Copy).then_inc(dense.free[n], 1)

            @block.vector
            def _(dve):
                norm.scale(dve, h, xn, par("g_ffn"))

            @block.tensor
            def _(pe):
                norm.sums(pe, xn)
                norm.out_wait(pe)
                dense.multiply(pe, turns, lambda t: xn[:, t, :], [DC])
        norm.close()
        dense.close(turns)

        keys = sb("sub_keys", [P, M, NK])
        qs = sb("query_tile", [P, M, P])
        sc = sb("key_scores", [P, M, NK])
        v = sb("key_values", [P, M, TK])
        ix = sb("key_indices", [P, M, TK], U32)
        ixf = sb("key_indices_f32", [P, M, TK])
        cand = sb("pair_scores", [P, PH, TK * TK])
        hit = sb("rank_hits", [P, PH, TK, TK])
        fv = sb("pair_values", [P, PH, TK])
        fi = sb("pair_indices", [P, PH, TK], U32)
        rank = sb("pair_ranks", [P, 2, PH, TK], U32)
        rankf = sb("pair_ranks_f32", [P, 2, PH, TK])
        pick = sb("picks_by_token", [P, 3, PH, TK])
        ex = sb("weight_exp", [P, PH, TK])
        sm = sb("weight_sum", [P, PH])
        rs = sb("weight_reciprocal", [P, PH])
        spare = sb("spare_column", [P, 1])
        loaded, staged, scored, copied, chain, shifted, exped, picked, turned, out = (sem(n) for n in (
            "sub_keys_loaded", "query_tile_staged", "key_scores_product", "key_scores_copied", "choose_chain",
            "weights_shifted", "weights_exp", "picks_ready", "picks_transposed", "choices_copied"))
        LINKS = 5 * M + 5 * PH + 11
        with nc.Block() as block:
            @block.sync
            def _(sp):
                sp.dma_start(keys[:, :, :], dram["sub_keys"]).then_inc(loaded, 16)

            @block.gpsimd
            def _(pool):
                with pool.Fori(0, NB) as b:
                    pool.tensor_copy(qs[:, :, :], qy[:, :, bass.ds(b * P, P)]).then_inc(staged, 1)
                    pool.wait_ge(scored, b * 4 + 4)

            @block.tensor
            def _(pe):
                pe.wait_ge(loaded, 16)
                with pe.Fori(0, NB) as b:
                    pe.wait_ge(staged, b + 1)
                    for m in range(M):
                        mm = pe.matmul(ps[:, m // 4, (m % 4) * NK:(m % 4 + 1) * NK], qs[:, m, :], keys[:, m, :],
                                       start=True, stop=True)
                        if m % 4 == 3:
                            mm.then_inc(scored, 1)
                    for j in range(3):
                        pe.wait_ge(picked, b * 3 + (j + 1))
                        mm = pe.transpose(ps[:, 4 + j, 0:P], pick[:, j, :, :].rearrange("p h k -> p (h k)"), consts("ident"))
                        mm.then_inc(turned, 1)
                    pe.wait_ge(out, b * 3 + 3)

            @block.scalar
            def _(act):
                with act.Fori(0, NB) as b:
                    for j in range(4):
                        act.wait_ge(scored, b * 4 + (j + 1))
                        act.activation(sc[:, 4 * j:4 * j + 4, :], ps[:, j, :], ACT.Copy).then_inc(copied, 1)
                    act.wait_ge(shifted, b + 1)
                    act.activation(ex[:, :, :], ex[:, :, :], ACT.Exp).then_inc(exped, 1)
                    for j in range(3):
                        act.wait_ge(turned, b * 3 + (j + 1))
                        act.activation(sel[:, j, bass.ds(b * P, P)], ps[:, 4 + j, 0:P], ACT.Copy).then_inc(out, 1)

            @block.vector
            def _(dve):
                with dve.Fori(0, NB) as b:
                    link = Count(chain, 0, LINKS, b)

                    def top16(rows, values, val, idx):
                        for r in range(2):
                            part = slice(8 * r, 8 * r + 8)
                            dve.memset(spare[:, :], 0.0)
                            for m in range(rows):
                                link.inc(dve.max(val[:, m, part], values[:, m, :]))
                            link.wait(dve)
                            dve.memset(spare[:, :], 0.0)
                            for m in range(rows):
                                link.inc(dve.max_index(idx[:, m, part], val[:, m, part], values[:, m, :]))
                            if r == 0:
                                link.wait(dve)
                                dve.memset(spare[:, :], 0.0)
                                for m in range(rows):
                                    link.inc(dve.match_replace(values[:, m, :], val[:, m, part], values[:, m, :], -3.0e38))
                                link.wait(dve)

                    dve.wait_ge(copied, b * 4 + 4)
                    top16(M, sc, v, ix)
                    link.wait(dve)
                    link.inc(dve.tensor_copy(ixf[:, :, :], ix[:, :, :]))
                    pair = v[:, :, :].rearrange("p (h s) k -> p h s k", s=2)
                    link.inc(dve.tensor_tensor(cand[:, :, :].rearrange("p h (a b) -> p h a b", a=TK),
                                               pair[:, :, 0, :, None].to_broadcast([P, PH, TK, TK]),
                                               pair[:, :, 1, None, :].to_broadcast([P, PH, TK, TK]), ALU.add))
                    link.wait(dve)
                    top16(PH, cand, fv, fi)
                    link.wait(dve)
                    dve.tensor_tensor(ex[:, :, :], fv[:, :, :], fv[:, :, 0:1].to_broadcast([P, PH, TK]),
                                      ALU.subtract).then_inc(shifted, 1)
                    link.inc(dve.tensor_scalar(rank[:, 0, :, :], fi[:, :, :], 4, None, ALU.logical_shift_right))
                    link.inc(dve.tensor_scalar(rank[:, 1, :, :], fi[:, :, :], TK - 1, None, ALU.bitwise_and))
                    link.wait(dve)
                    link.inc(dve.tensor_copy(rankf[:, :, :, :], rank[:, :, :, :]))
                    ixp = ixf[:, :, :].rearrange("p (h s) k -> p h s k", s=2)
                    for j in range(2):
                        link.wait(dve)
                        link.inc(dve.tensor_tensor(hit[:, :, :, :], rankf[:, j, :, :, None].to_broadcast([P, PH, TK, TK]),
                                                   consts("iota")[:, None, None, 0:TK].to_broadcast([P, PH, TK, TK]),
                                                   ALU.is_equal))
                        link.wait(dve)
                        link.inc(dve.tensor_tensor(hit[:, :, :, :], hit[:, :, :, :],
                                                   ixp[:, :, j, None, :].to_broadcast([P, PH, TK, TK]), ALU.mult))
                        link.wait(dve)
                        dve.tensor_reduce(pick[:, j, :, :], hit[:, :, :, :], AXX, ALU.add).then_inc(picked, 1)
                        dve.wait_ge(picked, b * 3 + (j + 1))
                    dve.wait_ge(exped, b + 1)
                    link.inc(dve.tensor_reduce(sm[:, :], ex[:, :, :], AXX, ALU.add))
                    link.wait(dve)
                    link.inc(dve.reciprocal(rs[:, :], sm[:, :]))
                    link.wait(dve)
                    dve.tensor_tensor(pick[:, 2, :, :], ex[:, :, :], rs[:, :, None].to_broadcast([P, PH, TK]),
                                      ALU.mult).then_inc(picked, 1)
                    assert link.n == LINKS


def build_table(nc, k, dram, sel):
    ps, consts = k.ps, k.consts
    QT = 4
    NQ = TB // QT
    with ExitStack() as ctx:
        def sb(name, shape, dt=F32):
            return ctx.enter_context(nc.sbuf_tensor(name, shape, dt))

        sem = k.semaphore

        first = sb("first_key_onehot", [P, 2, QT, NK])
        second = sb("second_key_weighted", [P, 2, QT, NK])
        stage = sb("table_stage", [P, 2, NK, TB])
        made_s, product, read = (sem(n) for n in (
            "onehots_made", "table_product", "table_bank_read"))
        stored = [sem(f"table_stored{n}") for n in range(2)]
        iota = consts("iota")

        def walk(eng, step, after=lambda tb2, par: None, before=lambda tb2, par: None):
            with eng.Fori(0, NTB // 2) as tb2:
                for par in range(2):
                    before(tb2, par)
                    with eng.Fori(0, NQ // 2) as j:
                        for u in range(2):
                            step(par, tb2 * (2 * NQ) + par * NQ + j * 2 + u, u,
                                 tb2 * (2 * TB) + par * TB + j * (2 * QT) + u * QT, j * (2 * QT) + u * QT)
                    after(tb2, par)

        with nc.Block() as block:
            @block.vector
            def _(dve):
                def step(par, n, u, t, tl):
                    dve.wait_ge(product, n + 1)
                    dve.tensor_tensor(first[:, u, :, :], iota[:, None, :].to_broadcast([P, QT, NK]),
                                      sel[:, 0, bass.ds(t, QT)][:, :, None].to_broadcast([P, QT, NK]), ALU.is_equal)
                    for q in range(QT):
                        ins = dve.tensor_scalar(second[:, u, q, :], iota, sel[:, 1, bass.ds(t + q, 1)],
                                                sel[:, 2, bass.ds(t + q, 1)], ALU.is_equal, ALU.mult)
                    ins.then_inc(made_s, 1)
                walk(dve, step)

            @block.tensor
            def _(pe):
                pe.sem_inc(product, 2)

                def step(par, n, u, t, tl):
                    pe.wait_ge(made_s, n + 1)
                    pe.wait_ge(read, n + 1)
                    for q in range(QT):
                        mm = pe.matmul(ps[:, u, q * NK:(q + 1) * NK], second[:, u, q, :], first[:, u, q, :],
                                       start=True, stop=True)
                    mm.then_inc(product, 1)
                walk(pe, step)

            @block.scalar
            def _(act):
                act.sem_inc(read, 2)
                act.sem_inc(stored[0], 16)
                act.sem_inc(stored[1], 16)

                def step(par, n, u, t, tl):
                    act.wait_ge(product, n + 3)
                    act.activation(stage[:, par, :, bass.ds(tl, QT)], ps[:, u, :].rearrange("p (t i) -> p i t", t=QT),
                                   ACT.Copy).then_inc(read, 1)
                walk(act, step, before=lambda tb2, par: act.wait_ge(stored[par], tb2 * 16 + 16))

            @block.sync
            def _(sp):
                with sp.Fori(0, NTB // 2) as tb2:
                    for par in range(2):
                        sp.wait_ge(read, tb2 * (2 * NQ) + (par + 1) * NQ + 2)
                        sp.dma_start(dram["table"][tb2 * 2 + par], stage[:, par, :, :]).then_inc(stored[par], 16)
                for par in range(2):
                    sp.wait_ge(stored[par], 16 * (NTB // 2) + 16)


def apply_experts(nc, k, dram, xn):
    ps, h = k.ps, k.h
    VS = 2
    with ExitStack() as ctx:
        def sb(name, shape, dt=F32):
            return ctx.enter_context(nc.sbuf_tensor(name, shape, dt))

        sem = k.semaphore

        ur = sb("u_ring", [P, BANK, DC * P])
        vr = sb("v_ring", [P, VS, GI * P])
        g = sb("table_then_coefficients", [P, 2, NTB, GI, TB])
        gl = sb("gelu_out", [P, 2, T])
        u_in = [sem(f"u_slot_loaded{n}") for n in range(BANK)]
        v_in = [sem(f"v_slot_loaded{n}") for n in range(VS)]
        g_in = [sem(f"table_group_loaded{n}") for n in range(2)]
        up, gelu, coef, down, added = (sem(n) for n in (
            "u_product", "gelu_done", "coefficients_ready", "v_product", "v_product_added"))
        table = dram["table"].rearrange("b p (g n) -> g p b n", g=NG)

        with nc.Block() as block:
            @block.sync
            def _(sp):
                with sp.Fori(0, NG // 2) as gg:
                    for par in range(2):
                        for n in range(GI):
                            sp.wait_ge(up, gg * (2 * GI) + (par * GI + n + 1))
                            sp.dma_start(ur[:, n % BANK, :], dram["u"][gg * (2 * GI) + (par * GI + n)]).then_inc(u_in[n % BANK], 16)
                        for c in range(DC):
                            sp.wait_ge(down, gg * (2 * DC) + (par * DC + c + 1))
                            sp.dma_start(vr[:, c % VS, :], dram["v"][gg * (2 * DC) + (par * DC + c)]).then_inc(v_in[c % VS], 16)

            @block.gpsimd
            def _(pool):
                for par in range(2):
                    pool.dma_start(g[:, par, :, :, :], table[par]).then_inc(g_in[par], 16)
                with pool.Fori(1, NG // 2) as gg:
                    for par in range(2):
                        pool.wait_ge(down, gg * (2 * DC) + (par * DC - DC + 2))
                        pool.dma_start(g[:, par, :, :, :], table[gg * 2 + par]).then_inc(g_in[par], 16)

            @block.tensor
            def _(pe):
                pe.sem_inc(up, BANK)
                pe.sem_inc(down, 2)
                with pe.Fori(0, NG // 2) as gg:
                    for par in range(2):
                        for n in range(GI):
                            pe.wait_ge(gelu, gg * (2 * GI) + (par * GI + n + 1))
                            pe.wait_ge(u_in[n % BANK], gg * (2 * 16 * GI // BANK) + 16 * (par * GI // BANK + n // BANK + 1))
                            for t in range(DC):
                                mm = pe.matmul(ps[:, n % BANK, :], ur[:, n % BANK, t * P:(t + 1) * P], xn[:, t, :],
                                               start=(t == 0), stop=(t == DC - 1))
                            mm.then_inc(up, 1)
                        for c in range(DC):
                            if c == 0:
                                pe.wait_ge(coef, gg * (2 * GI) + ((par + 1) * GI + 2))
                            pe.wait_ge(added, gg * (2 * DC) + (par * DC + c + 1))
                            pe.wait_ge(v_in[c % VS], gg * (2 * 16 * DC // VS) + 16 * (par * DC // VS + c // VS + 1))
                            for n in range(GI):
                                mm = pe.matmul(ps[:, 4 + c % 2, :], vr[:, c % VS, n * P:(n + 1) * P], g[:, par, :, n, :],
                                               start=(n == 0), stop=(n == GI - 1))
                            mm.then_inc(down, 1)

            @block.scalar
            def _(act):
                act.sem_inc(gelu, BANK)
                with act.Fori(0, NG // 2) as gg:
                    for par in range(2):
                        for n in range(GI):
                            act.wait_ge(up, gg * (2 * GI) + (par * GI + n + 1 + BANK))
                            act.wait_ge(coef, gg * (2 * GI) + (par * GI + n + 1))
                            act.activation(gl[:, n % 2, :], ps[:, n % BANK, :], ACT.Gelu).then_inc(gelu, 1)

            @block.vector
            def _(dve):
                dve.sem_inc(coef, 2)
                dve.sem_inc(added, 2)
                with dve.Fori(0, NG // 2) as gg:
                    for par in range(2):
                        dve.wait_ge(g_in[par], gg * 16 + 16)
                        for n in range(GI):
                            dve.wait_ge(gelu, gg * (2 * GI) + (par * GI + n + 1 + BANK))
                            dve.tensor_tensor(g[:, par, :, n, :], g[:, par, :, n, :],
                                              gl[:, n % 2, :].rearrange("p (b t) -> p b t", b=NTB), ALU.mult).then_inc(coef, 1)
                        for c in range(DC):
                            dve.wait_ge(down, gg * (2 * DC) + (par * DC + c + 1 + 2))
                            dve.tensor_tensor(h[:, c, :], h[:, c, :], ps[:, 4 + c % 2, :], ALU.add).then_inc(added, 1)


def norm_in_place(nc, k, gain, eps):
    norm, h = k.norm, k.h
    with ExitStack() as ctx:
        sq = ctx.enter_context(nc.sbuf_tensor("final_norm_squares", [P, DC, T], F32))
        with nc.Block() as block:
            @block.scalar
            def _(act):
                norm.squares(act, h, sq)
                norm.roots(act, k.par(eps))

            @block.vector
            def _(dve):
                norm.scale(dve, h, h, k.par(gain))

            @block.tensor
            def _(pe):
                norm.sums(pe, sq)
    norm.close()


def second_mixer(nc, k, dram):
    with ExitStack() as ctx:
        gate = ctx.enter_context(nc.sbuf_tensor("rwkv_gate_then_out", [P, RC, T], F32))
        with ExitStack() as inner:
            bonus = inner.enter_context(nc.sbuf_tensor("rwkv_bonus", [P, RC, T], F32))
            ends = inner.enter_context(nc.sbuf_tensor("rwkv_chunk_decay", [P, 2 * RC, NCH], F32))
            rwkv_inputs(nc, k, dram, gate, bonus, ends)
            ys = inner.enter_context(nc.sbuf_tensor("rwkv_scan_out", [P, 2 * RC, T], F32))
            rwkv_scan(nc, k, dram, ends, ys)
            rwkv_output(nc, k, gate, bonus, ys)
        out = ctx.enter_context(nc.sbuf_tensor("gla_out", [P, RC, T], F32))
        gla(nc, k, dram, out)
        with ExitStack() as inner:
            u = inner.enter_context(nc.sbuf_tensor("mixer_projected", [P, DC, T], F32))
            sq = inner.enter_context(nc.sbuf_tensor("mixer_projected_squares", [P, DC, T], F32))
            projected(nc, k, dram["w_out"], 2, lambda t: (gate if t < RC else out)[:, t % RC, :], [DC], u, sq, "g_mix_post")


def projected(nc, k, w, turns, rhs, kts, u, sq, gain, extra=None):
    dense, norm, par, h = k.dense, k.norm, k.par, k.h
    per = len(kts)
    with nc.Block() as block:
        @block.sync
        def _(sp):
            dense.load(sp, w, turns, per)

        @block.scalar
        def _(act):
            with act.Fori(0, turns) as i:
                for n in range(BANK):
                    dense.full_wait(act, i, n, per)
                    act.activation(u[:, i * BANK + n, :], dense.acc[n], ACT.Copy).then_inc(dense.free[n], 1)
            for n in range(BANK):
                act.wait_ge(dense.free[n], dense.read_value(turns - 1, n))
            norm.squares(act, u, sq)
            norm.roots(act, par("eps6"))

        @block.vector
        def _(dve):
            norm.scale(dve, u, u, par(gain), add=h)

        @block.tensor
        def _(pe):
            dense.multiply(pe, turns, rhs, kts)
            norm.sums(pe, sq)
    norm.close(add=True)
    dense.close(turns, per)


DECAY = -float(np.exp(-0.5))


def rwkv_inputs(nc, k, dram, gate, bonus, ends):
    dense, norm, par, h, ps, consts = k.dense, k.norm, k.par, k.h, k.ps, k.consts
    with ExitStack() as ctx:
        def sb(name, shape, dt=F32):
            return ctx.enter_context(nc.sbuf_tensor(name, shape, dt))

        sem = k.semaphore

        NZ = 15
        z = sb("rwkv_z", [P, NZ, T + 2])
        with ExitStack() as inner:
            xn = inner.enter_context(nc.sbuf_tensor("mix_in", [P, DC, T], F32))
            low = inner.enter_context(nc.sbuf_tensor("gla_low_rank_in", [P, T], F32))
            tmp = inner.enter_context(nc.sbuf_tensor("shift_sum", [P, BANK, T], F32))
            zeroed, shifted, saved = (sem(n) for n in ("z_margins_zeroed", "shift_chain", "mix_in_saved"))
            turns = 4
            with nc.Block() as block:
                @block.sync
                def _(sp):
                    dense.load(sp, dram["w_rwkv"], turns)
                    norm.out_wait(sp)
                    sp.dma_start(dram["mix_in"], xn[:, :, :]).then_inc(saved, 16)
                    for n in range(BANK):
                        sp.wait_ge(dense.free[n], dense.read_value(turns - 1, n))
                    sp.dma_start(dram["gla_low"], low[:, :]).then_inc(saved, 16)
                    sp.wait_ge(saved, 32)

                @block.gpsimd
                def _(pool):
                    pool.memset(z[:, :, 0:1], 0.0).then_inc(zeroed, 1)
                    pool.memset(z[:, :, T + 1:T + 2], 0.0).then_inc(zeroed, 1)

                @block.scalar
                def _(act):
                    norm.squares(act, h, xn)
                    norm.roots(act, par("eps6"))
                    for i in range(turns):
                        for n in range(BANK):
                            m = i * BANK + n
                            dense.full_wait(act, i, n)
                            act.activation(z[:, m, 1:T + 1] if m < NZ else low[:, :], dense.acc[n],
                                           ACT.Copy).then_inc(dense.free[n], 1)

                @block.vector
                def _(dve):
                    norm.scale(dve, h, xn, par("g_mix_pre"))
                    dve.wait_ge(zeroed, 2)
                    link = Count(shifted)
                    for i in range(turns):
                        m0, m1 = i * BANK, min((i + 1) * BANK, NZ)
                        for n in range(m1 - m0):
                            dve.wait_ge(dense.free[n], dense.read_value(i, n))
                        s = tmp[:, 0:m1 - m0, :]
                        link.inc(dve.tensor_tensor(s, z[:, m0:m1, 0:T], z[:, m0:m1, 2:T + 2], ALU.add))
                        link.wait(dve)
                        link.inc(dve.scalar_tensor_tensor(out=s, in0=s, scalar=0.5, in1=z[:, m0:m1, 1:T + 1],
                                                          op0=ALU.mult, op1=ALU.subtract))
                        link.wait(dve)
                        for m in range(m0, m1):
                            link.inc(dve.scalar_tensor_tensor(out=z[:, m, 1:T + 1], in0=tmp[:, m - m0, :],
                                                              scalar=par("mu")[:, m:m + 1], in1=z[:, m, 1:T + 1],
                                                              op0=ALU.mult, op1=ALU.add))
                        link.wait(dve)

                @block.tensor
                def _(pe):
                    norm.sums(pe, xn)
                    norm.out_wait(pe)
                    dense.multiply(pe, turns, lambda t: xn[:, t, :], [DC])
            norm.close()
            dense.close(turns)

        def zc(m):
            return z[:, m, 1:T + 1]

        R, K, V, W, A, G = 0, RC, 2 * RC, 3 * RC, 3 * RC + 1, 3 * RC + 2
        w_up, a_up, g_up = sb("decay_up", [P, 2, RC * P]), sb("a_up", [P, RC * P]), sb("gate_up", [P, RC * P])
        lw = sb("decay_sigmoid", [P, 2 * RC, T])
        cum = sb("decay_sum", [P, 2, T])
        aa = sb("a_then_b", [P, RC, T])
        kk = sb("kk", [P, RC, T])
        sq = sb("kk_squares_then_rkr", [P, RC, T])
        e = sb("decay_exps", [P, 2, 3, T])
        st = sb("scan_stage", [P, 2, 4, T])
        vr = sb("v_reversed", [P, RC, T])
        loaded, low_ready, made, lwd, ad, gd, raw, sqd, clamped, logs, root, rkr, chain, cumd, exd, unit = (sem(n) for n in (
            "rwkv_small_weights_loaded", "low_rank_activated", "low_rank_product", "decay_ready", "a_ready",
            "gate_ready", "kk_unscaled", "kk_squares_ready", "kk_squares_clamped", "kk_logs", "kk_roots", "r_k_products",
            "rwkv_inputs_chain", "decay_sums_ready", "decay_exps_ready",
            "unit_staged"))
        stored = [sem(f"unit_stored{n}") for n in range(2)]
        tmp = sb("rwkv_inputs_tmp", [P, RC, T])
        vst = sem("reversed_v_stored")
        with nc.Block() as block:
            @block.sync
            def _(sp):
                for dst, name in ((w_up[:, :, :], "w_up"), (a_up[:, :], "a_up"), (g_up[:, :], "g_up")):
                    sp.dma_start(dst, dram[name]).then_inc(loaded, 16)
                for c in range(RC):
                    sp.dma_start(dram["scan"][:, 4, c, :], zc(V + c)).then_inc(vst, 16)
                for u in range(2 * RC):
                    sp.wait_ge(unit, u + 1)
                    sp.dma_start(dram["scan"][:, 0:4, u, :], st[:, u % 2, :, :]).then_inc(stored[u % 2], 16)
                sp.dma_start(dram["scan"][:, 4, RC:2 * RC, :], vr[:, :, :]).then_inc(vst, 16)
                for n in range(2):
                    sp.wait_ge(stored[n], 16 * RC)
                sp.wait_ge(vst, 16 * (RC + 1))

            @block.tensor
            def _(pe):
                pe.wait_ge(loaded, 48)
                pe.wait_ge(low_ready, 2)
                for n in range(2 * RC):
                    pe.matmul(ps[:, n, :], w_up[:, n // RC, (n % RC) * P:(n % RC + 1) * P], zc(W),
                              start=True, stop=True).then_inc(made, 1)
                for n in range(RC):
                    pe.wait_ge(lwd, n + 1)
                    pe.matmul(ps[:, n, :], a_up[:, n * P:(n + 1) * P], zc(A), start=True, stop=True).then_inc(made, 1)
                for n in range(RC):
                    pe.wait_ge(lwd, RC + n + 1)
                    pe.matmul(ps[:, 4 + n, :], g_up[:, n * P:(n + 1) * P], zc(G), start=True, stop=True).then_inc(made, 1)
                for n in range(RC):
                    pe.wait_ge(ad, n + 1)
                    pe.wait_ge(sqd, n + 1)
                    pe.matmul(ps[:, n, :], consts("half"), sq[:, n, :], start=True, stop=True).then_inc(made, 1)
                for n in range(RC):
                    pe.wait_ge(gd, n + 1)
                    pe.wait_ge(rkr, n + 1)
                    pe.matmul(ps[:, 4 + n, :], consts("half"), tmp[:, n, :], start=True, stop=True).then_inc(made, 1)

            @block.scalar
            def _(act):
                act.activation(zc(W), zc(W), ACT.Tanh).then_inc(low_ready, 1)
                act.activation(zc(G), zc(G), ACT.Sigmoid).then_inc(low_ready, 1)
                for n in range(2 * RC):
                    act.wait_ge(made, n + 1)
                    dst = lw[:, n, :] if n < RC else lw[:, n, ::-1]
                    act.activation(dst, ps[:, n, :], ACT.Sigmoid, bias=par("w0")[:, n:n + 1]).then_inc(lwd, 1)
                for n in range(RC):
                    act.wait_ge(made, 2 * RC + n + 1)
                    act.activation(aa[:, n, :], ps[:, n, :], ACT.Sigmoid, bias=par("a0")[:, n:n + 1]).then_inc(ad, 1)
                for n in range(RC):
                    act.wait_ge(made, 3 * RC + n + 1)
                    act.activation(gate[:, n, :], ps[:, 4 + n, :], ACT.Copy).then_inc(gd, 1)
                act.wait_ge(raw, RC)
                for n in range(RC):
                    act.activation(sq[:, n, :], kk[:, n, :], ACT.Square).then_inc(sqd, 1)
                for n in range(RC):
                    act.wait_ge(clamped, n + 1)
                    act.activation(sq[:, n, :], sq[:, n, :], ACT.Ln).then_inc(logs, 1)
                for n in range(RC):
                    act.wait_ge(logs, n + 1)
                    act.activation(sq[:, n, :], sq[:, n, :], ACT.Exp, scale=-0.5).then_inc(root, 1)
                for u in range(2 * RC):
                    if u >= 2:
                        act.wait_ge(unit, u - 1)
                    for j, sc in enumerate((DECAY, -DECAY, DECAY)):
                        if j == 0:
                            act.wait_ge(cumd, 2 * u + 1)
                        if j == 2:
                            act.wait_ge(cumd, 2 * u + 2)
                        src = cum[:, u % 2, :] if j < 2 else lw[:, u, :]
                        act.activation(e[:, u % 2, j, :], src, ACT.Exp, scale=sc).then_inc(exd, 1)

            @block.vector
            def _(dve):
                link = Count(chain)
                for n in range(RC):
                    dve.tensor_scalar(kk[:, n, :], zc(K + n), par("k_k")[:, n:n + 1], None, ALU.mult).then_inc(raw, 1)
                for n in range(RC):
                    link.inc(dve.tensor_copy(vr[:, n, ::-1], zc(V + n)))
                dve.wait_ge(ad, RC)
                for n in range(RC):
                    link.inc(dve.tensor_scalar(tmp[:, n, :], aa[:, n, :], -1.0, par("k_a")[:, n:n + 1], ALU.add, ALU.mult))
                link.wait(dve)
                for n in range(RC):
                    link.inc(dve.scalar_tensor_tensor(out=zc(K + n), in0=tmp[:, n, :], scalar=1.0, in1=zc(K + n),
                                                      op0=ALU.add, op1=ALU.mult))
                for n in range(RC):
                    dve.wait_ge(made, 4 * RC + n + 1)
                    dve.tensor_scalar(sq[:, n, :], ps[:, n, :], 1e-24, None, ALU.max).then_inc(clamped, 1)
                link.wait(dve)
                for n in range(RC):
                    dve.scalar_tensor_tensor(out=tmp[:, n, :], in0=zc(R + n), scalar=par("r_k")[:, n:n + 1], in1=zc(K + n),
                                             op0=ALU.mult, op1=ALU.mult).then_inc(rkr, 1)
                dve.wait_ge(root, RC)
                for n in range(RC):
                    link.inc(dve.tensor_tensor(kk[:, n, :], kk[:, n, :], sq[:, n, :], ALU.mult))
                link.wait(dve)
                for n in range(RC):
                    link.inc(dve.tensor_tensor(aa[:, n, :], aa[:, n, :], kk[:, n, :], ALU.mult))
                for n in range(RC):
                    dve.wait_ge(made, 5 * RC + n + 1)
                    link.inc(dve.tensor_tensor(bonus[:, n, :], ps[:, 4 + n, :], zc(V + n), ALU.mult))
                link.wait(dve)
                for u in range(2 * RC):
                    c = u % RC
                    time = slice(None) if u < RC else slice(None, None, -1)
                    if u >= 2:
                        dve.wait_ge(exd, 3 * (u - 1))
                    dve.wait_ge(lwd, u + 1)
                    dve.tensor_tensor_scan(cum[:, u % 2, :], consts("chunk_start"), lw[:, u, :], 0.0,
                                           ALU.mult, ALU.add).then_inc(cumd, 1)
                    dve.wait_ge(cumd, 2 * u + 1)
                    dve.tensor_tensor(lw[:, u, :], cum[:, u % 2, :], lw[:, u, :], ALU.subtract).then_inc(cumd, 1)
                    dve.wait_ge(exd, 3 * (u + 1))
                    if u >= 2:
                        dve.wait_ge(stored[u % 2], 16 * (u // 2))
                    ev = [e[:, u % 2, j, :] for j in range(3)]
                    dve.scalar_tensor_tensor(out=st[:, u % 2, 0, :], in0=kk[:, c, time], scalar=-1.0, in1=ev[2],
                                             op0=ALU.mult, op1=ALU.mult)
                    dve.tensor_tensor(st[:, u % 2, 1, :], zc(R + c)[:, time], ev[0], ALU.mult)
                    dve.tensor_tensor(st[:, u % 2, 2, :], aa[:, c, time], ev[1], ALU.mult)
                    dve.tensor_copy(ends[:, u, :], ev[0][:, C - 1::C])
                    dve.tensor_tensor(st[:, u % 2, 3, :], zc(K + c)[:, time], ev[1], ALU.mult).then_inc(unit, 1)


class Bank:

    def __init__(self, k, scan, number, uses):
        self.ps = k.ps[:, number, :]
        self.made = k.semaphore(f"{scan}_bank{number}_made")
        self.read = k.semaphore(f"{scan}_bank{number}_read")
        self.uses = uses
        self.reads = sum(r for _, r in uses)

    def place(self, name):
        n = [u for u, _ in self.uses].index(name)
        return n, sum(r for _, r in self.uses[:n]), self.uses[n][1]

    def free(self, pe, i, name):
        pe.wait_ge(self.read, i * self.reads + (self.place(name)[1] + 1))

    def full(self, eng, i, name):
        eng.wait_ge(self.made, i * len(self.uses) + (self.place(name)[0] + 2))

    def taken(self, eng, i, name):
        _, before, own = self.place(name)
        eng.wait_ge(self.read, i * self.reads + (before + own + 1))


def rwkv_scan(nc, k, dram, ends, ys):
    ps, consts = k.ps, k.consts
    U, H = 2 * RC, RC
    LV = 6
    with ExitStack() as ctx:
        def sb(name, shape, dt=F32):
            return ctx.enter_context(nc.sbuf_tensor(name, shape, dt))

        sem = k.semaphore

        cb = sb("chunk_vectors", [P, 2, 5, U, C])
        bd = sb("block_diagonal_vectors", [P, 4, U, P])
        bt, kt, vt = sb("b_by_token", [P, U, P]), sb("k_by_token", [P, U, P]), sb("v_by_token", [P, U, P])
        vc = sb("v_compact", [P, U, C])
        L = sb("L_transposed", [P, U, C])
        mb, mk = sb("b_r_products", [P, U, C]), sb("k_r_products", [P, U, C])
        lk = sb("k_a_products", [P, U, P])
        bl = sb("L_level", [P, 2, U, P])
        wc, wb = sb("W_compact", [P, U, C]), sb("W_block_diagonal", [P, U, P])
        X, XT = sb("X_compact", [P, U, C]), sb("X_transposed", [P, U, P])
        rr, sa, sab = sb("right_side", [P, U, C]), sb("sa_compact", [P, U, C]), sb("sa_block_diagonal", [P, U, P])
        S, Sb = sb("state", [P, U, C]), sb("state_block_diagonal", [P, U, P])
        zeroed = sem("block_diagonals_zeroed")
        cb_in = [sem(f"chunk_vectors_loaded{n}") for n in range(2)]
        built = [sem(f"vectors_built{g}") for g in range(2)]
        lev = [sem(f"L_levels_built{g}") for g in range(2)]
        sbuilt = [sem(f"state_built{g}") for g in range(2)]
        ready = [sem(f"X_started{g}") for g in range(2)]
        chain = [sem(f"state_chain{g}") for g in range(2)]
        KINDS = ((2, 0), (3, 1), (0, 2), (4, 3))

        def uses(g):
            lv = range(LV)
            return [
                Bank(k, "rwkv", 4 * g, [("scores_b", 1)] + [(f"W{l}", 1) for l in lv] + [("sa", 1)]),
                Bank(k, "rwkv", 4 * g + 1, [("scores_k", 1)] + [(f"dX{l}", 1) for l in lv[:-1]] + [("y", 1)]),
                Bank(k, "rwkv", 4 * g + 2, [("b_t", 1), ("v_t", 1)] + [(f"dXT{l}", 1) for l in lv] + [("S", 1)]),
                Bank(k, "rwkv", 4 * g + 3, [("k_t", 1), ("v_c", 1), ("rhs", 1)])]

        banks = [uses(g) for g in range(2)]

        def half(g):
            return slice(g * H, g * H + H)

        with nc.Block() as block:
            @block.sync
            def _(sp):
                for n in range(2):
                    sp.dma_start(cb[:, n, :, :, :].rearrange("p a u t -> p (a u) t"),
                                 dram["scan"].rearrange("p a u t -> p (a u) t")[:, :, n * C:(n + 1) * C]).then_inc(cb_in[n], 16)
                with sp.Fori(0, NCH // 2 - 1) as ii:
                    for n in range(2):
                        for g in range(2):
                            banks[g][1].full(sp, ii * 2 + n, "y")
                        sp.dma_start(cb[:, n, :, :, :].rearrange("p a u t -> p (a u) t"),
                                     dram["scan"].rearrange("p a u t -> p (a u) t")[:, :, bass.ds(ii * (2 * C) + (n + 2) * C, C)]
                                     ).then_inc(cb_in[n], 16)

            @block.gpsimd
            def _(pool):
                for t in (bd, lk, bl, wb, sab, Sb, S):
                    pool.memset(t[tuple([slice(None)] * len(t.shape))], 0.0).then_inc(zeroed, 1)
                pool.wait_ge(zeroed, 7)

                def place(dst, src, r):
                    return pool.tensor_tensor(dst, src, consts("ones")[r, None, 0:C].to_broadcast([C, H, C]), ALU.mult)

                with pool.Fori(0, NCH // 2) as ii:
                    for n in range(2):
                        i = ii * 2 + n
                        pool.wait_ge(cb_in[n], ii * 16 + 16)
                        for g in range(2):
                            pool.wait_ge(banks[g][2].made, i * len(banks[g][2].uses) + 1)
                            for src, dst in KINDS:
                                for hh in range(2):
                                    r = slice(hh * C, hh * C + C)
                                    ins = place(bd[r, dst, half(g), r], cb[r, n, src, half(g), :], r)
                                ins.then_inc(built[g], 1)
                        for l in range(LV):
                            for g in range(2):
                                if l == 0:
                                    banks[g][0].taken(pool, i, "scores_b")
                                if l >= 2:
                                    banks[g][0].full(pool, i, f"W{l - 2}")
                                for hh in range(2):
                                    r = slice(hh * C, hh * C + C)
                                    m = consts("levels")[r, None, l * C:(l + 1) * C].to_broadcast([C, H, C])
                                    ins = pool.tensor_tensor(bl[r, l % 2, half(g), r], L[r, half(g), :], m, ALU.mult)
                                ins.then_inc(lev[g], 1)
                        for g in range(2):
                            banks[g][2].taken(pool, i, "S")
                            for hh in range(2):
                                r = slice(hh * C, hh * C + C)
                                ins = place(Sb[r, half(g), r], S[r, half(g), :], r)
                            ins.then_inc(sbuilt[g], 1)

            @block.tensor
            def _(pe):
                for g in range(2):
                    for b in banks[g]:
                        pe.sem_inc(b.made, 1)
                    pe.sem_inc(sbuilt[g], 1)
                pe.wait_ge(zeroed, 7)
                with pe.Fori(0, NCH // 2) as ii:
                    for n in range(2):
                        i = ii * 2 + n

                        def product(g, b, name, width, terms, transpose=False):
                            bank = banks[g][b]
                            bank.free(pe, i, name)
                            for u in range(H):
                                out = bank.ps[:, u * width:(u + 1) * width]
                                for j, (lhs, rhs) in enumerate(terms):
                                    if transpose:
                                        mm = pe.transpose(out, lhs(g * H + u), consts("ident"))
                                    else:
                                        mm = pe.matmul(out, lhs(g * H + u), rhs(g * H + u), start=(j == 0),
                                                       stop=(j == len(terms) - 1))
                            mm.then_inc(bank.made, 1)

                        def blk(kind):
                            return lambda u: bd[:, kind, u, :]

                        for g in range(2):
                            pe.wait_ge(built[g], i * 4 + 4)
                            product(g, 0, "scores_b", P, [(blk(0), lambda u: cb[:, n, 0:2, u, :])])
                            product(g, 1, "scores_k", P, [(blk(1), lambda u: cb[:, n, 0:2, u, :])])
                        for g in range(2):
                            product(g, 2, "b_t", P, [(blk(0), None)], True)
                            product(g, 3, "k_t", P, [(blk(1), None)], True)
                        for g in range(2):
                            product(g, 2, "v_t", P, [(blk(3), None)], True)
                            product(g, 3, "v_c", C, [(blk(3), lambda u: consts("eye2"))])
                        for l in range(LV):
                            for g in range(2):
                                pe.wait_ge(lev[g], i * LV + (l + 1))
                                if l == 0:
                                    pe.wait_ge(ready[g], i + 1)
                                elif l:
                                    banks[g][1].taken(pe, i, f"dX{l - 1}")
                                product(g, 0, f"W{l}", C, [(lambda u: bl[:, l % 2, u, :], lambda u: X[:, u, :])])
                            for g in range(2):
                                banks[g][0].taken(pe, i, f"W{l}")
                                if l:
                                    banks[g][2].taken(pe, i, f"dXT{l - 1}")
                                if l < LV - 1:
                                    product(g, 1, f"dX{l}", C, [(lambda u: XT[:, u, :], lambda u: wc[:, u, :])])
                                product(g, 2, f"dXT{l}", P, [(lambda u: wb[:, u, :], lambda u: XT[:, u, :])])
                        for g in range(2):
                            pe.wait_ge(sbuilt[g], i + 1)
                            banks[g][1].taken(pe, i, "scores_k")
                            banks[g][3].taken(pe, i, "v_c")
                            product(g, 3, "rhs", C, [(blk(2), lambda u: S[:, u, :]),
                                                     (lambda u: lk[:, u, :], lambda u: vc[:, u, :])])
                        for g in range(2):
                            banks[g][3].taken(pe, i, "rhs")
                            banks[g][2].taken(pe, i, f"dXT{LV - 1}")
                            product(g, 0, "sa", C, [(lambda u: XT[:, u, :], lambda u: rr[:, u, :])])
                        for g in range(2):
                            banks[g][0].taken(pe, i, "sa")
                            product(g, 1, "y", C, [(lambda u: Sb[:, u, :], lambda u: cb[:, n, 1, u, :]),
                                                   (lambda u: sab[:, u, :], lambda u: mb[:, u, :]),
                                                   (lambda u: vt[:, u, :], lambda u: mk[:, u, :])])
                            product(g, 2, "S", C, [(lambda u: bt[:, u, :], lambda u: sa[:, u, :]),
                                                   (lambda u: kt[:, u, :], lambda u: vc[:, u, :])])

            @block.scalar
            def _(act):
                act.wait_ge(zeroed, 7)

                def both_forms(g, src, compact, block_diagonal):
                    act.activation(compact[:, half(g), :], src, ACT.Copy)
                    for hh in range(2):
                        r = slice(hh * C, hh * C + C)
                        ins = act.activation(block_diagonal[r, half(g), r], src[r, :, :], ACT.Copy)
                    ins.then_inc(banks[g][0].read, 1)

                with act.Fori(0, NCH // 2) as ii:
                    for n in range(2):
                        i = ii * 2 + n

                        def take(g, b, name, dst, width):
                            banks[g][b].full(act, i, name)
                            act.activation(dst, banks[g][b].ps[:, 0:H * width].rearrange("p (u t) -> p u t", u=H),
                                           ACT.Copy).then_inc(banks[g][b].read, 1)

                        for g in range(2):
                            take(g, 2, "b_t", bt[:, half(g), :], P)
                            take(g, 3, "k_t", kt[:, half(g), :], P)
                        for g in range(2):
                            take(g, 2, "v_t", vt[:, half(g), :], P)
                            take(g, 3, "v_c", vc[:, half(g), :], C)
                        for l in range(LV):
                            for g in range(2):
                                bank = banks[g][0]
                                bank.full(act, i, f"W{l}")
                                src = bank.ps[:, 0:H * C].rearrange("p (u t) -> p u t", u=H)
                                both_forms(g, src, wc, wb)
                        for g in range(2):
                            take(g, 3, "rhs", rr[:, half(g), :], C)
                        for g in range(2):
                            banks[g][0].full(act, i, "sa")
                            both_forms(g, banks[g][0].ps[:, 0:H * C].rearrange("p (u t) -> p u t", u=H), sa, sab)
                        for g in range(2):
                            bank = banks[g][1]
                            bank.full(act, i, "y")
                            act.activation(ys[:, half(g), bass.ds(i * C, C)],
                                           bank.ps[:, 0:H * C].rearrange("p (u t) -> p u t", u=H),
                                           ACT.Copy).then_inc(bank.read, 1)

            @block.vector
            def _(dve):
                for g in range(2):
                    for b in banks[g]:
                        dve.sem_inc(b.read, 1)
                dve.wait_ge(zeroed, 7)
                with dve.Fori(0, NCH // 2) as ii:
                    for n in range(2):
                        i = ii * 2 + n

                        def view(g, b, width):
                            return banks[g][b].ps[:, 0:H * width].rearrange("p (u t) -> p u t", u=H)

                        def mask(name, rows=slice(None)):
                            m = consts(name)[rows, None, :]
                            return m.to_broadcast([m.shape[0], H, C])

                        for g in range(2):
                            dve.tensor_copy(X[:, half(g), :], mask("eye2"))
                            dve.tensor_copy(XT[:, half(g), :], consts("ident")[:, None, :].to_broadcast([P, H, P])
                                            ).then_inc(ready[g], 1)
                            banks[g][0].full(dve, i, "scores_b")
                            src = view(g, 0, P)
                            dve.tensor_tensor(L[:, half(g), :], src[:, :, 0:C], mask("upper"), ALU.mult)
                            dve.tensor_tensor(mb[:, half(g), :], src[:, :, C:P], mask("upper_eq"),
                                              ALU.mult).then_inc(banks[g][0].read, 1)
                        for g in range(2):
                            banks[g][1].full(dve, i, "scores_k")
                            src = view(g, 1, P)
                            for hh in range(2):
                                r = slice(hh * C, hh * C + C)
                                dve.tensor_tensor(lk[r, half(g), r], src[r, :, 0:C], mask("upper", r), ALU.mult)
                            dve.tensor_tensor(mk[:, half(g), :], src[:, :, C:P], mask("upper_eq"),
                                              ALU.mult).then_inc(banks[g][1].read, 1)
                        for l in range(LV):
                            for g in range(2):
                                if l == 0:
                                    dve.wait_ge(ready[g], i + 1)
                                if l < LV - 1:
                                    banks[g][1].full(dve, i, f"dX{l}")
                                    if l:
                                        banks[g][1].taken(dve, i, f"dX{l - 1}")
                                    dve.tensor_tensor(X[:, half(g), :], view(g, 1, C), X[:, half(g), :],
                                                      ALU.add).then_inc(banks[g][1].read, 1)
                                banks[g][2].full(dve, i, f"dXT{l}")
                                if l:
                                    banks[g][2].taken(dve, i, f"dXT{l - 1}")
                                dve.tensor_tensor(XT[:, half(g), :], view(g, 2, P), XT[:, half(g), :],
                                                  ALU.add).then_inc(banks[g][2].read, 1)
                        for g in range(2):
                            bank = banks[g][2]
                            bank.full(dve, i, "S")
                            dve.tensor_tensor(S[:, half(g), :], view(g, 2, C), S[:, half(g), :], ALU.add).then_inc(chain[g], 1)
                            dve.wait_ge(chain[g], i + 1)
                            dve.tensor_tensor(S[:, half(g), :], S[:, half(g), :],
                                              ends[:, half(g), bass.ds(i, 1)].to_broadcast([P, H, C]),
                                              ALU.mult).then_inc(bank.read, 1)


def rwkv_output(nc, k, gate, bonus, ys):
    ps, par, consts, y = k.ps, k.par, k.consts, ys
    with ExitStack() as ctx:
        def sb(name, shape, dt=F32):
            return ctx.enter_context(nc.sbuf_tensor(name, shape, dt))

        sem = k.semaphore

        sq = sb("group_squares", [P, RC, T])
        sums, chain, mean, cen, sqd, var, lnd, root = (sem(n) for n in (
            "directions_summed", "group_chain", "group_mean", "centred", "group_squares_ready", "group_variance",
            "group_log", "group_root"))
        with nc.Block() as block:
            @block.tensor
            def _(pe):
                for n in range(RC):
                    pe.wait_ge(sums, n + 1)
                    pe.matmul(ps[:, n, :], consts("half"), y[:, n, :], start=True, stop=True).then_inc(mean, 1)
                for n in range(RC):
                    pe.wait_ge(sqd, n + 1)
                    pe.matmul(ps[:, 4 + n, :], consts("half"), sq[:, n, :], start=True, stop=True).then_inc(var, 1)

            @block.scalar
            def _(act):
                for n in range(RC):
                    act.wait_ge(cen, n + 1)
                    act.activation(sq[:, n, :], y[:, n, :], ACT.Square).then_inc(sqd, 1)
                for n in range(RC):
                    act.wait_ge(var, n + 1)
                    act.activation(sq[:, n, :], ps[:, 4 + n, :], ACT.Ln, bias=par("eps_gn"), scale=1.0 / HD).then_inc(lnd, 1)
                act.wait_ge(lnd, RC)
                for n in range(RC):
                    act.activation(sq[:, n, :], sq[:, n, :], ACT.Exp, scale=-0.5).then_inc(root, 1)

            @block.vector
            def _(dve):
                for n in range(RC):
                    dve.tensor_tensor(y[:, n, :], y[:, n, :], y[:, RC + n, ::-1], ALU.add).then_inc(sums, 1)
                for n in range(RC):
                    dve.wait_ge(mean, n + 1)
                    dve.scalar_tensor_tensor(out=y[:, n, :], in0=ps[:, n, :], scalar=-1.0 / HD, in1=y[:, n, :],
                                             op0=ALU.mult, op1=ALU.add).then_inc(cen, 1)
                link = Count(chain)
                dve.wait_ge(sqd, RC)
                for n in range(RC):
                    dve.wait_ge(root, n + 1)
                    link.inc(dve.scalar_tensor_tensor(out=y[:, n, :], in0=y[:, n, :], scalar=par("ln_w")[:, n:n + 1],
                                                      in1=sq[:, n, :], op0=ALU.mult, op1=ALU.mult))
                link.wait(dve)
                for n in range(RC):
                    link.inc(dve.scalar_tensor_tensor(out=y[:, n, :], in0=y[:, n, :], scalar=par("ln_b")[:, n:n + 1],
                                                      in1=bonus[:, n, :], op0=ALU.add, op1=ALU.add))
                link.wait(dve)
                dve.tensor_tensor(gate[:, :, :], y[:, 0:RC, :], gate[:, :, :], ALU.mult)


GLA_DK = 64
GLA_TEMP = 16.0
EXP_MAX = 80.0


def gla(nc, k, dram, out):
    dense, par, ps, consts = k.dense, k.par, k.ps, k.consts
    U = 2 * GP
    MID = C // 2 - 1
    with ExitStack() as ctx:
        def sb(name, shape, dt=F32):
            return ctx.enter_context(nc.sbuf_tensor(name, shape, dt))

        sem = k.semaphore

        gg = sb("gla_gate", [P, RC, T])
        v = sb("gla_v", [P, 2, RC, T])
        q, kx = sb("gla_q_scaled", [P, U, T]), sb("gla_k_scaled", [P, U, T])
        ends = sb("gla_chunk_decay", [P, U, NCH])
        with ExitStack() as inner:
            def sbi(name, shape, dt=F32):
                return inner.enter_context(nc.sbuf_tensor(name, shape, dt))

            xn = sbi("gla_in", [P, DC, T])
            low = sbi("gla_low_rank", [P, T])
            up = sbi("gla_decay_up", [P, U, P])
            z = sbi("gla_z", [P, 2 * RC, T + 2])
            cv = sbi("gla_qk", [P, RC, T])
            la = sbi("log_decay", [P, U, T])
            t1 = sbi("log_decay_tail", [P, U, T])
            e = sbi("gla_decay_exps", [P, 2, 2, T])
            (zeroed, loaded, made, biased, absed, exped, tails, chain, cumd, exd, endd, conv, silu, scaled, rev) = (
                sem(n) for n in (
                    "gla_margins_zeroed", "gla_inputs_loaded", "gla_decay_product", "gla_decay_biased", "gla_decay_abs",
                    "gla_decay_exp", "gla_decay_tail", "gla_chain", "gla_sums_ready", "gla_exps_ready",
                    "gla_ends_summed", "conv_ready", "silu_ready", "gla_scaled", "gla_v_reversed"))
            turns = 3
            with nc.Block() as block:
                @block.sync
                def _(sp):
                    sp.dma_start(xn[:, :, :], dram["mix_in"]).then_inc(loaded, 16)
                    sp.dma_start(low[:, :], dram["gla_low"]).then_inc(loaded, 16)
                    sp.dma_start(up[:, :, :], dram["gla_up"]).then_inc(loaded, 16)
                    dense.load(sp, dram["w_gla"], turns)

                @block.gpsimd
                def _(pool):
                    pool.memset(z[:, :, 0:1], 0.0).then_inc(zeroed, 1)
                    pool.memset(z[:, :, T + 1:T + 2], 0.0).then_inc(zeroed, 1)

                @block.tensor
                def _(pe):
                    pe.wait_ge(loaded, 48)
                    for u in range(U):
                        pe.matmul(ps[:, 4 + u, :], up[:, u, :], low[:, :], start=True, stop=True).then_inc(made, 1)
                    dense.multiply(pe, turns, lambda t: xn[:, t, :], [DC])

                @block.scalar
                def _(act):
                    for u in range(U):
                        act.wait_ge(made, u + 1)
                        b = par("a_b")[:, u:u + 1]
                        dst = la[:, u, :] if u < GP else la[:, u, ::-1]
                        act.activation(dst, ps[:, 4 + u, :], ACT.Identity, bias=b).then_inc(biased, 1)
                    for u in range(U):
                        act.wait_ge(biased, u + 1)
                        act.activation(t1[:, u, :], la[:, u, :], ACT.Abs).then_inc(absed, 1)
                    for u in range(U):
                        act.wait_ge(absed, u + 1)
                        act.activation(t1[:, u, :], t1[:, u, :], ACT.Exp, scale=-1.0).then_inc(exped, 1)
                    for u in range(U):
                        act.wait_ge(exped, u + 1)
                        act.activation(t1[:, u, :], t1[:, u, :], ACT.Ln, bias=1.0).then_inc(tails, 1)
                    for i in range(turns):
                        for n in range(BANK):
                            dense.full_wait(act, i, n)
                            if i < 2:
                                act.activation(z[:, i * BANK + n, 1:T + 1], dense.acc[n], ACT.Copy).then_inc(dense.free[n], 1)
                            else:
                                act.activation(gg[:, n, :], dense.acc[n], ACT.Silu).then_inc(dense.free[n], 1)
                    for m in range(2 * RC):
                        act.wait_ge(conv, 3 * (m + 1))
                        dst = cv[:, m, :] if m < RC else v[:, 0, m - RC, :]
                        act.activation(dst, dst, ACT.Silu).then_inc(silu, 1)
                    act.wait_ge(endd, 2)
                    act.activation(ends[:, :, :], ends[:, :, :], ACT.Exp, scale=1.0 / GLA_TEMP)
                    for u in range(U):
                        if u >= 2:
                            act.wait_ge(scaled, 2 * (u - 1))
                        act.wait_ge(cumd, 2 * U + u + 1)
                        for j, sc in enumerate((1.0 / GLA_TEMP, -1.0 / GLA_TEMP)):
                            act.activation(e[:, u % 2, j, :], la[:, u, :], ACT.Exp, scale=sc).then_inc(exd, 1)

                @block.vector
                def _(dve):
                    for u in range(U):
                        dve.wait_ge(tails, u + 1)
                        dve.scalar_tensor_tensor(out=t1[:, u, :], in0=la[:, u, :], scalar=0.0, in1=t1[:, u, :],
                                                 op0=ALU.min, op1=ALU.subtract).then_inc(cumd, 1)
                    for u in range(U):
                        dve.wait_ge(cumd, u + 1)
                        dve.tensor_tensor_scan(la[:, u, :], consts("chunk_start"), t1[:, u, :], 0.0,
                                               ALU.mult, ALU.add).then_inc(cumd, 1)
                    dve.wait_ge(cumd, 2 * U)
                    dve.tensor_tensor(ends[:, :, :], la[:, :, C - 1::C], la[:, :, MID::C], ALU.subtract).then_inc(endd, 1)
                    dve.wait_ge(endd, 1)
                    dve.tensor_tensor(ends[:, :, 0:NCH - 1], ends[:, :, 0:NCH - 1], la[:, :, C + MID::C],
                                      ALU.add).then_inc(endd, 1)
                    link = Count(chain)
                    for u in range(U):
                        ch = la[:, u, :].rearrange("p (c t) -> p c t", c=NCH)
                        t1c = t1[:, u, :].rearrange("p (c t) -> p c t", c=NCH)
                        link.inc(dve.tensor_tensor(t1c, ch, ch[:, :, MID:MID + 1].to_broadcast([P, NCH, C]), ALU.subtract))
                    link.wait(dve)
                    dve.wait_ge(endd, 2)
                    for u in range(U):
                        dve.tensor_scalar(la[:, u, :], t1[:, u, :], EXP_MAX * GLA_TEMP, -EXP_MAX * GLA_TEMP,
                                          ALU.min, ALU.max).then_inc(cumd, 1)
                    dve.wait_ge(zeroed, 2)
                    for m in range(2 * RC):
                        n = m % BANK
                        dve.wait_ge(dense.free[n], dense.read_value(m // BANK, n))
                        dst = cv[:, m, :] if m < RC else v[:, 0, m - RC, :]
                        dve.tensor_scalar(dst, z[:, m, 0:T], par("conv0")[:, m:m + 1], None, ALU.mult).then_inc(conv, 1)
                        for j in (1, 2):
                            dve.wait_ge(conv, 3 * m + j)
                            dve.scalar_tensor_tensor(out=dst, in0=z[:, m, j:T + j], scalar=par(f"conv{j}")[:, m:m + 1],
                                                     in1=dst, op0=ALU.mult, op1=ALU.add).then_inc(conv, 1)
                    for u in range(U):
                        time = slice(None) if u < GP else slice(None, None, -1)
                        p = u % GP
                        dve.wait_ge(exd, 2 * (u + 1))
                        dve.wait_ge(silu, RC)
                        dve.scalar_tensor_tensor(out=q[:, u, :], in0=cv[:, p, time], scalar=GLA_DK ** -0.5,
                                                 in1=e[:, u % 2, 0, :], op0=ALU.mult, op1=ALU.mult).then_inc(scaled, 1)
                        dve.tensor_tensor(kx[:, u, :], cv[:, GP + p, time], e[:, u % 2, 1, :], ALU.mult).then_inc(scaled, 1)
                    dve.wait_ge(silu, 2 * RC)
                    for n in range(RC):
                        dve.tensor_copy(v[:, 1, n, ::-1], v[:, 0, n, :])
            dense.close(turns)

        ob = sb("gla_directions", [P, 2, RC, T])
        gla_scan(nc, k, q, kx, v, ends, ob)
        gla_output(nc, k, ob, gg, out)


def gla_scan(nc, k, q, kx, v, ends, ob):
    ps, consts = k.ps, k.consts
    U, H = 2 * GP, GP
    with ExitStack() as ctx:
        def sb(name, shape, dt=F32):
            return ctx.enter_context(nc.sbuf_tensor(name, shape, dt))

        sem = k.semaphore

        bd = sb("gla_block_diagonal", [P, 2, U, P])
        vx = sb("gla_v_chunk", [P, U, P])
        pb = sb("gla_weights", [P, U, P])
        kv = sb("gla_k_v_by_token", [P, 2, 2, H, P])
        S = sb("gla_state", [P, U, P])
        zeroed = sem("gla_block_diagonals_zeroed")
        built = [sem(f"gla_vectors_built{g}") for g in range(2)]
        vbuilt = [sem(f"gla_v_chunk_copied{g}") for g in range(2)]
        chain = [sem(f"gla_state_chain{g}") for g in range(2)]
        banks = [[Bank(k, "gla", 4 * g + b, [(name, 1)]) for b, name in enumerate(("scores", "turned", "o", "S"))]
                 for g in range(2)]

        def half(g):
            return slice(g * H, g * H + H)

        with nc.Block() as block:
            @block.gpsimd
            def _(pool):
                for t in (bd, pb, S):
                    pool.memset(t[tuple([slice(None)] * len(t.shape))], 0.0).then_inc(zeroed, 1)
                pool.wait_ge(zeroed, 3)
                with pool.Fori(0, NCH) as i:
                    for g in range(2):
                        pool.wait_ge(banks[g][3].made, i + 1)
                        for src, dst in ((kx, 0), (q, 1)):
                            for hh in range(2):
                                r = slice(hh * C, hh * C + C)
                                pool.tensor_copy(bd[r, dst, half(g), r], src[r, half(g), bass.ds(i * C, C)]).then_inc(built[g], 1)

            @block.tensor
            def _(pe):
                for g in range(2):
                    for b in banks[g]:
                        pe.sem_inc(b.made, 1)
                pe.wait_ge(zeroed, 3)
                with pe.Fori(0, NCH) as i:
                    for g in range(2):
                        sc, tr = banks[g][0], banks[g][1]
                        pe.wait_ge(built[g], i * 4 + 4)
                        pe.wait_ge(vbuilt[g], i + 1)
                        sc.free(pe, i, "scores")
                        for u in range(H):
                            mm = pe.matmul(sc.ps[:, u * C:(u + 1) * C], bd[:, 0, g * H + u, :],
                                           q[:, g * H + u, bass.ds(i * C, C)], start=True, stop=True)
                        mm.then_inc(sc.made, 1)
                        tr.free(pe, i, "turned")
                        for j, src in enumerate((bd[:, 0, half(g), :], vx[:, half(g), :])):
                            for u in range(H):
                                mm = pe.transpose(tr.ps[:, (j * H + u) * P:(j * H + u + 1) * P], src[:, u, :], consts("ident"))
                        mm.then_inc(tr.made, 1)
                    for g in range(2):
                        sc, tr, o, st = banks[g]
                        sc.taken(pe, i, "scores")
                        tr.taken(pe, i, "turned")
                        o.free(pe, i, "o")
                        st.free(pe, i, "S")
                        for u in range(H):
                            w = g * H + u
                            pe.matmul(o.ps[:, u * P:(u + 1) * P], S[:, w, :], bd[:, 1, w, :], start=True, stop=False)
                            mm = pe.matmul(o.ps[:, u * P:(u + 1) * P], kv[:, g, 1, u, :], pb[:, w, :], start=False, stop=True)
                        mm.then_inc(o.made, 1)
                        for u in range(H):
                            mm = pe.matmul(st.ps[:, u * P:(u + 1) * P], kv[:, g, 0, u, :], kv[:, g, 1, u, :], start=True, stop=True)
                        mm.then_inc(st.made, 1)

            @block.scalar
            def _(act):
                with act.Fori(0, NCH) as i:
                    for g in range(2):
                        act.activation(vx[:, half(g), :].rearrange("p u (h t) -> p (u h) t", h=2),
                                       v[:, g, :, bass.ds(i * C, C)], ACT.Copy).then_inc(vbuilt[g], 1)
                    for g in range(2):
                        tr = banks[g][1]
                        tr.full(act, i, "turned")
                        act.activation(kv[:, g, :, :, :].rearrange("p a u t -> p (a u t)"), tr.ps, ACT.Copy).then_inc(tr.read, 1)
                    for g in range(2):
                        o = banks[g][2]
                        o.full(act, i, "o")
                        act.activation(ob[:, g, :, bass.ds(i * C, C)], o.ps[:, 0:2 * H * C].rearrange("p (h t) -> p h t", t=C),
                                       ACT.Copy).then_inc(o.read, 1)

            @block.vector
            def _(dve):
                for g in range(2):
                    for b in banks[g]:
                        dve.sem_inc(b.read, 1)
                dve.wait_ge(zeroed, 3)
                with dve.Fori(0, NCH) as i:
                    for g in range(2):
                        sc = banks[g][0]
                        sc.full(dve, i, "scores")
                        for hh in range(2):
                            r = slice(hh * C, hh * C + C)
                            m = consts("upper_eq")[r, None, :].to_broadcast([C, H, C])
                            ins = dve.tensor_tensor(pb[r, half(g), r], sc.ps[r, 0:H * C].rearrange("p (u t) -> p u t", u=H),
                                                    m, ALU.mult)
                        ins.then_inc(sc.read, 1)
                    for g in range(2):
                        st = banks[g][3]
                        st.full(dve, i, "S")
                        src = st.ps[:, 0:H * P].rearrange("p (u t) -> p u t", u=H)
                        dve.tensor_tensor(S[:, half(g), :], src, S[:, half(g), :], ALU.add).then_inc(chain[g], 1)
                        dve.wait_ge(chain[g], i + 1)
                        dve.tensor_tensor(S[:, half(g), :], S[:, half(g), :],
                                          ends[:, half(g), bass.ds(i, 1)].to_broadcast([P, H, P]), ALU.mult).then_inc(st.read, 1)


def gla_output(nc, k, ob, gg, out):
    ps, par, consts = k.ps, k.par, k.consts
    with ExitStack() as ctx:
        sq = ctx.enter_context(nc.sbuf_tensor("gla_squares", [P, RC, T], F32))
        sums, sqd, var, lnd, root, gained = (k.semaphore(n) for n in (
            "gla_directions_summed", "gla_squares_ready", "gla_squares_summed", "gla_log", "gla_root", "gla_normed"))
        with nc.Block() as block:
            @block.tensor
            def _(pe):
                for n in range(RC):
                    pe.wait_ge(sqd, n + 1)
                    pe.matmul(ps[:, n, :], consts("ones"), sq[:, n, :], start=True, stop=True).then_inc(var, 1)

            @block.scalar
            def _(act):
                for n in range(RC):
                    act.wait_ge(sums, n + 1)
                    act.activation(sq[:, n, :], out[:, n, :], ACT.Square).then_inc(sqd, 1)
                for n in range(RC):
                    act.wait_ge(var, n + 1)
                    act.activation(sq[:, n, :], ps[:, n, :], ACT.Ln, bias=par("eps6"), scale=1.0 / P).then_inc(lnd, 1)
                for n in range(RC):
                    act.wait_ge(lnd, n + 1)
                    act.activation(sq[:, n, :], sq[:, n, :], ACT.Exp, scale=-0.5).then_inc(root, 1)

            @block.vector
            def _(dve):
                for n in range(RC):
                    dve.tensor_tensor(out[:, n, :], ob[:, 0, n, :], ob[:, 1, n, ::-1], ALU.add).then_inc(sums, 1)
                dve.wait_ge(sqd, RC)
                for n in range(RC):
                    dve.wait_ge(root, n + 1)
                    dve.scalar_tensor_tensor(out=out[:, n, :], in0=out[:, n, :], scalar=par("gla_norm"), in1=sq[:, n, :],
                                             op0=ALU.mult, op1=ALU.mult).then_inc(gained, 1)
                for n in range(RC):
                    dve.wait_ge(gained, n + 1)
                    dve.tensor_tensor(out[:, n, :], out[:, n, :], gg[:, n, :], ALU.mult)


def feed_forward(nc, k, dram):
    dense, norm, par, h = k.dense, k.norm, k.par, k.h
    with ExitStack() as ctx:
        f = ctx.enter_context(nc.sbuf_tensor("ffn_hidden", [P, FFC, T], F32))
        xn = ctx.enter_context(nc.sbuf_tensor("ffn_in_then_out", [P, DC, T], F32))
        sg = ctx.enter_context(nc.sbuf_tensor("ffn_silu", [P, 2, T], F32))
        turns = FFC // 2
        with nc.Block() as block:
            @block.sync
            def _(sp):
                dense.load(sp, dram["w_gate_up"], turns)

            @block.scalar
            def _(act):
                norm.squares(act, h, xn)
                norm.roots(act, par("eps6"))
                with act.Fori(0, turns) as i:
                    for j in range(2):
                        dense.full_wait(act, i, 2 * j)
                        dense.free_wait(act, i, 2 * j + 1)
                        act.activation(sg[:, j, :], dense.acc[2 * j], ACT.Silu).then_inc(dense.free[2 * j], 1)

            @block.vector
            def _(dve):
                norm.scale(dve, h, xn, par("g_ffn_pre"))
                with dve.Fori(0, turns) as i:
                    for j in range(2):
                        dve.wait_ge(dense.free[2 * j], dense.read_value(i, 2 * j))
                        dense.full_wait(dve, i, 2 * j + 1)
                        dve.tensor_tensor(f[:, i * 2 + j, :], dense.acc[2 * j + 1], sg[:, j, :],
                                          ALU.mult).then_inc(dense.free[2 * j + 1], 1)

            @block.tensor
            def _(pe):
                norm.sums(pe, xn)
                norm.out_wait(pe)
                dense.multiply(pe, turns, lambda t: xn[:, t, :], [DC])
        norm.close()
        dense.close(turns)
        sq = ctx.enter_context(nc.sbuf_tensor("ffn_out_squares", [P, DC, T], F32))
        projected(nc, k, dram["w_down"], 2, lambda t: f[:, t, :], [DC, DC, FFC - 2 * DC], xn, sq, "g_ffn_post")


def layer_embedding(nc, k, dram):
    dense, norm, par, h = k.dense, k.norm, k.par, k.h
    with ExitStack() as ctx:
        pt = ctx.enter_context(nc.sbuf_tensor("embedding_in", [P, 2, T], F32))
        e = ctx.enter_context(nc.sbuf_tensor("embedding", [P, DC, T], F32))
        s = ctx.enter_context(nc.sbuf_tensor("embedding_gate_then_squares", [P, DC, T], F32))
        loaded = k.semaphore("embedding_loaded")
        gated = k.semaphore("embedding_gated")
        start = (dense.slots, dense.units)
        with nc.Block() as block:
            @block.sync
            def _(sp):
                sp.dma_start(pt[:, :, :], dram["p"]).then_inc(loaded, 16)
                dense.load(sp, dram["w_ple"], 2)
                dense.close(2)
                dense.load(sp, dram["w_ple_gate"], 2)

            @block.scalar
            def _(act):
                dense.slots, dense.units = start
                for dst, func, bias in ((e, ACT.Copy, None), (s, ACT.Sigmoid, par("b_ple"))):
                    with act.Fori(0, 2) as i:
                        for n in range(BANK):
                            dense.full_wait(act, i, n)
                            m = i * BANK + n
                            if bias is None:
                                ins = act.activation(dst[:, m, :], dense.acc[n], func)
                            else:
                                ins = act.activation(dst[:, m, :], dense.acc[n], func, bias=bias[:, bass.ds(m, 1)])
                            ins.then_inc(dense.free[n], 1)
                    dense.close(2)
                for m in range(DC):
                    act.wait_ge(gated, m + 1)
                norm.squares(act, e, s)
                norm.roots(act, par("eps6"))

            @block.vector
            def _(dve):
                dense.slots, dense.units = start[0] + 2 * BANK, start[1] + 2 * BANK
                for m in range(DC):
                    i, n = divmod(m, BANK)
                    dve.wait_ge(dense.free[n], dense.read_value(i, n))
                    dve.tensor_tensor(e[:, m, :], e[:, m, :], s[:, m, :], ALU.mult).then_inc(gated, 1)
                norm.scale(dve, e, e, par("g_ple"), add=h)

            @block.tensor
            def _(pe):
                dense.slots, dense.units = start
                pe.wait_ge(loaded, 16)
                dense.multiply(pe, 2, lambda t: pt[:, t, :], [2])
                dense.close(2)
                dense.multiply(pe, 2, lambda t: h[:, t, :], [DC])
                dense.close(2)
                norm.sums(pe, s)
        norm.close(add=True)


class Columns:

    def __init__(self, tile, where, first=0):
        self.tile, self.where, self.first = tile, where, first

    def __call__(self, name):
        at, n = self.where[name]
        return self.tile[:, at - self.first:at - self.first + n]


def build(nc, dram, param_at, const_at, out):
    k = Kernel(nc)
    k.dram = dram
    with ExitStack() as ctx:
        def sb(name, shape, dt=F32):
            return ctx.enter_context(nc.sbuf_tensor(name, shape, dt))

        k.boot = ctx.enter_context(nc.semaphore("tables_loaded"))
        k.ps = ctx.enter_context(nc.psum_tensor("psum", [P, 8, T], F32))
        k.h = sb("residual_stream", [P, DC, T])
        n_par = sum(w for _, w in param_at.values())
        n_const = sum(w for _, w in const_at.values())
        first = const_at["ident"][0]
        k.par = Columns(sb("params", [P, n_par])[:, :], param_at)
        k.consts = Columns(sb("tables", [P, n_const - first])[:, :], const_at, first)
        k.dense = Dense(ctx, nc, k.ps)
        k.norm = Norm(ctx, nc, k.ps, k.consts("ones"))
        first_mixer(nc, k, dram)
        experts(nc, k, dram)
        norm_in_place(nc, k, "g_final", "eps5")
        k.clear_semaphores()
        second_mixer(nc, k, dram)
        feed_forward(nc, k, dram)
        layer_embedding(nc, k, dram)
        stored = ctx.enter_context(nc.semaphore("output_stored"))
        with nc.Block() as block:
            @block.sync
            def _(sp):
                sp.dma_start(out, k.h[:, :, :]).then_inc(stored, 16)
                sp.wait_ge(stored, 16)


def kernel(**inputs):
    from concourse.bass_utils import run_bass_kernel_spmd
    import concourse.bacc as bacc

    a = {n: np.asarray(v) for n, v in inputs.items()}
    param_at, params = layout_params(a)
    const_at, consts = layout_constants()
    w_in = a["w_in"][0]
    qw, kw = NH * HD, NKV * HD
    o_pool = qw + 2 * kw
    o_ga = o_pool + len(PW) * P
    wk = [w_in[:, qw + v * HD:qw + (v + 1) * HD] for v in range(NKV)]
    group = a["w_pool_grp"][0].transpose(1, 0, 2).reshape(1, P, len(PW) * P)
    group = np.concatenate([group, np.zeros((1, P, D - len(PW) * P), np.float32)], 2)
    w_z = np.concatenate([w_in[:, 0:qw], w_in[:, o_ga:], w_in[:, o_pool:o_ga], wk[0], wk[0], wk[1], wk[1],
                          w_in[:, qw + kw:o_pool]], 1)
    arrays = {
        "x": np.ascontiguousarray(a["x"][0].T.reshape(DC, P, T).transpose(1, 0, 2)),
        "params": params, "consts": consts,
        "w_z": np.concatenate([tiles(w_z), group], 0),
        "w_attn_up": tiles(a["w_attn_up"][0]), "w_pool_up": tiles(a["w_pool_up"][0]), "w_o": tiles(a["w_o"][0]),
    }
    arrays["w_query"] = tiles(a["w_query"][0])
    arrays["sub_keys"] = np.ascontiguousarray(a["sub_keys"][0].reshape(2 * PH, NK, P).transpose(2, 0, 1))
    arrays["u"] = tiles(a["u_experts"][0].T)
    arrays["v"] = np.ascontiguousarray(a["v_experts"][0].reshape(NG, GI, P, DC, P).transpose(0, 3, 2, 1, 4)
                                       .reshape(NG * DC, P, GI * P))
    w2 = a["w_in_2"][0]
    rw = 13 * P + 64
    gl = rw + P
    wide = 2 * GP * P + RC * P
    w_rwkv = np.zeros((D, 16 * P), np.float32)
    w_rwkv[:, 0:rw] = w2[:, 0:rw]
    w_rwkv[:, 14 * P:15 * P] = w2[:, rw:gl]
    low = gl + wide + RC * P
    for d in range(2):
        w_rwkv[:, 15 * P + 32 * d:15 * P + 32 * d + 16] = w2[:, low + 16 * d:low + 16 * d + 16]
    arrays["w_rwkv"] = tiles(w_rwkv)
    arrays["w_gla"] = tiles(w2[:, gl:low])
    w_up = np.zeros((P, 2, RC * P), np.float32)
    gla_up = np.zeros((P, 2, GP * P), np.float32)
    for d in range(2):
        w_up[64 * d:64 * d + 64, d] = a["rwkv_w_up_2"][0, d]
        gla_up[32 * d:32 * d + 16, d] = a["gla_a_up_2"][0, d]
    a_up = np.zeros((P, RC * P), np.float32)
    a_up[0:64] = a["rwkv_a_up_2"][0]
    arrays["w_up"], arrays["a_up"] = w_up, a_up
    arrays["g_up"] = np.ascontiguousarray(a["rwkv_g_up_2"][0])
    arrays["gla_up"] = gla_up.reshape(P, 2 * GP, P)
    arrays["w_out"] = tiles(a["w_out_2"][0])
    gate, up = tiles(a["ffn_gate_2"][0]), tiles(a["ffn_up_2"][0])
    arrays["w_gate_up"] = np.stack([gate, up], 1).reshape(2 * FFC, P, D)
    down = np.zeros((DC, P, 3 * D), np.float32)
    down[:, :, 0:FFC * P] = tiles(a["ffn_down_2"][0])
    arrays["w_down"] = np.ascontiguousarray(down.reshape(DC, P, 3, D).transpose(0, 2, 1, 3).reshape(3 * DC, P, D))
    arrays["w_ple"], arrays["w_ple_gate"] = tiles(a["ple_proj_2"][0]), tiles(a["ple_gate_2"][0])
    arrays["p"] = np.ascontiguousarray(a["p_2"][0, 0].T.reshape(2, P, T).transpose(1, 0, 2))
    nc = bacc.Bacc("TRN2", target_bir_lowering=False, num_devices=1)
    dram = {n: nc.dram_tensor(f"in_{n}", v.shape, F32, kind="ExternalInput").ap() for n, v in arrays.items()}
    at, n = const_at["inv_count"]
    dram["inv_count"] = dram["consts"][:, at:at + n].rearrange("p (g t) -> p g t", g=len(PW))
    dram["table"] = nc.dram_tensor("coefficient_table", (NTB, P, NK * TB), F32, kind="Internal").ap()
    dram["mix_in"] = nc.dram_tensor("mix_in_copy", (P, DC, T), F32, kind="Internal").ap()
    dram["gla_low"] = nc.dram_tensor("gla_low_copy", (P, T), F32, kind="Internal").ap()
    dram["scan"] = nc.dram_tensor("scan_vectors", (P, 5, 2 * RC, T), F32, kind="Internal").ap()
    out = nc.dram_tensor("out", (P, DC, T), F32, kind="ExternalOutput").ap()
    build(nc, dram, param_at, const_at, out)
    r = run_bass_kernel_spmd(nc, [{f"in_{n}": v for n, v in arrays.items()}], core_ids=[0])
    return r.results[0]["out"].transpose(1, 0, 2).reshape(D, T).T.reshape(1, T, D)
```

```python
from contextlib import ExitStack

import numpy as np

import concourse.bass as bass
from concourse import mybir

F32 = mybir.dt.float32
F32R = mybir.dt.float32r
U32 = mybir.dt.uint32
ALU = mybir.AluOpType
ACT = mybir.ActivationFunctionType
AXX = mybir.AxisListType.X

P = 128
T = 512
D = 1024
DC = D // P
BANK = 4
RAW = 2
SPLIT = 2
LEAD = RAW + SPLIT

NH, NKV, HD = 16, 2, 64
QC = NH * HD // P
NB = T // P
SCALE = HD ** -0.5
NEG = -1e30
PW = (2, 4, 8, 16)
PH = 8
NK = 128
TK = 16
NE = NK * NK
TB = 64
NTB = T // TB
GI = 16
NG = NK // GI

C = 64
NCH = T // C
RC = 4
GP = 2
FFC = 2816 // P


class Count:

    def __init__(self, sem, base=0, per=0, i=0):
        self.sem, self.start, self.n, self.per, self.i = sem, base, 0, per, i

    def inc(self, ins):
        ins.then_inc(self.sem, 1)
        self.n += 1

    def at(self):
        return self.start + self.n + (self.i * self.per if self.per else 0)

    def wait(self, eng):
        eng.wait_ge(self.sem, self.at())


class Dense:

    def __init__(self, ctx, nc, ps, weights):
        def sem(name):
            return ctx.enter_context(nc.semaphore(name))

        self.raw = ctx.enter_context(nc.sbuf_tensor("weights_raw", [P, RAW, D], F32))
        self.hi = ctx.enter_context(nc.sbuf_tensor("weights_high", [P, SPLIT, D], F32R))
        self.lo = ctx.enter_context(nc.sbuf_tensor("weights_low", [P, SPLIT, D], F32R))
        self.weights, self.total = weights, weights.shape[0]
        self.acc = [ps[:, k, :] for k in range(BANK)]
        self.loaded = [sem(f"weights_loaded{k}") for k in range(RAW)]
        self.high, self.split, self.used = sem("weights_high_done"), sem("weights_split"), sem("weights_used")
        self.free = [sem(f"accumulator_read{k}") for k in range(BANK)]
        self.slots = 0
        self.units = 0

    def load_first(self, sp):
        for m in range(LEAD):
            if m >= RAW:
                sp.wait_ge(self.split, m - RAW + 1)
            sp.dma_start(self.raw[:, m % RAW, :], self.weights[m]).then_inc(self.loaded[m % RAW], 16)

    def high_first(self, act):
        for k in range(BANK):
            act.sem_inc(self.free[k], 1)
        for m in range(SPLIT):
            act.wait_ge(self.loaded[m], 16)
            act.activation(self.hi[:, m, :], self.raw[:, m, :], ACT.Copy).then_inc(self.high, 1)

    def low_first(self, pool):
        for m in range(SPLIT):
            pool.wait_ge(self.high, m + 1)
            pool.tensor_tensor(self.lo[:, m, :], self.raw[:, m, :], self.hi[:, m, :].bitcast(F32),
                               ALU.subtract).then_inc(self.split, 1)

    def cursor(self):
        return Cursor(self)

    def close(self, slots, units):
        self.slots += slots
        self.units += units


class Cursor:

    def __init__(self, dense):
        self.d, self.slots, self.units = dense, dense.slots, dense.units

    def advance(self, slots, units=0):
        self.slots += slots
        self.units += units

    def load(self, sp, i, j, per):
        m, d = self.slots + j + LEAD, self.d
        if isinstance(i, int) and i * per + m >= d.total:
            return
        sp.wait_ge(d.split, i * per + (m - RAW + 1))
        sp.dma_start(d.raw[:, m % RAW, :], d.weights[i * per + m]).then_inc(d.loaded[m % RAW], 16)

    def high(self, act, i, j, per):
        m, d = self.slots + j + SPLIT, self.d
        if isinstance(i, int) and i * per + m >= d.total:
            return
        act.wait_ge(d.loaded[m % RAW], i * (per * 16 // RAW) + (m // RAW + 1) * 16)
        act.wait_ge(d.used, i * per + (self.slots + j + 1))
        act.activation(d.hi[:, m % SPLIT, :], d.raw[:, m % RAW, :], ACT.Copy).then_inc(d.high, 1)

    def low(self, pool, i, j, per):
        m, d = self.slots + j + SPLIT, self.d
        if isinstance(i, int) and i * per + m >= d.total:
            return
        pool.wait_ge(d.high, i * per + (m + 1))
        pool.tensor_tensor(d.lo[:, m % SPLIT, :], d.raw[:, m % RAW, :], d.hi[:, m % SPLIT, :].bitcast(F32),
                           ALU.subtract).then_inc(d.split, 1)

    def run(self, eng, step, turns, per):
        if turns > 1 and self.slots + turns * per + LEAD <= self.d.total:
            with eng.Fori(0, turns) as i:
                for j in range(per):
                    step(eng, i, j, per)
        else:
            for i in range(turns):
                for j in range(per):
                    step(eng, i, j, per)
        self.advance(turns * per)

    def slot_wait(self, pe, i, j, per):
        pe.wait_ge(self.d.split, i * per + (self.slots + j + 1))

    def weights(self, j):
        at = (self.slots + j) % SPLIT
        return self.d.hi[:, at, :], self.d.lo[:, at, :]

    def free_wait(self, pe, i, k):
        pe.wait_ge(self.d.free[k], i + (self.units // BANK + 1))

    def multiply(self, pe, turns, rhs, kts, rhs_wait=None):
        per = len(kts) * BANK
        with pe.Fori(0, turns) as i:
            for k in range(BANK):
                self.free_wait(pe, i, k)
                done = 0
                for j, kt in enumerate(kts):
                    n = k * len(kts) + j
                    self.slot_wait(pe, i, n, per)
                    for t in range(kt):
                        if rhs_wait is not None and k == 0:
                            rhs_wait(done)
                        mm = product(pe, self.d.acc[k], self.weights(n), t, rhs(done), done == 0, done == sum(kts) - 1)
                        done += 1
                    mm.then_inc(self.d.used, 1)
        self.advance(turns * per, turns * BANK)

    def packed(self, pe, units, rhs, kt, rhs_wait=None):
        per = D // P // kt
        for u in range(units):
            self.free_wait(pe, u // BANK, u % BANK)
            self.slot_wait(pe, 0, u // per, units // per)
            for t in range(kt):
                if rhs_wait is not None and u == 0:
                    rhs_wait(t)
                mm = product(pe, self.d.acc[u % BANK], self.weights(u // per), (u % per) * kt + t, rhs(t),
                             t == 0, t == kt - 1)
            if u % per == per - 1:
                mm.then_inc(self.d.used, 1)
        self.advance(units // per, units)

    def full_wait(self, eng, i, k, per=1):
        eng.wait_ge(self.d.used, i * (BANK * per) + (self.slots + (k + 1) * per))

    def read_value(self, i, k):
        return i + (self.units // BANK + 2)


def product(pe, acc, w, t, x, start, stop):
    cols = slice(t * P, (t + 1) * P)
    pe.matmul(acc, w[0][:, cols], x[0], start=start, stop=False)
    pe.matmul(acc, w[0][:, cols], x[1], start=False, stop=False)
    return pe.matmul(acc, w[1][:, cols], x[0], start=False, stop=stop)


class Norm:

    def __init__(self, ctx, nc, ps, ones):
        def sem(n):
            return ctx.enter_context(nc.semaphore(n))

        self.sq, self.sum, self.rstd_ok, self.out, self.part = (sem(n) for n in (
            "norm_squares", "norm_summed", "norm_rstd", "norm_out", "norm_parts"))
        self.added = sem("norm_added")
        self.adds, self.outs, self.splits, self.sums_done = 0, 0, 0, 0
        self.rstd = ctx.enter_context(nc.sbuf_tensor("norm_rstd_tile", [P, T], F32))
        self.tmp = ctx.enter_context(nc.sbuf_tensor("norm_tmp", [P, 2, T], F32))
        self.ps, self.ones, self.n = ps[:, 4, :], ones, 0

    def squares(self, act, src):
        for k in range(DC):
            if k >= 2:
                act.wait_ge(self.sum, DC * self.n + k - 1)
            act.activation(self.tmp[:, k % 2, :], src[:, k, :], ACT.Square).then_inc(self.sq, 1)

    def sums(self, pe):
        for k in range(DC):
            pe.wait_ge(self.sq, DC * self.n + k + 1)
            pe.matmul(self.ps, self.ones, self.tmp[:, k % 2, :], start=(k == 0), stop=(k == DC - 1)).then_inc(self.sum, 1)

    def roots(self, act, eps):
        act.wait_ge(self.sum, DC * self.n + DC)
        act.activation(self.rstd[:, :], self.ps, ACT.Ln, bias=eps, scale=1.0 / D).then_inc(self.rstd_ok, 1)
        act.wait_ge(self.rstd_ok, 2 * self.n + 1)
        act.activation(self.rstd[:, :], self.rstd[:, :], ACT.Exp, scale=-0.5).then_inc(self.rstd_ok, 1)

    def ready(self, eng):
        eng.wait_ge(self.rstd_ok, 2 * self.n + 2)

    def scale(self, dve, src, dst, gain, add=None):
        self.ready(dve)
        for k in range(DC):
            dve.scalar_tensor_tensor(out=dst[:, k, :], in0=src[:, k, :], scalar=gain[:, k:k + 1],
                                     in1=self.rstd[:, :], op0=ALU.mult, op1=ALU.mult).then_inc(self.out, 1)
        if add is not None:
            for k in range(DC):
                dve.wait_ge(self.out, DC * self.outs + k + 1)
                dve.tensor_tensor(add[:, k, :], add[:, k, :], dst[:, k, :], ALU.add).then_inc(self.added, 1)

    def scale_split(self, dve, src, dst, gain):
        split_chunks(dve, lambda k, out: dve.scalar_tensor_tensor(
            out=out, in0=src[:, k, :], scalar=gain[:, k:k + 1], in1=self.rstd[:, :], op0=ALU.mult, op1=ALU.mult),
            DC, dst, self.tmp, self.part, 2 * DC * self.splits, self.out, DC * self.outs)

    def split_low(self, pool, dst):
        split_lows(pool, DC, dst, self.tmp, self.part, 2 * DC * self.splits, self.out)

    def out_wait(self, eng, k=DC - 1):
        eng.wait_ge(self.out, DC * self.outs + k + 1)

    def added_wait(self, eng, k=DC - 1):
        eng.wait_ge(self.added, DC * self.adds + k + 1)

    def close(self, add=False, split=False, again=False):
        self.n += not again
        self.adds += add
        self.splits += split
        self.outs += 1


def split_chunks(dve, make, chunks, dst, tmp, part, parts, done, dones):
    for k in range(chunks):
        if dones + k > 1:
            dve.wait_ge(done, dones + k - 1)
        make(k, dst[0][:, k, :]).then_inc(part, 1)
        make(k, tmp[:, k % 2, :]).then_inc(part, 1)


def split_lows(pool, chunks, dst, tmp, part, parts, done):
    hi, lo = dst
    for k in range(chunks):
        pool.wait_ge(part, parts + 2 * k + 2)
        pool.tensor_tensor(lo[:, k, :], tmp[:, k % 2, :], hi[:, k, :].bitcast(F32), ALU.subtract).then_inc(done, 1)


def pair(ctx, nc, name, chunks):
    return tuple(ctx.enter_context(nc.sbuf_tensor(f"{name}_{part}", [P, chunks, T], F32R)) for part in ("high", "low"))


def chunk(x, t, cols=slice(None)):
    return x[0][:, t, cols], x[1][:, t, cols]


def layout_params(a):
    def col(v):
        return np.asarray(v, np.float32).reshape(-1, P).T

    b = np.asarray(a["b_in"])[0]
    qw, kw = NH * HD, NKV * HD
    o_pool = qw + 2 * kw
    o_ga = o_pool + len(PW) * P
    bk = b[qw:qw + kw].reshape(NKV, HD)
    mu = np.zeros((15 * P,), np.float32)
    rmu = np.asarray(a["rwkv_mu_2"])[0]
    mu[0:13 * P + 64] = rmu[0:13 * P + 64]
    mu[14 * P:15 * P] = rmu[13 * P + 64:]
    conv = np.asarray(a["gla_conv_2"])[0, :, 0, :]
    parts = [
        ("g_mix", col(a["ln_mix_g"][0])), ("b_q", col(b[0:qw])),
        ("b_k", np.concatenate([np.concatenate([bk[v], bk[v]])[:, None] for v in range(NKV)], 1)),
        ("b_v", np.broadcast_to(b[qw + kw:o_pool][None, :], (P, kw))),
        ("b_pool", col(b[o_pool:o_ga])), ("b_ga", col(b[o_ga:o_ga + D])), ("b_gp", col(b[o_ga + D:])),
        ("sinks", np.broadcast_to(np.asarray(a["attn_sinks"])[0][None, :], (P, NH))),
        ("pool_scale", col(a["pool_scale"][0])), ("g_ffn", col(a["ln_ffn_g"][0])),
        ("g_final", col(a["ln_final_g"])),
        ("g_mix_pre", col(a["norm_mix_pre_2"][0])), ("g_mix_post", col(a["norm_mix_post_2"][0])),
        ("g_ffn_pre", col(a["norm_ffn_pre_2"][0])), ("g_ffn_post", col(a["norm_ffn_post_2"][0])),
        ("g_ple", col(a["norm_ple_2"][0])), ("mu", col(mu)),
        ("w0", col(np.asarray(a["rwkv_w0_2"])[0].reshape(-1))), ("a0", col(a["rwkv_a0_2"][0])),
        ("k_k", col(a["rwkv_k_k_2"][0])), ("k_a", col(a["rwkv_k_a_2"][0])),
        ("r_k", col(np.asarray(a["rwkv_r_k_2"])[0].reshape(-1))),
        ("ln_w", col(a["rwkv_ln_w_2"][0])), ("ln_b", col(a["rwkv_ln_b_2"][0])),
        ("conv0", col(conv[0])), ("conv1", col(conv[1])), ("conv2", col(conv[2])),
        ("a_b", col(np.asarray(a["gla_a_b_2"])[0].reshape(-1))), ("gla_norm", col(a["gla_norm_2"][0])),
        ("b_ple", col(a["ple_gate_b_2"][0])),
        ("eps5", np.full((P, 1), 1e-5, np.float32)), ("eps6", np.full((P, 1), 1e-6, np.float32)),
        ("eps_gn", np.full((P, 1), 64e-5, np.float32)), ("tiny", np.full((P, 1), 1e-24, np.float32)),
    ]
    where, at = {}, 0
    for name, v in parts:
        where[name] = (at, v.shape[1])
        at += v.shape[1]
    return where, np.ascontiguousarray(np.concatenate([v for _, v in parts], 1))


def tiles(w):
    w = np.asarray(w)
    k, n = w.shape
    return np.ascontiguousarray(w.reshape(k // P, P, n // P, P).transpose(2, 1, 0, 3).reshape(n // P, P, k))


def packed_tiles(w):
    t = tiles(w)
    n, _, k = t.shape
    return t.reshape(n * k // D, D // k, P, k).transpose(0, 2, 1, 3).reshape(n * k // D, P, D)


def layout_constants():
    q, k = np.arange(P)[:, None], np.arange(2 * P)[None, :]
    rel = q - (k - P)
    ok = (rel >= 0) & (rel < P)
    mask = np.where(ok, 0.0, NEG).astype(np.float32)
    mask0 = np.where(ok & (k >= P), 0.0, NEG).astype(np.float32)
    t1 = np.arange(1, T + 1, dtype=np.float32)
    inv = np.concatenate([np.broadcast_to((1.0 / np.minimum(t1, float(w)))[None, :], (P, T)) for w in PW], 1)
    ident = np.eye(P, dtype=np.float32)
    iota = np.broadcast_to(np.arange(P, dtype=np.float32)[None, :], (P, P))
    ones = np.ones((P, P), np.float32)
    half = np.kron(np.eye(2), np.ones((64, 64))).astype(np.float32)
    s, t = (np.arange(P) % C)[:, None], np.arange(C)[None, :]
    upper = (s < t).astype(np.float32)
    upper_eq = (s <= t).astype(np.float32)
    levels = []
    m = 1
    while m < C:
        levels.append(((s // (2 * m) == t // (2 * m)) & (s % (2 * m) < m) & (t % (2 * m) >= m)).astype(np.float32))
        m *= 2
    eye2 = (s == t).astype(np.float32)
    start = np.broadcast_to((np.arange(T) % C != 0).astype(np.float32)[None, :], (P, T))
    parts = [("mask", np.concatenate([mask0, mask, mask, mask], 1)), ("inv_count", inv), ("ident", ident),
             ("iota", iota), ("ones", ones), ("half", half), ("upper", upper), ("upper_eq", upper_eq),
             ("eye2", eye2), ("levels", np.concatenate(levels, 1)), ("chunk_start", start)]
    where, at = {}, 0
    for name, v in parts:
        where[name] = (at, v.shape[1])
        at += v.shape[1]
    return where, np.ascontiguousarray(np.concatenate([v for _, v in parts], 1).astype(np.float32))


class Kernel:

    def __init__(self, nc):
        self.nc, self.spent = nc, []

    def semaphore(self, name):
        self.spent.append(self.nc.alloc_semaphore(name))
        return self.spent[-1]

    def clear_semaphores(self):
        self.nc.clear_and_free_semaphores(self.spent)
        self.nc.all_engine_barrier()
        self.spent = []


def first_mixer(nc, k, dram):
    dense, norm, par, h, ps, consts = k.dense, k.norm, k.par, k.h, k.ps, k.consts
    with ExitStack() as ctx:
        def sb(name, shape, dt=F32):
            return ctx.enter_context(nc.sbuf_tensor(name, shape, dt))

        sem = k.semaphore

        q = sb("q_then_attention_out", [P, QC, T])
        ga = sb("gate_attention", [P, DC, T])
        gp = sb("gate_pool", [P, DC, T])
        zp = sb("pool_in", [P, len(PW), 16 + T])
        keys = sb("keys_by_kv_and_half", [P, NKV, 2, P + T])
        vals = sb("values_by_token", [P, NB + 1, NKV * HD])
        yp = sb("pooled", [P, len(PW), T])
        cm = sb("mask_by_block", [P, NB, 2 * P])
        gw = sb("pool_group_weights", [P, len(PW), P])
        ctx_xn = ExitStack()
        xn = pair(ctx_xn, nc, "mix_in_1", DC)

        zeroed = sem("pool_engine_zeroed")
        with nc.Block() as block:
            @block.sync
            def _(sp):
                sp.dma_start(h[:, :, :], dram["x"]).then_inc(k.boot, 16)
                sp.dma_start(par.tile, dram["params"]).then_inc(k.boot, 16)
                sp.dma_start(consts.tile, dram["consts"][:, consts.first:]).then_inc(k.boot, 16)
                sp.dma_start(cm[:, :, :], dram["consts"][:, 0:NB * 2 * P].rearrange("p (b n) -> p b n", b=NB)).then_inc(k.boot, 16)
                sp.dma_start(gw[:, :, :], dram["w_group"]).then_inc(k.boot, 16)
                w = dense.cursor()
                dense.load_first(sp)
                w.run(sp, w.load, 7, BANK)
                w.run(sp, w.load, 1, 3)

            @block.gpsimd
            def _(pool):
                w = dense.cursor()
                pool.memset(keys[:, :, :, :], 0.0).then_inc(zeroed, 1)
                pool.memset(vals[:, 0, :], 0.0).then_inc(zeroed, 1)
                pool.memset(zp[:, :, 0:16], 0.0).then_inc(zeroed, 1)
                dense.low_first(pool)
                norm.split_low(pool, xn)
                w.run(pool, w.low, 7, BANK)
                w.run(pool, w.low, 1, 3)

            @block.scalar
            def _(act):
                act.wait_ge(k.boot, 80)
                norm.squares(act, h)
                norm.roots(act, par("eps5"))
                dense.high_first(act)
                w = dense.cursor()

                def gemm_out(dst, bias, func):
                    with act.Fori(0, 2) as i:
                        for n in range(BANK):
                            w.high(act, i, n, BANK)
                            w.full_wait(act, i, n)
                            act.activation(dst(i * BANK + n), dense.acc[n], func,
                                           bias=bias[:, bass.ds(i * BANK + n, 1)]).then_inc(dense.free[n], 1)
                    w.advance(2 * BANK, 2 * BANK)

                gemm_out(lambda m: q[:, m, :], par("b_q"), ACT.Identity)
                gemm_out(lambda m: ga[:, m, :], par("b_ga"), ACT.Sigmoid)
                gemm_out(lambda m: gp[:, m, :], par("b_gp"), ACT.Sigmoid)
                act.wait_ge(zeroed, 3)
                for n in range(BANK):
                    w.high(act, 0, n, BANK)
                    w.full_wait(act, 0, n)
                    act.activation(zp[:, n, 16:], dense.acc[n], ACT.Identity,
                                   bias=par("b_pool")[:, n:n + 1]).then_inc(dense.free[n], 1)
                w.advance(BANK, BANK)
                for v in range(NKV):
                    w.high(act, 0, v, 3)
                    w.full_wait(act, 0, v)
                    act.activation(keys[0:HD, v, 0, P:], dense.acc[v][0:HD, :], ACT.Identity,
                                   bias=par("b_k")[0:HD, v:v + 1])
                    act.activation(keys[HD:P, v, 1, P:], dense.acc[v][HD:P, :], ACT.Identity,
                                   bias=par("b_k")[HD:P, v:v + 1]).then_inc(dense.free[v], 1)
                w.high(act, 0, NKV, 3)
                act.sem_inc(dense.free[3], 1)

            @block.vector
            def _(dve):
                dve.wait_ge(k.boot, 80)
                norm.ready(dve)
                norm.scale_split(dve, h, xn, par("g_mix"))
                w = dense.cursor()
                w.advance(7 * BANK)
                w.full_wait(dve, 0, 2)
                dve.tensor_tensor(vals[:, 1:, :], dense.acc[2].rearrange("p (b n) -> p b n", b=NB),
                                  par("b_v")[:, None, :].to_broadcast([P, NB, P]), ALU.add).then_inc(dense.free[2], 1)

            @block.tensor
            def _(pe):
                pe.wait_ge(k.boot, 80)
                norm.sums(pe)
                w = dense.cursor()
                w.multiply(pe, 7, lambda t: chunk(xn, t), [DC], lambda t: norm.out_wait(pe, t))
                for v in range(NKV):
                    w.free_wait(pe, 0, v)
                    w.slot_wait(pe, 0, v, 3)
                    for t in range(DC):
                        mm = product(pe, dense.acc[v], w.weights(v), t, chunk(xn, t), t == 0, t == DC - 1)
                    mm.then_inc(dense.used, 1)
                w.free_wait(pe, 0, 2)
                w.slot_wait(pe, 0, 2, 3)
                wv = w.weights(2)
                for b in range(NB):
                    cols = slice(b * P, (b + 1) * P)
                    for t in range(DC):
                        x, y = chunk(xn, t, cols), (wv[0][:, t * P:(t + 1) * P], wv[1][:, t * P:(t + 1) * P])
                        mm = product(pe, dense.acc[2][:, cols], x, 0, y, t == 0, t == DC - 1)
                mm.then_inc(dense.used, 1)
        norm.close(split=True)
        dense.close(31, 32)
        ctx_xn.close()

        attention(nc, k, q, keys, vals, cm, zp, yp)

        xs = pair(ctx, nc, "attention_out_then_merged", DC)
        yps = zp[:, :, 16:]
        ypp = pair(ctx, nc, "pool_groups_split", len(PW))
        tmp = norm.tmp
        group_done, group_out, group_split, part, split = (sem(n) for n in (
            "pool_group_product", "pool_group_scaled", "pool_group_split", "merge_parts", "merge_split"))
        G = len(PW)
        with nc.Block() as block:
            @block.sync
            def _(sp):
                w = dense.cursor()
                w.run(sp, w.load, 2, BANK)
                w.run(sp, w.load, 1, 4)
                w.run(sp, w.load, 2, BANK)

            @block.gpsimd
            def _(pool):
                w = dense.cursor()
                split_lows(pool, DC, xs, tmp, part, 0, split)
                w.run(pool, w.low, 2, BANK)
                w.run(pool, w.low, 1, 4)
                split_lows(pool, DC, xs, tmp, part, 2 * DC, split)
                w.run(pool, w.low, 2, BANK)

            @block.scalar
            def _(act):
                w = dense.cursor()
                for g in range(G):
                    act.wait_ge(group_done, g + 1)
                    for dst in (yps, ypp[0]):
                        ins = act.activation(dst[:, g, :], ps[:, 4 + g, :], ACT.Copy, scale=par("pool_scale")[:, g:g + 1])
                    ins.then_inc(group_out, 1)
                w.run(act, w.high, 2, BANK)
                w.run(act, w.high, 1, 4)
                w.run(act, w.high, 2, BANK)

            @block.vector
            def _(dve):
                w = dense.cursor()
                split_chunks(dve, lambda m, out: dve.tensor_copy(out, q[:, m, :]), DC, xs, tmp, part, 0, split, 0)
                for g in range(G):
                    dve.wait_ge(group_out, g + 1)
                    dve.tensor_tensor(ypp[1][:, g, :], yps[:, g, :], ypp[0][:, g, :].bitcast(F32),
                                      ALU.subtract).then_inc(group_split, 1)
                for m in range(DC):
                    w.full_wait(dve, m // BANK, m % BANK)
                    dve.tensor_tensor(ga[:, m, :], dense.acc[m % BANK], ga[:, m, :], ALU.mult).then_inc(dense.free[m % BANK], 1)
                w.advance(DC, DC)
                for m in range(DC):
                    dve.wait_ge(dense.used, w.slots + m // 2 + 1)
                    dve.tensor_tensor(gp[:, m, :], dense.acc[m % BANK], gp[:, m, :], ALU.mult).then_inc(dense.free[m % BANK], 1)
                w.advance(DC // 2, DC)
                for n in range(BANK):
                    dve.wait_ge(dense.free[n], w.units // BANK + 1)
                split_chunks(dve, lambda m, out: dve.tensor_tensor(out, ga[:, m, :], gp[:, m, :], ALU.add),
                             DC, xs, tmp, part, 2 * DC, split, DC)
                with dve.Fori(0, 2) as i:
                    for n in range(BANK):
                        w.full_wait(dve, i, n)
                        dve.tensor_tensor(h[:, i * BANK + n, :], dense.acc[n], h[:, i * BANK + n, :],
                                          ALU.add).then_inc(dense.free[n], 1)

            @block.tensor
            def _(pe):
                w = dense.cursor()
                for g in range(G):
                    pe.matmul(ps[:, 4 + g, :], gw[:, g, :], yp[:, g, :], start=True, stop=True).then_inc(group_done, 1)
                w.multiply(pe, 2, lambda t: chunk(xs, t), [DC], lambda t: pe.wait_ge(split, t + 1))
                w.packed(pe, DC, lambda t: chunk(ypp, t), G, lambda t: pe.wait_ge(group_split, t + 1))
                w.multiply(pe, 2, lambda t: chunk(xs, t), [DC], lambda t: pe.wait_ge(split, DC + t + 1))
        dense.close(20, 3 * DC)


def attention(nc, k, q, keys, vals, masks, zp, yp):
    ps, par, consts = k.ps, k.par, k.consts
    with ExitStack() as ctx:
        def sb(name, shape, dt=F32):
            return ctx.enter_context(nc.sbuf_tensor(name, shape, dt))

        sem = k.semaphore

        qs = sb("query_block", [P, QC, P])
        vs = sb("value_blocks", [P, 2, NKV, 2, P])
        s = sb("scores", [P, 2, 2, 2 * P])
        e = sb("probabilities", [P, 2, 2, 2 * P])
        pt = sb("probabilities_transposed", [P, 4 * P])
        mx, nm, su, es, den, rc = (sb(n, [P, NH]) for n in (
            "row_max", "negated_max", "row_sum", "sink_exp", "denominator", "reciprocal"))
        nsink = sb("negated_sinks", [P, NH])
        inv = sb("inverse_counts", [P, len(PW), T])
        w1, w2 = (sb(n, [P, len(PW), 16 + T]) for n in ("window_sums_a", "window_sums_b"))
        inv_in, zeroed, staged, scored, scaled, chain, negmax, exps, probs, turned, copied, mixed, out, pooled = (
            sem(n) for n in ("inverse_counts_loaded", "value_blocks_zeroed", "query_block_staged", "scores_product",
                             "scores_scaled", "attention_vector_chain", "negated_max_ready", "exps_done", "probs_ready",
                             "probs_transposed", "transposed_copied", "value_product", "attention_out", "pool_chain"))
        with nc.Block() as block:
            @block.sync
            def _(sp):
                sp.dma_start(inv[:, :, :], k.dram["inv_count"]).then_inc(inv_in, 16)

            @block.gpsimd
            def _(pool):
                pool.memset(vs[:, :, :, :, :], 0.0).then_inc(zeroed, 1)
                pool.memset(w1[:, :, 0:16], 0.0).then_inc(pooled, 1)
                pool.memset(w2[:, :, 0:16], 0.0).then_inc(pooled, 1)
                src = zp
                for n, dst in enumerate((w1, w2, w1, w2)):
                    lag = PW[n] // 2
                    pool.wait_ge(pooled, 2 + n)
                    pool.tensor_tensor(dst[:, n:, 16:], src[:, n:, 16:], src[:, n:, 16 - lag:16 + T - lag],
                                       ALU.add).then_inc(pooled, 1)
                    src = dst
                pool.wait_ge(pooled, 6)
                pool.wait_ge(inv_in, 16)
                for g in range(len(PW)):
                    pool.tensor_tensor(yp[:, g, :], (w1, w2)[g % 2][:, g, 16:], inv[:, g, :], ALU.mult).then_inc(pooled, 1)
                for g in range(len(PW)):
                    pool.wait_ge(pooled, 7 + g)
                    pool.tensor_tensor(yp[:, g, :], yp[:, g, :], zp[:, g, 16:], ALU.subtract).then_inc(pooled, 1)

            @block.tensor
            def _(pe):
                with pe.Fori(0, NB) as b:
                    pe.wait_ge(staged, b * 3 + 3)

                    def scores(c):
                        if c >= 2:
                            pe.wait_ge(scaled, b * QC + (c - 1))
                        for half in range(2):
                            mm = pe.matmul(ps[:, c % 2, half * 2 * P:(half + 1) * 2 * P], qs[:, c, :],
                                           keys[:, c * NKV // QC, half, bass.ds(b * P, 2 * P)], start=True, stop=True)
                        mm.then_inc(scored, 1)

                    scores(0)
                    scores(1)
                    for c in range(QC):
                        pe.wait_ge(probs, b * QC + (c + 1))
                        if c:
                            pe.wait_ge(copied, b * QC + c)
                        for half in range(2):
                            for kb in range(2):
                                n = half * 2 + kb
                                mm = pe.transpose(ps[:, 2, n * P:(n + 1) * P], e[:, c % 2, half, kb * P:(kb + 1) * P],
                                                  consts("ident"))
                        mm.then_inc(turned, 1)
                        if c + 2 < QC:
                            scores(c + 2)
                        pe.wait_ge(copied, b * QC + (c + 1))
                        if c:
                            pe.wait_ge(out, b * QC + c)
                        for half in range(2):
                            for kb in range(2):
                                n = half * 2 + kb
                                mm = pe.matmul(ps[:, 3, 0:P], vs[:, kb, c * NKV // QC, half, :], pt[:, n * P:(n + 1) * P],
                                               start=(n == 0), stop=(n == 3))
                        mm.then_inc(mixed, 1)
                    pe.wait_ge(out, b * QC + QC)

            @block.vector
            def _(dve):
                sinks = par("sinks")
                dve.tensor_scalar(nsink[:, :], sinks, -1.0, None, ALU.mult).then_inc(chain, 1)
                per = 3 * QC
                dve.wait_ge(zeroed, 1)
                with dve.Fori(0, NB) as b:
                    dve.tensor_copy(qs[:, :, :], q[:, :, bass.ds(b * P, P)]).then_inc(staged, 1)
                    for half in range(2):
                        dve.tensor_copy(vs[:, :, :, half, half * HD:(half + 1) * HD],
                                        vals[:, bass.ds(b, 2), :].rearrange("p b (v n) -> p b v n", v=NKV)).then_inc(staged, 1)
                    link = Count(chain, 1, per, b)

                    def scale_and_max(c):
                        dve.wait_ge(scored, b * QC + (c + 1))
                        dve.scalar_tensor_tensor(
                            out=s[:, c % 2, :, :], in0=ps[:, c % 2, :].rearrange("p (g n) -> p g n", g=2), scalar=SCALE,
                            in1=masks[:, bass.ds(b, 1), :].to_broadcast([P, 2, 2 * P]),
                            op0=ALU.mult, op1=ALU.add).then_inc(scaled, 1)
                        dve.wait_ge(scaled, b * QC + (c + 1))
                        link.inc(dve.tensor_reduce(mx[:, 2 * c:2 * c + 2], s[:, c % 2, :, :], AXX, ALU.max))
                        link.wait(dve)
                        dve.scalar_tensor_tensor(out=nm[:, 2 * c:2 * c + 2], in0=mx[:, 2 * c:2 * c + 2], scalar=-1.0,
                                                 in1=nsink[:, 2 * c:2 * c + 2], op0=ALU.mult,
                                                 op1=ALU.min).then_inc(negmax, 1)

                    def normalise(c):
                        dve.wait_ge(exps, b * (4 * QC) + 4 * (c + 1))
                        r = slice(2 * c, 2 * c + 2)
                        link.inc(dve.tensor_tensor(den[:, r], su[:, r], es[:, r], ALU.add))
                        link.wait(dve)
                        link.inc(dve.reciprocal(rc[:, r], den[:, r]))
                        link.wait(dve)
                        dve.tensor_tensor(e[:, c % 2, :, :], e[:, c % 2, :, :],
                                          rc[:, r, None].to_broadcast([P, 2, 2 * P]), ALU.mult).then_inc(probs, 1)

                    scale_and_max(0)
                    scale_and_max(1)
                    for c in range(QC):
                        normalise(c)
                        if c + 2 < QC:
                            scale_and_max(c + 2)
                    dve.wait_ge(mixed, b * QC + QC)

            @block.scalar
            def _(act):
                with act.Fori(0, NB) as b:
                    def exp(c):
                        act.wait_ge(negmax, b * QC + (c + 1))
                        for half in range(2):
                            j = 2 * c + half
                            act.activation(e[:, c % 2, half, :], s[:, c % 2, half, :], ACT.Exp, bias=nm[:, j:j + 1],
                                           accum_out=su[:, j:j + 1]).then_inc(exps, 1)
                            act.activation(es[:, j:j + 1], par("sinks")[:, j:j + 1], ACT.Exp,
                                           bias=nm[:, j:j + 1]).then_inc(exps, 1)

                    exp(0)
                    exp(1)
                    for c in range(QC):
                        act.wait_ge(turned, b * QC + (c + 1))
                        act.activation(pt[:, :], ps[:, 2, :], ACT.Copy).then_inc(copied, 1)
                        if c + 2 < QC:
                            exp(c + 2)
                        act.wait_ge(mixed, b * QC + (c + 1))
                        act.activation(q[:, c, bass.ds(b * P, P)], ps[:, 3, 0:P], ACT.Copy).then_inc(out, 1)


def experts(nc, k, dram):
    with ExitStack() as ctx:
        xn = pair(ctx, nc, "expert_in", DC)
        stored = [k.semaphore(f"table_stored{n}") for n in range(2)]
        with ExitStack() as ctx_sel:
            sel = ctx_sel.enter_context(nc.sbuf_tensor("choices", [P, 3, T], F32))
            choose(nc, k, dram, xn, sel)
            build_table(nc, k, dram, sel, stored)
        apply_experts(nc, k, dram, xn, stored)


def choose(nc, k, dram, xn, sel):
    ps, consts = k.ps, k.consts
    M = 2 * PH
    with ExitStack() as ctx:
        def sb(name, shape, dt=F32):
            return ctx.enter_context(nc.sbuf_tensor(name, shape, dt))

        sem = k.semaphore

        keys = sb("sub_keys", [P, M, NK])
        v = sb("key_values", [P, M, NB, TK])
        ix = sb("key_indices", [P, M, NB, TK])
        spare = sb("spare_column", [P, 1])

        def top16(dve, link, rows, values, val, idx, last=None):
            for r in range(2):
                part = slice(8 * r, 8 * r + 8)
                dve.memset(spare[:, :], 0.0)
                for m in range(rows):
                    link.inc(dve.max(val(m, part), values(m)))
                link.wait(dve)
                dve.memset(spare[:, :], 0.0)
                for m in range(rows):
                    ins = dve.max_index(idx(m, part), val(m, part), values(m))
                    if r == 1 and m == rows - 1 and last is not None:
                        ins.then_inc(last, 1)
                    else:
                        link.inc(ins)
                if r == 0:
                    link.wait(dve)
                    dve.memset(spare[:, :], 0.0)
                    for m in range(rows):
                        link.inc(dve.match_replace(values(m), val(m, part), values(m), -3.0e38))
                    link.wait(dve)

        rank_keys(nc, k, dram, xn, keys, v, ix, top16)

        cand = sb("pair_scores", [P, PH, TK * TK])
        hit = sb("rank_hits", [P, PH, TK, TK])
        fv = sb("pair_values", [P, PH, TK])
        fi = sb("pair_indices", [P, PH, TK], U32)
        rank = sb("pair_ranks", [P, 2, PH, TK], U32)
        rankf = sb("pair_ranks_f32", [P, 2, PH, TK])
        pick = sb("picks_by_token", [P, 3, PH, TK])
        ex = sb("weight_exp", [P, PH, TK])
        sm = sb("weight_sum", [P, PH])
        rs = sb("weight_reciprocal", [P, PH])
        chain, shifted, exped, picked, turned, out = (sem(n) for n in (
            "choose_chain", "weights_shifted", "weights_exp", "picks_ready", "picks_transposed", "choices_copied"))
        LINKS = 5 * PH + 10
        with nc.Block() as block:
            @block.tensor
            def _(pe):
                pe.sem_inc(turned, 3)
                with pe.Fori(0, NB) as b:
                    for j in range(3):
                        pe.wait_ge(picked, b * 3 + (j + 1))
                        mm = pe.transpose(ps[:, 4 + j, 0:P], pick[:, j, :, :].rearrange("p h k -> p (h k)"), consts("ident"))
                        mm.then_inc(turned, 1)
                    pe.wait_ge(out, b * 3 + 3)

            @block.scalar
            def _(act):
                with act.Fori(0, NB) as b:
                    act.wait_ge(shifted, b + 1)
                    act.activation(ex[:, :, :], ex[:, :, :], ACT.Exp).then_inc(exped, 1)
                    for j in range(3):
                        act.wait_ge(turned, b * 3 + (j + 4))
                        act.activation(sel[:, j, bass.ds(b * P, P)], ps[:, 4 + j, 0:P], ACT.Copy).then_inc(out, 1)

            @block.vector
            def _(dve):
                with dve.Fori(0, NB) as b:
                    link = Count(chain, 0, LINKS, b)
                    tile = bass.ds(b, 1)
                    pair = v[:, :, tile, :].rearrange("p (h s) b k -> p h s (b k)", s=2)
                    link.inc(dve.tensor_tensor(cand[:, :, :].rearrange("p h (a b) -> p h a b", a=TK),
                                               pair[:, :, 0, :, None].to_broadcast([P, PH, TK, TK]),
                                               pair[:, :, 1, None, :].to_broadcast([P, PH, TK, TK]), ALU.add))
                    link.wait(dve)
                    top16(dve, link, PH, lambda m: cand[:, m, :], lambda m, part: fv[:, m, part],
                          lambda m, part: fi[:, m, part])
                    link.wait(dve)
                    dve.wait_ge(turned, b * 3 + 3)
                    dve.tensor_tensor(ex[:, :, :], fv[:, :, :], fv[:, :, 0:1].to_broadcast([P, PH, TK]),
                                      ALU.subtract).then_inc(shifted, 1)
                    link.inc(dve.tensor_scalar(rank[:, 0, :, :], fi[:, :, :], 4, None, ALU.logical_shift_right))
                    link.inc(dve.tensor_scalar(rank[:, 1, :, :], fi[:, :, :], TK - 1, None, ALU.bitwise_and))
                    link.wait(dve)
                    link.inc(dve.tensor_copy(rankf[:, :, :, :], rank[:, :, :, :]))
                    ixp = ix[:, :, tile, :].rearrange("p (h s) b k -> p h s (b k)", s=2)
                    for j in range(2):
                        link.wait(dve)
                        link.inc(dve.tensor_tensor(hit[:, :, :, :], rankf[:, j, :, :, None].to_broadcast([P, PH, TK, TK]),
                                                   consts("iota")[:, None, None, 0:TK].to_broadcast([P, PH, TK, TK]),
                                                   ALU.is_equal))
                        link.wait(dve)
                        link.inc(dve.tensor_tensor(hit[:, :, :, :], hit[:, :, :, :],
                                                   ixp[:, :, j, None, :].to_broadcast([P, PH, TK, TK]), ALU.mult))
                        link.wait(dve)
                        dve.tensor_reduce(pick[:, j, :, :], hit[:, :, :, :], AXX, ALU.add).then_inc(picked, 1)
                        dve.wait_ge(picked, b * 3 + (j + 1))
                    dve.wait_ge(exped, b + 1)
                    link.inc(dve.tensor_reduce(sm[:, :], ex[:, :, :], AXX, ALU.add))
                    link.wait(dve)
                    link.inc(dve.reciprocal(rs[:, :], sm[:, :]))
                    link.wait(dve)
                    dve.tensor_tensor(pick[:, 2, :, :], ex[:, :, :], rs[:, :, None].to_broadcast([P, PH, TK]),
                                      ALU.mult).then_inc(picked, 1)
                    assert link.n == LINKS


def rank_keys(nc, k, dram, xn, keys, v, ix, top16):
    dense, norm, par, h, ps = k.dense, k.norm, k.par, k.h, k.ps
    M = 2 * PH
    turns = M // BANK
    with ExitStack() as ctx:
        def sb(name, shape, dt=F32):
            return ctx.enter_context(nc.sbuf_tensor(name, shape, dt))

        sem = k.semaphore

        qy = sb("expert_queries", [P, BANK, T])
        sc = sb("key_scores", [P, 2, NB, NK])
        tv, ti = sb("top_values", [P, 2, NB, TK]), sb("top_indices", [P, 2, NB, TK], U32)
        loaded, scored, copied, ranked, chain = (sem(n) for n in (
            "sub_keys_loaded", "key_scores_product", "key_scores_copied", "keys_ranked", "rank_chain"))
        LINKS = 5 * NB + 1

        def walk(eng, step):
            for n in range(BANK):
                step(0, n, n)
            with eng.Fori(1, turns) as i:
                for n in range(BANK):
                    step(i, n, i * BANK + n)

        with nc.Block() as block:
            @block.sync
            def _(sp):
                sp.dma_start(keys[:, :, :], dram["sub_keys"]).then_inc(loaded, 16)
                w = dense.cursor()
                w.run(sp, w.load, turns, BANK)

            @block.gpsimd
            def _(pool):
                w = dense.cursor()
                norm.split_low(pool, xn)
                w.run(pool, w.low, turns, BANK)

            @block.tensor
            def _(pe):
                w = dense.cursor()
                norm.sums(pe)

                def step(i, n, m):
                    w.free_wait(pe, i, n)
                    w.slot_wait(pe, i, n, BANK)
                    for t in range(DC):
                        if isinstance(i, int) and n == 0:
                            norm.out_wait(pe, t)
                        mm = product(pe, dense.acc[n], w.weights(n), t, chunk(xn, t), t == 0, t == DC - 1)
                    mm.then_inc(dense.used, 1)
                    if isinstance(m, int) and m == 0:
                        pe.wait_ge(loaded, 16)
                        return
                    before = (n - 1) % BANK
                    pe.wait_ge(dense.free[before], w.read_value(i, before) - int(n == 0))
                    pe.wait_ge(copied, m)
                    for b in range(NB):
                        ks = keys[:, m - 1, :] if isinstance(m, int) else keys[:, bass.ds(m - 1, 1), :]
                        mm = pe.matmul(ps[:, 5 + before % 2, b * NK:(b + 1) * NK], qy[:, before, b * P:(b + 1) * P],
                                       ks, start=True, stop=True)
                    mm.then_inc(scored, 1)

                walk(pe, step)
                last = BANK - 1
                pe.wait_ge(dense.free[last], w.read_value(turns - 1, last))
                pe.wait_ge(copied, M)
                for b in range(NB):
                    mm = pe.matmul(ps[:, 5 + last % 2, b * NK:(b + 1) * NK], qy[:, last, b * P:(b + 1) * P],
                                   keys[:, M - 1, :], start=True, stop=True)
                mm.then_inc(scored, 1)

            @block.scalar
            def _(act):
                w = dense.cursor()
                act.sem_inc(copied, 2)
                norm.squares(act, h)
                norm.roots(act, par("eps5"))

                def copy_scores(m, place):
                    act.wait_ge(scored, m)
                    act.wait_ge(ranked, m)
                    act.activation(sc[:, place, :, :].rearrange("p b n -> p (b n)"), ps[:, 5 + place, :],
                                   ACT.Copy).then_inc(copied, 1)

                def step(i, n, m):
                    w.high(act, i, n, BANK)
                    w.full_wait(act, i, n)
                    act.activation(qy[:, n, :], dense.acc[n], ACT.Copy).then_inc(dense.free[n], 1)
                    if not (isinstance(m, int) and m == 0):
                        copy_scores(m, (n - 1) % 2)

                walk(act, step)
                copy_scores(M, (M - 1) % 2)

            @block.vector
            def _(dve):
                dve.sem_inc(ranked, 2)
                norm.ready(dve)
                norm.scale_split(dve, h, xn, par("g_ffn"))
                with dve.Fori(0, M // 2) as mm:
                    for place in range(2):
                        m = mm * 2 + place
                        link = Count(chain, place * LINKS, 2 * LINKS, mm)
                        dve.wait_ge(copied, m + 3)
                        top16(dve, link, NB, lambda b: sc[:, place, b, :],
                              lambda b, part: tv[:, place, b, part], lambda b, part: ti[:, place, b, part], ranked)
                        dve.wait_ge(ranked, m + 3)
                        at = bass.ds(m, 1)
                        link.inc(dve.tensor_copy(v[:, at, :, :], tv[:, place:place + 1, :, :]))
                        link.inc(dve.tensor_copy(ix[:, at, :, :], ti[:, place:place + 1, :, :]))
                        assert link.n == LINKS
        norm.close(split=True)
        dense.close(M, M)


def build_table(nc, k, dram, sel, stored):
    ps, consts = k.ps, k.consts
    QT = 4
    NQ = TB // QT
    RING = 4
    with ExitStack() as ctx:
        def sb(name, shape, dt=F32):
            return ctx.enter_context(nc.sbuf_tensor(name, shape, dt))

        sem = k.semaphore

        onehot = sb("first_and_second_key_onehot", [P, RING, 2, QT, NK])
        second = sb("second_key_weighted", [P, RING, QT, NK])
        stage = sb("table_stage", [P, 2, NK, TB])
        made, weighted, product, read = (sem(n) for n in (
            "onehots_made", "onehots_weighted", "table_product", "table_bank_read"))
        iota = consts("iota")

        def walk(eng, step, after=lambda tb2, par: None, before=lambda tb2, par: None):
            with eng.Fori(0, NTB // 2) as tb2:
                for par in range(2):
                    before(tb2, par)
                    with eng.Fori(0, NQ // RING) as j:
                        for u in range(RING):
                            step(par, tb2 * (2 * NQ) + par * NQ + j * RING + u, u,
                                 tb2 * (2 * TB) + par * TB + j * (RING * QT) + u * QT, j * (RING * QT) + u * QT)
                    after(tb2, par)

        with nc.Block() as block:
            @block.vector
            def _(dve):
                def step(par, n, u, t, tl):
                    dve.wait_ge(product, n + 1)
                    dve.tensor_tensor(onehot[:, u, :, :, :], iota[:, None, None, :].to_broadcast([P, 2, QT, NK]),
                                      sel[:, 0:2, bass.ds(t, QT)][:, :, :, None].to_broadcast([P, 2, QT, NK]),
                                      ALU.is_equal).then_inc(made, 1)
                walk(dve, step)

            @block.gpsimd
            def _(pool):
                def step(par, n, u, t, tl):
                    pool.wait_ge(product, n + 1)
                    pool.wait_ge(made, n + 1)
                    pool.tensor_tensor(second[:, u, :, :], onehot[:, u, 1, :, :],
                                       sel[:, 2, bass.ds(t, QT)][:, :, None].to_broadcast([P, QT, NK]),
                                       ALU.mult).then_inc(weighted, 1)
                walk(pool, step)

            @block.tensor
            def _(pe):
                pe.sem_inc(product, RING)

                def step(par, n, u, t, tl):
                    pe.wait_ge(weighted, n + 1)
                    pe.wait_ge(read, n + 1)
                    for q in range(QT):
                        mm = pe.matmul(ps[:, u, q * NK:(q + 1) * NK], second[:, u, q, :], onehot[:, u, 0, q, :],
                                       start=True, stop=True)
                    mm.then_inc(product, 1)
                walk(pe, step)

            @block.scalar
            def _(act):
                act.sem_inc(read, RING)
                act.sem_inc(stored[0], 16)
                act.sem_inc(stored[1], 16)

                def step(par, n, u, t, tl):
                    act.wait_ge(product, n + (RING + 1))
                    act.activation(stage[:, par, :, bass.ds(tl, QT)], ps[:, u, :].rearrange("p (t i) -> p i t", t=QT),
                                   ACT.Copy).then_inc(read, 1)
                walk(act, step, before=lambda tb2, par: act.wait_ge(stored[par], tb2 * 16 + 16))

            @block.sync
            def _(sp):
                with sp.Fori(0, NTB // 2) as tb2:
                    for par in range(2):
                        sp.wait_ge(read, tb2 * (2 * NQ) + ((par + 1) * NQ + RING))
                        sp.dma_start(dram["table"][tb2 * 2 + par], stage[:, par, :, :]).then_inc(stored[par], 16)


def apply_experts(nc, k, dram, xn, stored):
    ps, h, dense = k.ps, k.h, k.dense
    SL = 2 * GI
    HALF = D // P
    NEXT = GI + 2
    with ExitStack() as ctx:
        def sb(name, shape, dt=F32):
            return ctx.enter_context(nc.sbuf_tensor(name, shape, dt))

        sem = k.semaphore

        g = sb("table_group", [P, NTB, GI, TB])
        co = pair(ctx, nc, "coefficients", GI)
        gl = sb("gelu_then_coefficient", [P, 2, T])
        g_in = sem("table_group_loaded")
        gelu, part, coef, added = (sem(n) for n in (
            "gelu_done", "coefficient_parts", "coefficients_ready", "v_product_added"))
        table = dram["table"].rearrange("b p (g n) -> g p b n", g=NG)

        with nc.Block() as block:
            @block.sync
            def _(sp):
                w = dense.cursor()
                for par in range(2):
                    sp.wait_ge(stored[par], 16 * (NTB // 2) + 16)
                sp.dma_start(g[:, :, :, :], table[0]).then_inc(g_in, 16)

                def group(gg, last):
                    for j in range(SL):
                        w.load(sp, gg, j, SL)
                        if j == NEXT and not last:
                            sp.wait_ge(coef, gg * GI + (GI + 2))
                            sp.dma_start(g[:, :, :, :], table[gg + 1]).then_inc(g_in, 16)
                with sp.Fori(0, NG - 1) as gg:
                    group(gg, False)
                group(NG - 1, True)

            @block.gpsimd
            def _(pool):
                w = dense.cursor()
                w.run(pool, w.low, NG, SL)

            @block.tensor
            def _(pe):
                w = dense.cursor()
                with pe.Fori(0, NG) as gg:
                    for n in range(GI):
                        pe.wait_ge(gelu, gg * GI + (n + 1))
                        w.slot_wait(pe, gg, n, SL)
                        for t in range(DC):
                            mm = product(pe, ps[:, n % BANK, :], w.weights(n), t, chunk(xn, t), t == 0, t == DC - 1)
                        mm.then_inc(dense.used, 1)
                    for c in range(DC):
                        pe.wait_ge(added, gg * DC + (c + 1))
                        for half in range(2):
                            j = GI + 2 * c + half
                            w.slot_wait(pe, gg, j, SL)
                            for t in range(HALF):
                                n = half * HALF + t
                                if c == 0:
                                    pe.wait_ge(coef, gg * GI + (n + 3))
                                mm = product(pe, ps[:, 4 + c % 2, :], w.weights(j), t, chunk(co, n), n == 0, n == GI - 1)
                            mm.then_inc(dense.used, 1)

            @block.scalar
            def _(act):
                act.sem_inc(gelu, BANK)
                w = dense.cursor()
                with act.Fori(0, NG) as gg:
                    for j in range(SL):
                        w.high(act, gg, j, SL)
                        if j < GI:
                            act.wait_ge(coef, gg * GI + (j + 1))
                            act.activation(gl[:, j % 2, :], ps[:, j % BANK, :], ACT.Gelu).then_inc(gelu, 1)

            @block.vector
            def _(dve):
                dve.sem_inc(coef, 2)
                dve.sem_inc(added, 2)
                w = dense.cursor()
                with dve.Fori(0, NG) as gg:
                    dve.wait_ge(g_in, gg * 16 + 16)
                    for n in range(GI):
                        def by_block(x):
                            return x.rearrange("p (b t) -> p b t", b=NTB)
                        dve.wait_ge(gelu, gg * GI + (n + 1 + BANK))
                        tile = gl[:, n % 2, :]
                        dve.tensor_tensor(by_block(co[0][:, n, :]), by_block(tile), g[:, :, n, :], ALU.mult).then_inc(part, 1)
                        dve.tensor_tensor(by_block(tile), by_block(tile), g[:, :, n, :], ALU.mult).then_inc(part, 1)
                        dve.wait_ge(part, gg * (2 * GI) + (2 * n + 2))
                        dve.tensor_tensor(co[1][:, n, :], tile, co[0][:, n, :].bitcast(F32), ALU.subtract).then_inc(coef, 1)
                    for c in range(DC):
                        dve.wait_ge(dense.used, gg * SL + (w.slots + GI + 2 * c + 2))
                        dve.tensor_tensor(h[:, c, :], h[:, c, :], ps[:, 4 + c % 2, :], ALU.add).then_inc(added, 1)
        dense.close(NG * SL, 0)


def norm_in_place(nc, k, gain, eps):
    norm, h = k.norm, k.h
    with nc.Block() as block:
        @block.scalar
        def _(act):
            norm.squares(act, h)
            norm.roots(act, k.par(eps))

        @block.vector
        def _(dve):
            norm.scale(dve, h, h, k.par(gain))

        @block.tensor
        def _(pe):
            norm.sums(pe)
    norm.close()


def second_mixer(nc, k, dram):
    with ExitStack() as ctx:
        gate = ctx.enter_context(nc.sbuf_tensor("rwkv_gate_then_out", [P, RC, T], F32))
        with ExitStack() as inner:
            bonus = inner.enter_context(nc.sbuf_tensor("rwkv_bonus", [P, RC, T], F32))
            ends = inner.enter_context(nc.sbuf_tensor("rwkv_chunk_decay", [P, 2 * RC, NCH], F32))
            rwkv_inputs(nc, k, dram, gate, bonus, ends)
            ys = inner.enter_context(nc.sbuf_tensor("rwkv_scan_out", [P, 2 * RC, T], F32))
            rwkv_scan(nc, k, dram, ends, ys)
            rwkv_output(nc, k, gate, bonus, ys)
        out = ctx.enter_context(nc.sbuf_tensor("gla_out", [P, RC, T], F32))
        gla(nc, k, dram, out)
        with ExitStack() as inner:
            u = inner.enter_context(nc.sbuf_tensor("mixer_projected", [P, DC, T], F32))
            xs = pair(inner, nc, "mixed", DC)
            part, split = k.semaphore("mixed_parts"), k.semaphore("mixed_split")

            def prepare(dve):
                split_chunks(dve, lambda t, dst: dve.tensor_copy(dst, (gate if t < RC else out)[:, t % RC, :]),
                             DC, xs, k.norm.tmp, part, 0, split, 0)

            def prepare_low(pool):
                split_lows(pool, DC, xs, k.norm.tmp, part, 0, split)
            projected(nc, k, 2, lambda t: chunk(xs, t), [DC], u, "g_mix_post", prepare, prepare_low,
                      lambda pe, t: pe.wait_ge(split, t + 1))


def projected(nc, k, turns, rhs, kts, u, gain, prepare=None, prepare_low=None, rhs_wait=None):
    dense, norm, par, h = k.dense, k.norm, k.par, k.h
    per = len(kts)
    with nc.Block() as block:
        @block.sync
        def _(sp):
            w = dense.cursor()
            w.run(sp, w.load, turns, BANK * per)

        @block.gpsimd
        def _(pool):
            w = dense.cursor()
            if prepare_low is not None:
                prepare_low(pool)
            w.run(pool, w.low, turns, BANK * per)

        @block.scalar
        def _(act):
            w = dense.cursor()
            with act.Fori(0, turns) as i:
                for n in range(BANK):
                    for j in range(per):
                        w.high(act, i, n * per + j, BANK * per)
                    w.full_wait(act, i, n, per)
                    act.activation(u[:, i * BANK + n, :], dense.acc[n], ACT.Copy).then_inc(dense.free[n], 1)
            for n in range(BANK):
                act.wait_ge(dense.free[n], w.read_value(turns - 1, n))
            norm.squares(act, u)
            norm.roots(act, par("eps6"))

        @block.vector
        def _(dve):
            if prepare is not None:
                prepare(dve)
            norm.scale(dve, u, u, par(gain), add=h)

        @block.tensor
        def _(pe):
            w = dense.cursor()
            w.multiply(pe, turns, rhs, kts, None if rhs_wait is None else lambda t: rhs_wait(pe, t))
            norm.sums(pe)
    norm.close(add=True)
    dense.close(turns * BANK * per, turns * BANK)


DECAY = -float(np.exp(-0.5))


def rwkv_inputs(nc, k, dram, gate, bonus, ends):
    dense, norm, par, h, ps, consts = k.dense, k.norm, k.par, k.h, k.ps, k.consts
    with ExitStack() as ctx:
        def sb(name, shape, dt=F32):
            return ctx.enter_context(nc.sbuf_tensor(name, shape, dt))

        sem = k.semaphore

        NZ = 15
        z = sb("rwkv_z", [P, NZ, T + 2])
        with ExitStack() as inner:
            xn = pair(inner, nc, "mix_in_2", DC)
            low = inner.enter_context(nc.sbuf_tensor("gla_low_rank_in", [P, T], F32))
            tmp = inner.enter_context(nc.sbuf_tensor("shift_sum", [P, BANK, T], F32))
            zeroed, shifted, saved = (sem(n) for n in ("z_margins_zeroed", "shift_chain", "gla_low_saved"))
            turns = 4
            with nc.Block() as block:
                @block.sync
                def _(sp):
                    w = dense.cursor()
                    w.run(sp, w.load, turns, BANK)
                    w = dense.cursor()
                    sp.wait_ge(dense.free[BANK - 1], w.read_value(turns - 1, BANK - 1))
                    sp.dma_start(dram["gla_low"], low[:, :]).then_inc(saved, 16)
                    sp.wait_ge(saved, 16)

                @block.gpsimd
                def _(pool):
                    pool.memset(z[:, :, 0:1], 0.0).then_inc(zeroed, 1)
                    pool.memset(z[:, :, T + 1:T + 2], 0.0).then_inc(zeroed, 1)
                    w = dense.cursor()
                    norm.split_low(pool, xn)
                    w.run(pool, w.low, turns, BANK)

                @block.scalar
                def _(act):
                    w = dense.cursor()
                    norm.squares(act, h)
                    norm.roots(act, par("eps6"))
                    for i in range(turns):
                        for n in range(BANK):
                            m = i * BANK + n
                            w.high(act, i, n, BANK)
                            w.full_wait(act, i, n)
                            act.activation(z[:, m, 1:T + 1] if m < NZ else low[:, :], dense.acc[n],
                                           ACT.Copy).then_inc(dense.free[n], 1)

                @block.vector
                def _(dve):
                    w = dense.cursor()
                    norm.ready(dve)
                    norm.scale_split(dve, h, xn, par("g_mix_pre"))
                    dve.wait_ge(zeroed, 2)
                    link = Count(shifted)
                    for i in range(turns):
                        m0, m1 = i * BANK, min((i + 1) * BANK, NZ)
                        for n in range(m1 - m0):
                            dve.wait_ge(dense.free[n], w.read_value(i, n))
                        s = tmp[:, 0:m1 - m0, :]
                        link.inc(dve.tensor_tensor(s, z[:, m0:m1, 0:T], z[:, m0:m1, 2:T + 2], ALU.add))
                        link.wait(dve)
                        link.inc(dve.scalar_tensor_tensor(out=s, in0=s, scalar=0.5, in1=z[:, m0:m1, 1:T + 1],
                                                          op0=ALU.mult, op1=ALU.subtract))
                        link.wait(dve)
                        for m in range(m0, m1):
                            link.inc(dve.scalar_tensor_tensor(out=z[:, m, 1:T + 1], in0=tmp[:, m - m0, :],
                                                              scalar=par("mu")[:, m:m + 1], in1=z[:, m, 1:T + 1],
                                                              op0=ALU.mult, op1=ALU.add))
                        link.wait(dve)

                @block.tensor
                def _(pe):
                    norm.sums(pe)
                    w = dense.cursor()
                    w.multiply(pe, turns, lambda t: chunk(xn, t), [DC], lambda t: norm.out_wait(pe, t))
            norm.close(split=True)
            dense.close(turns * BANK, turns * BANK)

        def zc(m):
            return z[:, m, 1:T + 1]

        R, K, V, W, A, G = 0, RC, 2 * RC, 3 * RC, 3 * RC + 1, 3 * RC + 2
        w_up, a_up, g_up = sb("decay_up", [P, 2, RC * P]), sb("a_up", [P, RC * P]), sb("gate_up", [P, RC * P])
        lw = sb("decay_sigmoid", [P, 2 * RC, T])
        cum = sb("decay_sum", [P, 2, T])
        aa = sb("a_then_b", [P, RC, T])
        kk = sb("kk", [P, RC, T])
        sq = sb("kk_squares_then_rkr", [P, RC, T])
        e = sb("decay_exps", [P, 2, 3, T])
        st = sb("scan_stage", [P, 2, 4, T])
        vr = sb("v_reversed", [P, RC, T])
        loaded, low_ready, made, lwd, ad, gd, raw, sqd, clamped, logs, root, rkr, chain, cumd, exd, unit = (sem(n) for n in (
            "rwkv_small_weights_loaded", "low_rank_activated", "low_rank_product", "decay_ready", "a_ready",
            "gate_ready", "kk_unscaled", "kk_squares_ready", "kk_squares_clamped", "kk_logs", "kk_roots", "r_k_products",
            "rwkv_inputs_chain", "decay_sums_ready", "decay_exps_ready",
            "unit_staged"))
        stored = [sem(f"unit_stored{n}") for n in range(2)]
        tmp = sb("rwkv_inputs_tmp", [P, RC, T])
        vst = sem("reversed_v_stored")
        with nc.Block() as block:
            @block.sync
            def _(sp):
                for dst, name in ((w_up[:, :, :], "w_up"), (a_up[:, :], "a_up"), (g_up[:, :], "g_up")):
                    sp.dma_start(dst, dram[name]).then_inc(loaded, 16)
                for c in range(RC):
                    sp.dma_start(dram["scan"][:, 4, c, :], zc(V + c)).then_inc(vst, 16)
                for u in range(2 * RC):
                    sp.wait_ge(unit, u + 1)
                    sp.dma_start(dram["scan"][:, 0:4, u, :], st[:, u % 2, :, :]).then_inc(stored[u % 2], 16)
                sp.dma_start(dram["scan"][:, 4, RC:2 * RC, :], vr[:, :, :]).then_inc(vst, 16)
                for n in range(2):
                    sp.wait_ge(stored[n], 16 * RC)
                sp.wait_ge(vst, 16 * (RC + 1))

            @block.tensor
            def _(pe):
                pe.wait_ge(loaded, 48)
                pe.wait_ge(low_ready, 2)
                for n in range(2 * RC):
                    pe.matmul(ps[:, n, :], w_up[:, n // RC, (n % RC) * P:(n % RC + 1) * P], zc(W),
                              start=True, stop=True).then_inc(made, 1)
                for n in range(RC):
                    pe.wait_ge(lwd, n + 1)
                    pe.matmul(ps[:, n, :], a_up[:, n * P:(n + 1) * P], zc(A), start=True, stop=True).then_inc(made, 1)
                for n in range(RC):
                    pe.wait_ge(lwd, RC + n + 1)
                    pe.matmul(ps[:, 4 + n, :], g_up[:, n * P:(n + 1) * P], zc(G), start=True, stop=True).then_inc(made, 1)
                for n in range(RC):
                    pe.wait_ge(ad, n + 1)
                    pe.wait_ge(sqd, n + 1)
                    pe.matmul(ps[:, n, :], consts("half"), sq[:, n, :], start=True, stop=True).then_inc(made, 1)
                for n in range(RC):
                    pe.wait_ge(gd, n + 1)
                    pe.wait_ge(rkr, n + 1)
                    pe.matmul(ps[:, 4 + n, :], consts("half"), tmp[:, n, :], start=True, stop=True).then_inc(made, 1)

            @block.scalar
            def _(act):
                act.activation(zc(W), zc(W), ACT.Tanh).then_inc(low_ready, 1)
                act.activation(zc(G), zc(G), ACT.Sigmoid).then_inc(low_ready, 1)
                for n in range(2 * RC):
                    act.wait_ge(made, n + 1)
                    dst = lw[:, n, :] if n < RC else lw[:, n, ::-1]
                    act.activation(dst, ps[:, n, :], ACT.Sigmoid, bias=par("w0")[:, n:n + 1]).then_inc(lwd, 1)
                for n in range(RC):
                    act.wait_ge(made, 2 * RC + n + 1)
                    act.activation(aa[:, n, :], ps[:, n, :], ACT.Sigmoid, bias=par("a0")[:, n:n + 1]).then_inc(ad, 1)
                for n in range(RC):
                    act.wait_ge(made, 3 * RC + n + 1)
                    act.activation(gate[:, n, :], ps[:, 4 + n, :], ACT.Copy).then_inc(gd, 1)
                act.wait_ge(raw, RC)
                for n in range(RC):
                    act.activation(sq[:, n, :], kk[:, n, :], ACT.Square).then_inc(sqd, 1)
                for n in range(RC):
                    act.wait_ge(clamped, n + 1)
                    act.activation(sq[:, n, :], sq[:, n, :], ACT.Ln).then_inc(logs, 1)
                for n in range(RC):
                    act.wait_ge(logs, n + 1)
                    act.activation(sq[:, n, :], sq[:, n, :], ACT.Exp, scale=-0.5).then_inc(root, 1)
                for u in range(2 * RC):
                    if u >= 2:
                        act.wait_ge(unit, u - 1)
                    for j, sc in enumerate((DECAY, -DECAY, DECAY)):
                        if j == 0:
                            act.wait_ge(cumd, 2 * u + 1)
                        if j == 2:
                            act.wait_ge(cumd, 2 * u + 2)
                        src = cum[:, u % 2, :] if j < 2 else lw[:, u, :]
                        act.activation(e[:, u % 2, j, :], src, ACT.Exp, scale=sc).then_inc(exd, 1)

            @block.vector
            def _(dve):
                link = Count(chain)
                for n in range(RC):
                    dve.tensor_scalar(kk[:, n, :], zc(K + n), par("k_k")[:, n:n + 1], None, ALU.mult).then_inc(raw, 1)
                for n in range(RC):
                    link.inc(dve.tensor_copy(vr[:, n, ::-1], zc(V + n)))
                dve.wait_ge(ad, RC)
                for n in range(RC):
                    link.inc(dve.tensor_scalar(tmp[:, n, :], aa[:, n, :], -1.0, par("k_a")[:, n:n + 1], ALU.add, ALU.mult))
                link.wait(dve)
                for n in range(RC):
                    link.inc(dve.scalar_tensor_tensor(out=zc(K + n), in0=tmp[:, n, :], scalar=1.0, in1=zc(K + n),
                                                      op0=ALU.add, op1=ALU.mult))
                for n in range(RC):
                    dve.wait_ge(made, 4 * RC + n + 1)
                    dve.tensor_scalar(sq[:, n, :], ps[:, n, :], 1e-24, None, ALU.max).then_inc(clamped, 1)
                link.wait(dve)
                for n in range(RC):
                    dve.scalar_tensor_tensor(out=tmp[:, n, :], in0=zc(R + n), scalar=par("r_k")[:, n:n + 1], in1=zc(K + n),
                                             op0=ALU.mult, op1=ALU.mult).then_inc(rkr, 1)
                dve.wait_ge(root, RC)
                for n in range(RC):
                    link.inc(dve.tensor_tensor(kk[:, n, :], kk[:, n, :], sq[:, n, :], ALU.mult))
                link.wait(dve)
                for n in range(RC):
                    link.inc(dve.tensor_tensor(aa[:, n, :], aa[:, n, :], kk[:, n, :], ALU.mult))
                for n in range(RC):
                    dve.wait_ge(made, 5 * RC + n + 1)
                    link.inc(dve.tensor_tensor(bonus[:, n, :], ps[:, 4 + n, :], zc(V + n), ALU.mult))
                link.wait(dve)
                for u in range(2 * RC):
                    c = u % RC
                    time = slice(None) if u < RC else slice(None, None, -1)
                    if u >= 2:
                        dve.wait_ge(exd, 3 * (u - 1))
                    dve.wait_ge(lwd, u + 1)
                    dve.tensor_tensor_scan(cum[:, u % 2, :], consts("chunk_start"), lw[:, u, :], 0.0,
                                           ALU.mult, ALU.add).then_inc(cumd, 1)
                    dve.wait_ge(cumd, 2 * u + 1)
                    dve.tensor_tensor(lw[:, u, :], cum[:, u % 2, :], lw[:, u, :], ALU.subtract).then_inc(cumd, 1)
                    dve.wait_ge(exd, 3 * (u + 1))
                    if u >= 2:
                        dve.wait_ge(stored[u % 2], 16 * (u // 2))
                    ev = [e[:, u % 2, j, :] for j in range(3)]
                    dve.scalar_tensor_tensor(out=st[:, u % 2, 0, :], in0=kk[:, c, time], scalar=-1.0, in1=ev[2],
                                             op0=ALU.mult, op1=ALU.mult)
                    dve.tensor_tensor(st[:, u % 2, 1, :], zc(R + c)[:, time], ev[0], ALU.mult)
                    dve.tensor_tensor(st[:, u % 2, 2, :], aa[:, c, time], ev[1], ALU.mult)
                    dve.tensor_copy(ends[:, u, :], ev[0][:, C - 1::C])
                    dve.tensor_tensor(st[:, u % 2, 3, :], zc(K + c)[:, time], ev[1], ALU.mult).then_inc(unit, 1)


class Bank:

    def __init__(self, k, scan, number, uses):
        self.ps = k.ps[:, number, :]
        self.made = k.semaphore(f"{scan}_bank{number}_made")
        self.read = k.semaphore(f"{scan}_bank{number}_read")
        self.uses = uses
        self.reads = sum(r for _, r in uses)

    def place(self, name):
        n = [u for u, _ in self.uses].index(name)
        return n, sum(r for _, r in self.uses[:n]), self.uses[n][1]

    def free(self, pe, i, name):
        pe.wait_ge(self.read, i * self.reads + (self.place(name)[1] + 1))

    def full(self, eng, i, name):
        eng.wait_ge(self.made, i * len(self.uses) + (self.place(name)[0] + 2))

    def taken(self, eng, i, name):
        _, before, own = self.place(name)
        eng.wait_ge(self.read, i * self.reads + (before + own + 1))


def rwkv_scan(nc, k, dram, ends, ys):
    consts = k.consts
    U, H = 2 * RC, RC
    LV = 6
    with ExitStack() as ctx:
        def sb(name, shape, dt=F32):
            return ctx.enter_context(nc.sbuf_tensor(name, shape, dt))

        sem = k.semaphore

        cb = sb("chunk_vectors", [P, 2, 5, U, C])
        bd = sb("block_diagonal_vectors", [P, 2, 4, U, P])
        bt, kt, vt = sb("b_by_token", [P, U, P]), sb("k_by_token", [P, U, P]), sb("v_by_token", [P, U, P])
        vc = sb("v_compact", [P, U, C])
        L = sb("L_transposed", [P, U, C])
        mb, mk = sb("b_r_products", [P, U, C]), sb("k_r_products", [P, U, C])
        lk = sb("k_a_products", [P, U, P])
        bl = sb("L_level", [P, 2, U, P])
        wc, wb = sb("W_compact", [P, U, C]), sb("W_block_diagonal", [P, U, P])
        X, XT = sb("X_compact", [P, U, C]), sb("X_transposed", [P, U, P])
        rr, sa, sab = sb("right_side", [P, U, C]), sb("sa_compact", [P, U, C]), sb("sa_block_diagonal", [P, U, P])
        S, Sb = sb("state", [P, U, C]), sb("state_block_diagonal", [P, U, P])
        zeroed = sem("block_diagonals_zeroed")
        cb_in = [sem(f"chunk_vectors_loaded{n}") for n in range(2)]
        built = [sem(f"vectors_built{g}") for g in range(2)]
        lev = [sem(f"L_levels_built{g}") for g in range(2)]
        sbuilt = [sem(f"state_built{g}") for g in range(2)]
        ready = [sem(f"X_transposed_started{g}") for g in range(2)]
        chain = [sem(f"state_chain{g}") for g in range(2)]
        KINDS = ((2, 0), (3, 1), (0, 2), (4, 3))

        def uses(g):
            lv = range(LV)
            return [
                Bank(k, "rwkv", 4 * g, [("scores_b", 1)] + [(f"W{l}", 1) for l in lv] + [("sa", 1)]),
                Bank(k, "rwkv", 4 * g + 1, [("scores_k", 1)] + [(f"dX{l}", 1) for l in lv[1:-1]] + [("y", 1)]),
                Bank(k, "rwkv", 4 * g + 2, [("b_t", 1), ("v_t", 1)] + [(f"dXT{l}", 1) for l in lv[1:]] + [("S", 1)]),
                Bank(k, "rwkv", 4 * g + 3, [("k_t", 1), ("rhs", 1)])]

        banks = [uses(g) for g in range(2)]

        def half(g):
            return slice(g * H, g * H + H)

        with nc.Block() as block:
            @block.sync
            def _(sp):
                for n in range(2):
                    sp.dma_start(cb[:, n, :, :, :].rearrange("p a u t -> p (a u) t"),
                                 dram["scan"].rearrange("p a u t -> p (a u) t")[:, :, n * C:(n + 1) * C]).then_inc(cb_in[n], 16)
                with sp.Fori(0, NCH // 2 - 1) as ii:
                    for n in range(2):
                        for g in range(2):
                            banks[g][1].full(sp, ii * 2 + n, "y")
                        sp.dma_start(cb[:, n, :, :, :].rearrange("p a u t -> p (a u) t"),
                                     dram["scan"].rearrange("p a u t -> p (a u) t")[:, :, bass.ds(ii * (2 * C) + (n + 2) * C, C)]
                                     ).then_inc(cb_in[n], 16)

            @block.gpsimd
            def _(pool):
                for t in (bd, lk, bl, wb, sab, Sb, S):
                    pool.memset(t[tuple([slice(None)] * len(t.shape))], 0.0).then_inc(zeroed, 1)
                pool.wait_ge(zeroed, 7)

                def place(dst, src, r):
                    return pool.tensor_tensor(dst, src, consts("ones")[r, None, 0:C].to_broadcast([C, H, C]), ALU.mult)

                def build(ii, n):
                    pool.wait_ge(cb_in[n], ii * 16 + 16)
                    for g in range(2):
                        for src, dst in KINDS:
                            for hh in range(2):
                                r = slice(hh * C, hh * C + C)
                                ins = place(bd[r, n, dst, half(g), r], cb[r, n, src, half(g), :], r)
                            ins.then_inc(built[g], 1)

                def turn(ii, last):
                    for n in range(2):
                        i = ii * 2 + n
                        for l in range(LV):
                            for g in range(2):
                                if l == 0:
                                    banks[g][0].taken(pool, i, "scores_b")
                                if l >= 2:
                                    banks[g][0].full(pool, i, f"W{l - 2}")
                                if l == 2:
                                    pool.wait_ge(ready[g], i + 1)
                                for hh in range(2):
                                    r = slice(hh * C, hh * C + C)
                                    m = consts("levels")[r, None, l * C:(l + 1) * C].to_broadcast([C, H, C])
                                    ins = pool.tensor_tensor(bl[r, l % 2, half(g), r], L[r, half(g), :], m, ALU.mult)
                                ins.then_inc(lev[g], 1)
                        if not (last and n == 1):
                            for g in range(2):
                                pool.wait_ge(banks[g][2].made, i * len(banks[g][2].uses) + 1)
                            build(ii + n, 1 - n)
                        for g in range(2):
                            banks[g][2].taken(pool, i, "S")
                            for hh in range(2):
                                r = slice(hh * C, hh * C + C)
                                ins = place(Sb[r, half(g), r], S[r, half(g), :], r)
                            ins.then_inc(sbuilt[g], 1)

                build(0, 0)
                with pool.Fori(0, NCH // 2 - 1) as ii:
                    turn(ii, False)
                turn(NCH // 2 - 1, True)

            @block.tensor
            def _(pe):
                for g in range(2):
                    for b in banks[g]:
                        pe.sem_inc(b.made, 1)
                    pe.sem_inc(sbuilt[g], 1)
                pe.wait_ge(zeroed, 7)
                with pe.Fori(0, NCH // 2) as ii:
                    for n in range(2):
                        i = ii * 2 + n

                        def product(g, b, name, width, terms, transpose=False):
                            bank = banks[g][b]
                            bank.free(pe, i, name)
                            for u in range(H):
                                out = bank.ps[:, u * width:(u + 1) * width]
                                for j, (lhs, rhs) in enumerate(terms):
                                    if transpose:
                                        mm = pe.transpose(out, lhs(g * H + u), consts("ident"))
                                    else:
                                        mm = pe.matmul(out, lhs(g * H + u), rhs(g * H + u), start=(j == 0),
                                                       stop=(j == len(terms) - 1))
                            mm.then_inc(bank.made, 1)

                        def blk(kind):
                            return lambda u: bd[:, n, kind, u, :]

                        for g in range(2):
                            pe.wait_ge(built[g], i * 4 + 4)
                            product(g, 0, "scores_b", P, [(blk(0), lambda u: cb[:, n, 0:2, u, :])])
                            product(g, 1, "scores_k", P, [(blk(1), lambda u: cb[:, n, 0:2, u, :])])
                        for g in range(2):
                            product(g, 2, "b_t", P, [(blk(0), None)], True)
                            product(g, 3, "k_t", P, [(blk(1), None)], True)
                        for g in range(2):
                            product(g, 2, "v_t", P, [(blk(3), None)], True)
                        for l in range(LV):
                            for g in range(2):
                                pe.wait_ge(lev[g], i * LV + (l + 1))
                                if l == 1:
                                    banks[g][0].taken(pe, i, "W0")
                                elif l > 1:
                                    banks[g][1].taken(pe, i, f"dX{l - 1}")
                                product(g, 0, f"W{l}", C, [(lambda u: bl[:, l % 2, u, :],
                                                           lambda u: X[:, u, :] if l else consts("eye2"))])
                            for g in range(2):
                                if l == 0:
                                    continue
                                banks[g][0].taken(pe, i, f"W{l}")
                                if l == 1:
                                    pe.wait_ge(ready[g], i + 1)
                                else:
                                    banks[g][2].taken(pe, i, f"dXT{l - 1}")
                                if l < LV - 1:
                                    product(g, 1, f"dX{l}", C, [(lambda u: XT[:, u, :], lambda u: wc[:, u, :])])
                                product(g, 2, f"dXT{l}", P, [(lambda u: wb[:, u, :], lambda u: XT[:, u, :])])
                        for g in range(2):
                            pe.wait_ge(sbuilt[g], i + 1)
                            banks[g][1].taken(pe, i, "scores_k")
                            banks[g][2].taken(pe, i, "v_t")
                            product(g, 3, "rhs", C, [(blk(2), lambda u: S[:, u, :]),
                                                     (lambda u: lk[:, u, :], lambda u: vc[:, u, :])])
                        for g in range(2):
                            banks[g][3].taken(pe, i, "rhs")
                            banks[g][2].taken(pe, i, f"dXT{LV - 1}")
                            product(g, 0, "sa", C, [(lambda u: XT[:, u, :], lambda u: rr[:, u, :])])
                        for g in range(2):
                            banks[g][0].taken(pe, i, "sa")
                            product(g, 1, "y", C, [(lambda u: Sb[:, u, :], lambda u: cb[:, n, 1, u, :]),
                                                   (lambda u: sab[:, u, :], lambda u: mb[:, u, :]),
                                                   (lambda u: vt[:, u, :], lambda u: mk[:, u, :])])
                            product(g, 2, "S", C, [(lambda u: bt[:, u, :], lambda u: sa[:, u, :]),
                                                   (lambda u: kt[:, u, :], lambda u: vc[:, u, :])])

            @block.scalar
            def _(act):
                act.wait_ge(zeroed, 7)

                def both_forms(g, src, compact, block_diagonal):
                    act.activation(compact[:, half(g), :], src, ACT.Copy)
                    for hh in range(2):
                        r = slice(hh * C, hh * C + C)
                        ins = act.activation(block_diagonal[r, half(g), r], src[r, :, :], ACT.Copy)
                    ins.then_inc(banks[g][0].read, 1)

                with act.Fori(0, NCH // 2) as ii:
                    for n in range(2):
                        i = ii * 2 + n

                        def take(g, b, name, dst, width):
                            banks[g][b].full(act, i, name)
                            act.activation(dst, banks[g][b].ps[:, 0:H * width].rearrange("p (u t) -> p u t", u=H),
                                           ACT.Copy).then_inc(banks[g][b].read, 1)

                        for g in range(2):
                            take(g, 2, "b_t", bt[:, half(g), :], P)
                            take(g, 3, "k_t", kt[:, half(g), :], P)
                        for g in range(2):
                            bank = banks[g][2]
                            bank.full(act, i, "v_t")
                            src = bank.ps[:, 0:H * P].rearrange("p (u t) -> p u t", u=H)
                            act.activation(vt[:, half(g), :], src, ACT.Copy)
                            for hh in range(2):
                                r = slice(hh * C, hh * C + C)
                                ins = act.activation(vc[r, half(g), :], src[r, :, r], ACT.Copy)
                            ins.then_inc(bank.read, 1)
                        for l in range(1, LV):
                            for g in range(2):
                                bank = banks[g][0]
                                bank.full(act, i, f"W{l}")
                                src = bank.ps[:, 0:H * C].rearrange("p (u t) -> p u t", u=H)
                                both_forms(g, src, wc, wb)
                        for g in range(2):
                            take(g, 3, "rhs", rr[:, half(g), :], C)
                        for g in range(2):
                            banks[g][0].full(act, i, "sa")
                            both_forms(g, banks[g][0].ps[:, 0:H * C].rearrange("p (u t) -> p u t", u=H), sa, sab)
                        for g in range(2):
                            bank = banks[g][1]
                            bank.full(act, i, "y")
                            act.activation(ys[:, half(g), bass.ds(i * C, C)],
                                           bank.ps[:, 0:H * C].rearrange("p (u t) -> p u t", u=H),
                                           ACT.Copy).then_inc(bank.read, 1)

            @block.vector
            def _(dve):
                for g in range(2):
                    for b in banks[g]:
                        dve.sem_inc(b.read, 1)
                dve.wait_ge(zeroed, 7)
                with dve.Fori(0, NCH // 2) as ii:
                    for n in range(2):
                        i = ii * 2 + n

                        def view(g, b, width):
                            return banks[g][b].ps[:, 0:H * width].rearrange("p (u t) -> p u t", u=H)

                        def mask(name, rows=slice(None)):
                            m = consts(name)[rows, None, :]
                            return m.to_broadcast([m.shape[0], H, C])

                        for g in range(2):
                            banks[g][0].full(dve, i, "scores_b")
                            src = view(g, 0, P)
                            dve.tensor_tensor(L[:, half(g), :], src[:, :, 0:C], mask("upper"), ALU.mult)
                            dve.tensor_tensor(mb[:, half(g), :], src[:, :, C:P], mask("upper_eq"),
                                              ALU.mult).then_inc(banks[g][0].read, 1)
                        for g in range(2):
                            banks[g][1].full(dve, i, "scores_k")
                            src = view(g, 1, P)
                            for hh in range(2):
                                r = slice(hh * C, hh * C + C)
                                dve.tensor_tensor(lk[r, half(g), r], src[r, :, 0:C], mask("upper", r), ALU.mult)
                            dve.tensor_tensor(mk[:, half(g), :], src[:, :, C:P], mask("upper_eq"),
                                              ALU.mult).then_inc(banks[g][1].read, 1)
                        for g in range(2):
                            dve.wait_ge(lev[g], i * LV + 1)
                            dve.tensor_tensor(XT[:, half(g), :], bl[:, 0, half(g), :],
                                              consts("ident")[:, None, :].to_broadcast([P, H, P]), ALU.add).then_inc(ready[g], 1)
                            banks[g][0].full(dve, i, "W0")
                            dve.tensor_tensor(X[:, half(g), :], view(g, 0, C), mask("eye2"), ALU.add).then_inc(banks[g][0].read, 1)
                        for l in range(1, LV):
                            for g in range(2):
                                if l < LV - 1:
                                    banks[g][1].full(dve, i, f"dX{l}")
                                    if l == 1:
                                        banks[g][0].taken(dve, i, "W0")
                                    else:
                                        banks[g][1].taken(dve, i, f"dX{l - 1}")
                                    dve.tensor_tensor(X[:, half(g), :], view(g, 1, C), X[:, half(g), :],
                                                      ALU.add).then_inc(banks[g][1].read, 1)
                                banks[g][2].full(dve, i, f"dXT{l}")
                                if l == 1:
                                    dve.wait_ge(ready[g], i + 1)
                                else:
                                    banks[g][2].taken(dve, i, f"dXT{l - 1}")
                                dve.tensor_tensor(XT[:, half(g), :], view(g, 2, P), XT[:, half(g), :],
                                                  ALU.add).then_inc(banks[g][2].read, 1)
                        for g in range(2):
                            bank = banks[g][2]
                            bank.full(dve, i, "S")
                            dve.tensor_tensor(S[:, half(g), :], view(g, 2, C), S[:, half(g), :], ALU.add).then_inc(chain[g], 1)
                            dve.wait_ge(chain[g], i + 1)
                            dve.tensor_tensor(S[:, half(g), :], S[:, half(g), :],
                                              ends[:, half(g), bass.ds(i, 1)].to_broadcast([P, H, C]),
                                              ALU.mult).then_inc(bank.read, 1)


def rwkv_output(nc, k, gate, bonus, ys):
    ps, par, consts, y = k.ps, k.par, k.consts, ys
    with ExitStack() as ctx:
        def sb(name, shape, dt=F32):
            return ctx.enter_context(nc.sbuf_tensor(name, shape, dt))

        sem = k.semaphore

        sq = sb("group_squares", [P, RC, T])
        sums, chain, mean, cen, sqd, var, lnd, root = (sem(n) for n in (
            "directions_summed", "group_chain", "group_mean", "centred", "group_squares_ready", "group_variance",
            "group_log", "group_root"))
        with nc.Block() as block:
            @block.tensor
            def _(pe):
                for n in range(RC):
                    pe.wait_ge(sums, n + 1)
                    pe.matmul(ps[:, n, :], consts("half"), y[:, n, :], start=True, stop=True).then_inc(mean, 1)
                for n in range(RC):
                    pe.wait_ge(sqd, n + 1)
                    pe.matmul(ps[:, 4 + n, :], consts("half"), sq[:, n, :], start=True, stop=True).then_inc(var, 1)

            @block.scalar
            def _(act):
                for n in range(RC):
                    act.wait_ge(cen, n + 1)
                    act.activation(sq[:, n, :], y[:, n, :], ACT.Square).then_inc(sqd, 1)
                for n in range(RC):
                    act.wait_ge(var, n + 1)
                    act.activation(sq[:, n, :], ps[:, 4 + n, :], ACT.Ln, bias=par("eps_gn"), scale=1.0 / HD).then_inc(lnd, 1)
                act.wait_ge(lnd, RC)
                for n in range(RC):
                    act.activation(sq[:, n, :], sq[:, n, :], ACT.Exp, scale=-0.5).then_inc(root, 1)

            @block.vector
            def _(dve):
                for n in range(RC):
                    dve.tensor_tensor(y[:, n, :], y[:, n, :], y[:, RC + n, ::-1], ALU.add).then_inc(sums, 1)
                for n in range(RC):
                    dve.wait_ge(mean, n + 1)
                    dve.scalar_tensor_tensor(out=y[:, n, :], in0=ps[:, n, :], scalar=-1.0 / HD, in1=y[:, n, :],
                                             op0=ALU.mult, op1=ALU.add).then_inc(cen, 1)
                link = Count(chain)
                dve.wait_ge(sqd, RC)
                for n in range(RC):
                    dve.wait_ge(root, n + 1)
                    link.inc(dve.scalar_tensor_tensor(out=y[:, n, :], in0=y[:, n, :], scalar=par("ln_w")[:, n:n + 1],
                                                      in1=sq[:, n, :], op0=ALU.mult, op1=ALU.mult))
                link.wait(dve)
                for n in range(RC):
                    link.inc(dve.scalar_tensor_tensor(out=y[:, n, :], in0=y[:, n, :], scalar=par("ln_b")[:, n:n + 1],
                                                      in1=bonus[:, n, :], op0=ALU.add, op1=ALU.add))
                link.wait(dve)
                dve.tensor_tensor(gate[:, :, :], y[:, 0:RC, :], gate[:, :, :], ALU.mult)


GLA_DK = 64
GLA_TEMP = 16.0
EXP_MAX = 80.0


def gla(nc, k, dram, out):
    dense, norm, par, ps, consts = k.dense, k.norm, k.par, k.ps, k.consts
    U = 2 * GP
    MID = C // 2 - 1
    with ExitStack() as ctx:
        def sb(name, shape, dt=F32):
            return ctx.enter_context(nc.sbuf_tensor(name, shape, dt))

        sem = k.semaphore

        gg = sb("gla_gate", [P, RC, T])
        v = sb("gla_v", [P, 2, RC, T])
        q, kx = sb("gla_q_scaled", [P, U, T]), sb("gla_k_scaled", [P, U, T])
        ends = sb("gla_chunk_decay", [P, U, NCH])
        with ExitStack() as inner:
            def sbi(name, shape, dt=F32):
                return inner.enter_context(nc.sbuf_tensor(name, shape, dt))

            xn = pair(inner, nc, "gla_in", DC)
            low = sbi("gla_low_rank", [P, T])
            up = sbi("gla_decay_up", [P, U, P])
            z = sbi("gla_z", [P, 2 * RC, T + 2])
            cv = sbi("gla_qk", [P, RC, T])
            la = sbi("log_decay", [P, U, T])
            t1 = sbi("log_decay_tail", [P, U, T])
            e = sbi("gla_decay_exps", [P, 2, 2, T])
            (zeroed, loaded, made, biased, absed, exped, tails, chain, cumd, exd, endd, conv, silu, scaled) = (
                sem(n) for n in (
                    "gla_margins_zeroed", "gla_inputs_loaded", "gla_decay_product", "gla_decay_biased", "gla_decay_abs",
                    "gla_decay_exp", "gla_decay_tail", "gla_chain", "gla_sums_ready", "gla_exps_ready",
                    "gla_ends_summed", "conv_ready", "silu_ready", "gla_scaled"))
            turns = 3
            with nc.Block() as block:
                @block.sync
                def _(sp):
                    sp.dma_start(low[:, :], dram["gla_low"]).then_inc(loaded, 16)
                    sp.dma_start(up[:, :, :], dram["gla_up"]).then_inc(loaded, 16)
                    w = dense.cursor()
                    w.run(sp, w.load, turns, BANK)

                @block.gpsimd
                def _(pool):
                    pool.memset(z[:, :, 0:1], 0.0).then_inc(zeroed, 1)
                    pool.memset(z[:, :, T + 1:T + 2], 0.0).then_inc(zeroed, 1)
                    w = dense.cursor()
                    norm.split_low(pool, xn)
                    w.run(pool, w.low, turns, BANK)

                @block.tensor
                def _(pe):
                    pe.wait_ge(loaded, 32)
                    for u in range(U):
                        pe.matmul(ps[:, 4 + u, :], up[:, u, :], low[:, :], start=True, stop=True).then_inc(made, 1)
                    w = dense.cursor()
                    w.multiply(pe, turns, lambda t: chunk(xn, t), [DC], lambda t: norm.out_wait(pe, t))

                @block.scalar
                def _(act):
                    w = dense.cursor()
                    for u in range(U):
                        act.wait_ge(made, u + 1)
                        b = par("a_b")[:, u:u + 1]
                        dst = la[:, u, :] if u < GP else la[:, u, ::-1]
                        act.activation(dst, ps[:, 4 + u, :], ACT.Identity, bias=b).then_inc(biased, 1)
                    for u in range(U):
                        act.wait_ge(biased, u + 1)
                        act.activation(t1[:, u, :], la[:, u, :], ACT.Abs).then_inc(absed, 1)
                    for u in range(U):
                        act.wait_ge(absed, u + 1)
                        act.activation(t1[:, u, :], t1[:, u, :], ACT.Exp, scale=-1.0).then_inc(exped, 1)
                    for u in range(U):
                        act.wait_ge(exped, u + 1)
                        act.activation(t1[:, u, :], t1[:, u, :], ACT.Ln, bias=1.0).then_inc(tails, 1)
                    for i in range(turns):
                        for n in range(BANK):
                            w.high(act, i, n, BANK)
                            w.full_wait(act, i, n)
                            if i < 2:
                                act.activation(z[:, i * BANK + n, 1:T + 1], dense.acc[n], ACT.Copy).then_inc(dense.free[n], 1)
                            else:
                                act.activation(gg[:, n, :], dense.acc[n], ACT.Silu).then_inc(dense.free[n], 1)
                    for m in range(2 * RC):
                        act.wait_ge(conv, 3 * (m + 1))
                        dst = cv[:, m, :] if m < RC else v[:, 0, m - RC, :]
                        act.activation(dst, dst, ACT.Silu).then_inc(silu, 1)
                    act.wait_ge(endd, 2)
                    act.activation(ends[:, :, :], ends[:, :, :], ACT.Exp, scale=1.0 / GLA_TEMP)
                    for u in range(U):
                        if u >= 2:
                            act.wait_ge(scaled, 2 * (u - 1))
                        act.wait_ge(cumd, 2 * U + u + 1)
                        for j, sc in enumerate((1.0 / GLA_TEMP, -1.0 / GLA_TEMP)):
                            act.activation(e[:, u % 2, j, :], la[:, u, :], ACT.Exp, scale=sc).then_inc(exd, 1)

                @block.vector
                def _(dve):
                    w = dense.cursor()
                    norm.scale_split(dve, k.h, xn, par("g_mix_pre"))
                    for u in range(U):
                        dve.wait_ge(tails, u + 1)
                        dve.scalar_tensor_tensor(out=t1[:, u, :], in0=la[:, u, :], scalar=0.0, in1=t1[:, u, :],
                                                 op0=ALU.min, op1=ALU.subtract).then_inc(cumd, 1)
                    for u in range(U):
                        dve.wait_ge(cumd, u + 1)
                        dve.tensor_tensor_scan(la[:, u, :], consts("chunk_start"), t1[:, u, :], 0.0,
                                               ALU.mult, ALU.add).then_inc(cumd, 1)
                    dve.wait_ge(cumd, 2 * U)
                    dve.tensor_tensor(ends[:, :, :], la[:, :, C - 1::C], la[:, :, MID::C], ALU.subtract).then_inc(endd, 1)
                    dve.wait_ge(endd, 1)
                    dve.tensor_tensor(ends[:, :, 0:NCH - 1], ends[:, :, 0:NCH - 1], la[:, :, C + MID::C],
                                      ALU.add).then_inc(endd, 1)
                    link = Count(chain)
                    for u in range(U):
                        ch = la[:, u, :].rearrange("p (c t) -> p c t", c=NCH)
                        t1c = t1[:, u, :].rearrange("p (c t) -> p c t", c=NCH)
                        link.inc(dve.tensor_tensor(t1c, ch, ch[:, :, MID:MID + 1].to_broadcast([P, NCH, C]), ALU.subtract))
                    link.wait(dve)
                    dve.wait_ge(endd, 2)
                    for u in range(U):
                        dve.tensor_scalar(la[:, u, :], t1[:, u, :], EXP_MAX * GLA_TEMP, -EXP_MAX * GLA_TEMP,
                                          ALU.min, ALU.max).then_inc(cumd, 1)
                    dve.wait_ge(zeroed, 2)
                    for m in range(2 * RC):
                        n = m % BANK
                        dve.wait_ge(dense.free[n], w.read_value(m // BANK, n))
                        dst = cv[:, m, :] if m < RC else v[:, 0, m - RC, :]
                        dve.tensor_scalar(dst, z[:, m, 0:T], par("conv0")[:, m:m + 1], None, ALU.mult).then_inc(conv, 1)
                        for j in (1, 2):
                            dve.wait_ge(conv, 3 * m + j)
                            dve.scalar_tensor_tensor(out=dst, in0=z[:, m, j:T + j], scalar=par(f"conv{j}")[:, m:m + 1],
                                                     in1=dst, op0=ALU.mult, op1=ALU.add).then_inc(conv, 1)
                    for u in range(U):
                        time = slice(None) if u < GP else slice(None, None, -1)
                        p = u % GP
                        dve.wait_ge(exd, 2 * (u + 1))
                        dve.wait_ge(silu, RC)
                        dve.scalar_tensor_tensor(out=q[:, u, :], in0=cv[:, p, time], scalar=GLA_DK ** -0.5,
                                                 in1=e[:, u % 2, 0, :], op0=ALU.mult, op1=ALU.mult).then_inc(scaled, 1)
                        dve.tensor_tensor(kx[:, u, :], cv[:, GP + p, time], e[:, u % 2, 1, :], ALU.mult).then_inc(scaled, 1)
                    dve.wait_ge(silu, 2 * RC)
                    for n in range(RC):
                        dve.tensor_copy(v[:, 1, n, ::-1], v[:, 0, n, :])
            norm.close(split=True, again=True)
            dense.close(turns * BANK, turns * BANK)

        ob = sb("gla_directions", [P, 2, RC, T])
        gla_scan(nc, k, q, kx, v, ends, ob)
        gla_output(nc, k, ob, gg, out)


def gla_scan(nc, k, q, kx, v, ends, ob):
    consts = k.consts
    U, H = 2 * GP, GP
    with ExitStack() as ctx:
        def sb(name, shape, dt=F32):
            return ctx.enter_context(nc.sbuf_tensor(name, shape, dt))

        sem = k.semaphore

        bd = sb("gla_block_diagonal", [P, 2, U, P])
        vx = sb("gla_v_chunk", [P, U, P])
        pb = sb("gla_weights", [P, U, P])
        kv = sb("gla_k_v_by_token", [P, 2, 2, H, P])
        S = sb("gla_state", [P, U, P])
        zeroed = sem("gla_block_diagonals_zeroed")
        built = [sem(f"gla_vectors_built{g}") for g in range(2)]
        vbuilt = [sem(f"gla_v_chunk_copied{g}") for g in range(2)]
        chain = [sem(f"gla_state_chain{g}") for g in range(2)]
        banks = [[Bank(k, "gla", 4 * g + b, [(name, 1)]) for b, name in enumerate(("scores", "turned", "o", "S"))]
                 for g in range(2)]

        def half(g):
            return slice(g * H, g * H + H)

        with nc.Block() as block:
            @block.gpsimd
            def _(pool):
                for t in (bd, pb, S):
                    pool.memset(t[tuple([slice(None)] * len(t.shape))], 0.0).then_inc(zeroed, 1)
                pool.wait_ge(zeroed, 3)
                with pool.Fori(0, NCH) as i:
                    for g in range(2):
                        pool.wait_ge(banks[g][3].made, i + 1)
                        for src, dst in ((kx, 0), (q, 1)):
                            for hh in range(2):
                                r = slice(hh * C, hh * C + C)
                                pool.tensor_copy(bd[r, dst, half(g), r], src[r, half(g), bass.ds(i * C, C)]).then_inc(built[g], 1)

            @block.tensor
            def _(pe):
                for g in range(2):
                    for b in banks[g]:
                        pe.sem_inc(b.made, 1)
                pe.wait_ge(zeroed, 3)
                with pe.Fori(0, NCH) as i:
                    for g in range(2):
                        sc, tr = banks[g][0], banks[g][1]
                        pe.wait_ge(built[g], i * 4 + 4)
                        pe.wait_ge(vbuilt[g], i + 1)
                        sc.free(pe, i, "scores")
                        for u in range(H):
                            mm = pe.matmul(sc.ps[:, u * C:(u + 1) * C], bd[:, 0, g * H + u, :],
                                           q[:, g * H + u, bass.ds(i * C, C)], start=True, stop=True)
                        mm.then_inc(sc.made, 1)
                        tr.free(pe, i, "turned")
                        for j, src in enumerate((bd[:, 0, half(g), :], vx[:, half(g), :])):
                            for u in range(H):
                                mm = pe.transpose(tr.ps[:, (j * H + u) * P:(j * H + u + 1) * P], src[:, u, :], consts("ident"))
                        mm.then_inc(tr.made, 1)
                    for g in range(2):
                        sc, tr, o, st = banks[g]
                        sc.taken(pe, i, "scores")
                        tr.taken(pe, i, "turned")
                        o.free(pe, i, "o")
                        st.free(pe, i, "S")
                        for u in range(H):
                            w = g * H + u
                            pe.matmul(o.ps[:, u * P:(u + 1) * P], S[:, w, :], bd[:, 1, w, :], start=True, stop=False)
                            mm = pe.matmul(o.ps[:, u * P:(u + 1) * P], kv[:, g, 1, u, :], pb[:, w, :], start=False, stop=True)
                        mm.then_inc(o.made, 1)
                        for u in range(H):
                            mm = pe.matmul(st.ps[:, u * P:(u + 1) * P], kv[:, g, 0, u, :], kv[:, g, 1, u, :], start=True, stop=True)
                        mm.then_inc(st.made, 1)

            @block.scalar
            def _(act):
                with act.Fori(0, NCH) as i:
                    for g in range(2):
                        act.activation(vx[:, half(g), :].rearrange("p u (h t) -> p (u h) t", h=2),
                                       v[:, g, :, bass.ds(i * C, C)], ACT.Copy).then_inc(vbuilt[g], 1)
                    for g in range(2):
                        tr = banks[g][1]
                        tr.full(act, i, "turned")
                        act.activation(kv[:, g, :, :, :].rearrange("p a u t -> p (a u t)"), tr.ps, ACT.Copy).then_inc(tr.read, 1)
                    for g in range(2):
                        o = banks[g][2]
                        o.full(act, i, "o")
                        act.activation(ob[:, g, :, bass.ds(i * C, C)], o.ps[:, 0:2 * H * C].rearrange("p (h t) -> p h t", t=C),
                                       ACT.Copy).then_inc(o.read, 1)

            @block.vector
            def _(dve):
                for g in range(2):
                    for b in banks[g]:
                        dve.sem_inc(b.read, 1)
                dve.wait_ge(zeroed, 3)
                with dve.Fori(0, NCH) as i:
                    for g in range(2):
                        sc = banks[g][0]
                        sc.full(dve, i, "scores")
                        for hh in range(2):
                            r = slice(hh * C, hh * C + C)
                            m = consts("upper_eq")[r, None, :].to_broadcast([C, H, C])
                            ins = dve.tensor_tensor(pb[r, half(g), r], sc.ps[r, 0:H * C].rearrange("p (u t) -> p u t", u=H),
                                                    m, ALU.mult)
                        ins.then_inc(sc.read, 1)
                    for g in range(2):
                        st = banks[g][3]
                        st.full(dve, i, "S")
                        src = st.ps[:, 0:H * P].rearrange("p (u t) -> p u t", u=H)
                        dve.tensor_tensor(S[:, half(g), :], src, S[:, half(g), :], ALU.add).then_inc(chain[g], 1)
                        dve.wait_ge(chain[g], i + 1)
                        dve.tensor_tensor(S[:, half(g), :], S[:, half(g), :],
                                          ends[:, half(g), bass.ds(i, 1)].to_broadcast([P, H, P]), ALU.mult).then_inc(st.read, 1)


def gla_output(nc, k, ob, gg, out):
    ps, par, consts = k.ps, k.par, k.consts
    with ExitStack() as ctx:
        sq = ctx.enter_context(nc.sbuf_tensor("gla_squares", [P, RC, T], F32))
        sums, sqd, var, lnd, root, gained = (k.semaphore(n) for n in (
            "gla_directions_summed", "gla_squares_ready", "gla_squares_summed", "gla_log", "gla_root", "gla_normed"))
        with nc.Block() as block:
            @block.tensor
            def _(pe):
                for n in range(RC):
                    pe.wait_ge(sqd, n + 1)
                    pe.matmul(ps[:, n, :], consts("ones"), sq[:, n, :], start=True, stop=True).then_inc(var, 1)

            @block.scalar
            def _(act):
                for n in range(RC):
                    act.wait_ge(sums, n + 1)
                    act.activation(sq[:, n, :], out[:, n, :], ACT.Square).then_inc(sqd, 1)
                for n in range(RC):
                    act.wait_ge(var, n + 1)
                    act.activation(sq[:, n, :], ps[:, n, :], ACT.Ln, bias=par("eps6"), scale=1.0 / P).then_inc(lnd, 1)
                for n in range(RC):
                    act.wait_ge(lnd, n + 1)
                    act.activation(sq[:, n, :], sq[:, n, :], ACT.Exp, scale=-0.5).then_inc(root, 1)

            @block.vector
            def _(dve):
                for n in range(RC):
                    dve.tensor_tensor(out[:, n, :], ob[:, 0, n, :], ob[:, 1, n, ::-1], ALU.add).then_inc(sums, 1)
                dve.wait_ge(sqd, RC)
                for n in range(RC):
                    dve.wait_ge(root, n + 1)
                    dve.scalar_tensor_tensor(out=out[:, n, :], in0=out[:, n, :], scalar=par("gla_norm"), in1=sq[:, n, :],
                                             op0=ALU.mult, op1=ALU.mult).then_inc(gained, 1)
                for n in range(RC):
                    dve.wait_ge(gained, n + 1)
                    dve.tensor_tensor(out[:, n, :], out[:, n, :], gg[:, n, :], ALU.mult)


def feed_forward(nc, k, dram):
    dense, norm, par, h = k.dense, k.norm, k.par, k.h
    with ExitStack() as ctx:
        f = pair(ctx, nc, "ffn_hidden", FFC)
        turns = FFC // 2
        with ExitStack() as inner:
            xn = pair(inner, nc, "ffn_in", DC)
            sg = inner.enter_context(nc.sbuf_tensor("ffn_silu", [P, 2, T], F32))
            tmp = inner.enter_context(nc.sbuf_tensor("ffn_hidden_full", [P, 2, T], F32))
            rounded, split = k.semaphore("ffn_hidden_rounded"), k.semaphore("ffn_hidden_split")
            with nc.Block() as block:
                @block.sync
                def _(sp):
                    w = dense.cursor()
                    w.run(sp, w.load, turns, BANK)

                @block.gpsimd
                def _(pool):
                    w = dense.cursor()
                    norm.split_low(pool, xn)
                    w.run(pool, w.low, turns, BANK)

                @block.scalar
                def _(act):
                    w = dense.cursor()
                    norm.squares(act, h)
                    norm.roots(act, par("eps6"))
                    with act.Fori(0, turns) as i:
                        for j in range(2):
                            w.high(act, i, 2 * j, BANK)
                            w.full_wait(act, i, 2 * j)
                            w.free_wait(act, i, 2 * j + 1)
                            act.activation(sg[:, j, :], dense.acc[2 * j], ACT.Silu).then_inc(dense.free[2 * j], 1)
                            w.high(act, i, 2 * j + 1, BANK)

                @block.vector
                def _(dve):
                    w = dense.cursor()
                    norm.ready(dve)
                    norm.scale_split(dve, h, xn, par("g_ffn_pre"))
                    with dve.Fori(0, turns) as i:
                        for j in range(2):
                            up, m = 2 * j + 1, i * 2 + j
                            dve.wait_ge(dense.free[2 * j], w.read_value(i, 2 * j))
                            w.full_wait(dve, i, up)
                            dve.tensor_tensor(f[0][:, m, :], dense.acc[up], sg[:, j, :], ALU.mult).then_inc(rounded, 1)
                            dve.tensor_tensor(tmp[:, j, :], dense.acc[up], sg[:, j, :], ALU.mult).then_inc(dense.free[up], 1)
                            dve.wait_ge(rounded, i * 2 + (j + 1))
                            dve.wait_ge(dense.free[up], w.read_value(i, up))
                            dve.tensor_tensor(f[1][:, m, :], tmp[:, j, :], f[0][:, m, :].bitcast(F32),
                                              ALU.subtract).then_inc(split, 1)

                @block.tensor
                def _(pe):
                    norm.sums(pe)
                    w = dense.cursor()
                    w.multiply(pe, turns, lambda t: chunk(xn, t), [DC], lambda t: norm.out_wait(pe, t))
            norm.close(split=True)
            dense.close(turns * BANK, turns * BANK)
        u = ctx.enter_context(nc.sbuf_tensor("ffn_out", [P, DC, T], F32))
        projected(nc, k, 2, lambda t: chunk(f, t), [DC, DC, FFC - 2 * DC], u, "g_ffn_post")


def layer_embedding(nc, k, dram):
    dense, norm, par, h = k.dense, k.norm, k.par, k.h
    with ExitStack() as ctx:
        PC = 2
        UNITS = DC // PC
        pt = ctx.enter_context(nc.sbuf_tensor("embedding_in", [P, PC, T], F32))
        pp, hp = pair(ctx, nc, "embedding_in_split", PC), pair(ctx, nc, "residual_split", DC)
        e = ctx.enter_context(nc.sbuf_tensor("embedding", [P, DC, T], F32))
        s = ctx.enter_context(nc.sbuf_tensor("embedding_gate", [P, DC, T], F32))
        loaded, gated, part, split = (k.semaphore(n) for n in (
            "embedding_loaded", "embedding_gated", "embedding_parts", "embedding_split"))
        with nc.Block() as block:
            @block.sync
            def _(sp):
                sp.dma_start(pt[:, :, :], dram["p"]).then_inc(loaded, 16)
                w = dense.cursor()
                w.run(sp, w.load, 1, DC // UNITS)
                w.run(sp, w.load, 2, BANK)

            @block.gpsimd
            def _(pool):
                w = dense.cursor()
                split_lows(pool, PC, pp, norm.tmp, part, 0, split)
                split_lows(pool, DC, hp, norm.tmp, part, 2 * PC, split)
                w.run(pool, w.low, 1, DC // UNITS)
                w.run(pool, w.low, 2, BANK)

            @block.scalar
            def _(act):
                w = dense.cursor()
                for m in range(DC):
                    if m % UNITS == 0:
                        w.high(act, 0, m // UNITS, DC // UNITS)
                    act.wait_ge(dense.used, w.slots + m // UNITS + 1)
                    act.activation(e[:, m, :], dense.acc[m % BANK], ACT.Copy).then_inc(dense.free[m % BANK], 1)
                w.advance(DC // UNITS, DC)
                for i in range(2):
                    for n in range(BANK):
                        m = i * BANK + n
                        w.high(act, i, n, BANK)
                        w.full_wait(act, i, n)
                        act.activation(s[:, m, :], dense.acc[n], ACT.Sigmoid, bias=par("b_ple")[:, m:m + 1]).then_inc(dense.free[n], 1)
                for m in range(DC):
                    act.wait_ge(gated, m + 1)
                norm.squares(act, e)
                norm.roots(act, par("eps6"))

            @block.vector
            def _(dve):
                w = dense.cursor()
                w.advance(DC // UNITS, DC)
                dve.wait_ge(loaded, 16)
                split_chunks(dve, lambda t, out: dve.tensor_copy(out, pt[:, t, :]), PC, pp, norm.tmp, part, 0, split, 0)
                split_chunks(dve, lambda t, out: dve.tensor_copy(out, h[:, t, :]), DC, hp, norm.tmp, part, 2 * PC, split, PC)
                for m in range(DC):
                    i, n = divmod(m, BANK)
                    dve.wait_ge(dense.free[n], w.read_value(i, n))
                    dve.tensor_tensor(e[:, m, :], e[:, m, :], s[:, m, :], ALU.mult).then_inc(gated, 1)
                norm.scale(dve, e, e, par("g_ple"), add=h)

            @block.tensor
            def _(pe):
                w = dense.cursor()
                w.packed(pe, DC, lambda t: chunk(pp, t), PC, lambda t: pe.wait_ge(split, t + 1))
                w.multiply(pe, 2, lambda t: chunk(hp, t), [DC], lambda t: pe.wait_ge(split, PC + t + 1))
                norm.sums(pe)
        norm.close(add=True)
        dense.close(DC // UNITS + DC, 2 * DC)


class Columns:

    def __init__(self, tile, where, first=0):
        self.tile, self.where, self.first = tile, where, first

    def __call__(self, name):
        at, n = self.where[name]
        return self.tile[:, at - self.first:at - self.first + n]


def build(nc, dram, param_at, const_at, out):
    k = Kernel(nc)
    k.dram = dram
    with ExitStack() as ctx:
        def sb(name, shape, dt=F32):
            return ctx.enter_context(nc.sbuf_tensor(name, shape, dt))

        k.boot = ctx.enter_context(nc.semaphore("tables_loaded"))
        k.ps = ctx.enter_context(nc.psum_tensor("psum", [P, 8, T], F32))
        k.h = sb("residual_stream", [P, DC, T])
        n_par = sum(w for _, w in param_at.values())
        n_const = sum(w for _, w in const_at.values())
        first = const_at["ident"][0]
        k.par = Columns(sb("params", [P, n_par])[:, :], param_at)
        k.consts = Columns(sb("tables", [P, n_const - first])[:, :], const_at, first)
        k.dense = Dense(ctx, nc, k.ps, dram["weights"])
        k.norm = Norm(ctx, nc, k.ps, k.consts("ones"))
        first_mixer(nc, k, dram)
        experts(nc, k, dram)
        norm_in_place(nc, k, "g_final", "eps5")
        k.clear_semaphores()
        second_mixer(nc, k, dram)
        feed_forward(nc, k, dram)
        layer_embedding(nc, k, dram)
        stored = ctx.enter_context(nc.semaphore("output_stored"))
        with nc.Block() as block:
            @block.sync
            def _(sp):
                sp.dma_start(out, k.h[:, :, :]).then_inc(stored, 16)
                sp.wait_ge(stored, 16)


def kernel(**inputs):
    from concourse.bass_utils import run_bass_kernel_spmd
    import concourse.bacc as bacc

    a = {n: np.asarray(v) for n, v in inputs.items()}
    param_at, params = layout_params(a)
    const_at, consts = layout_constants()
    w_in = a["w_in"][0]
    qw, kw = NH * HD, NKV * HD
    o_pool = qw + 2 * kw
    o_ga = o_pool + len(PW) * P
    wk = [w_in[:, qw + v * HD:qw + (v + 1) * HD] for v in range(NKV)]
    w_z = np.concatenate([w_in[:, 0:qw], w_in[:, o_ga:], w_in[:, o_pool:o_ga], wk[0], wk[0], wk[1], wk[1],
                          w_in[:, qw + kw:o_pool]], 1)
    arrays = {
        "x": np.ascontiguousarray(a["x"][0].T.reshape(DC, P, T).transpose(1, 0, 2)),
        "params": params, "consts": consts,
        "w_group": np.ascontiguousarray(a["w_pool_grp"][0].transpose(1, 0, 2)),
    }
    stream = [tiles(w_z), tiles(a["w_attn_up"][0]), packed_tiles(a["w_pool_up"][0]), tiles(a["w_o"][0]),
              tiles(a["w_query"][0])]
    arrays["sub_keys"] = np.ascontiguousarray(a["sub_keys"][0].reshape(2 * PH, NK, P).transpose(2, 0, 1))
    u = tiles(a["u_experts"][0].T).reshape(NG, GI, P, D)
    v = (a["v_experts"][0].reshape(NG, 2, GI // 2, P, DC, P).transpose(0, 4, 1, 3, 2, 5).reshape(NG, 2 * DC, P, D))
    stream.append(np.concatenate([u, v], 1).reshape(-1, P, D))
    w2 = a["w_in_2"][0]
    rw = 13 * P + 64
    gl = rw + P
    wide = 2 * GP * P + RC * P
    w_rwkv = np.zeros((D, 16 * P), np.float32)
    w_rwkv[:, 0:rw] = w2[:, 0:rw]
    w_rwkv[:, 14 * P:15 * P] = w2[:, rw:gl]
    low = gl + wide + RC * P
    for d in range(2):
        w_rwkv[:, 15 * P + 32 * d:15 * P + 32 * d + 16] = w2[:, low + 16 * d:low + 16 * d + 16]
    stream += [tiles(w_rwkv), tiles(w2[:, gl:low])]
    w_up = np.zeros((P, 2, RC * P), np.float32)
    gla_up = np.zeros((P, 2, GP * P), np.float32)
    for d in range(2):
        w_up[64 * d:64 * d + 64, d] = a["rwkv_w_up_2"][0, d]
        gla_up[32 * d:32 * d + 16, d] = a["gla_a_up_2"][0, d]
    a_up = np.zeros((P, RC * P), np.float32)
    a_up[0:64] = a["rwkv_a_up_2"][0]
    arrays["w_up"], arrays["a_up"] = w_up, a_up
    arrays["g_up"] = np.ascontiguousarray(a["rwkv_g_up_2"][0])
    arrays["gla_up"] = gla_up.reshape(P, 2 * GP, P)
    stream.append(tiles(a["w_out_2"][0]))
    gate, up = tiles(a["ffn_gate_2"][0]), tiles(a["ffn_up_2"][0])
    stream.append(np.stack([gate, up], 1).reshape(2 * FFC, P, D))
    down = np.zeros((DC, P, 3 * D), np.float32)
    down[:, :, 0:FFC * P] = tiles(a["ffn_down_2"][0])
    stream.append(down.reshape(DC, P, 3, D).transpose(0, 2, 1, 3).reshape(3 * DC, P, D))
    stream += [packed_tiles(a["ple_proj_2"][0]), tiles(a["ple_gate_2"][0])]
    arrays["weights"] = np.concatenate(stream, 0)
    arrays["p"] = np.ascontiguousarray(a["p_2"][0, 0].T.reshape(2, P, T).transpose(1, 0, 2))
    nc = bacc.Bacc("TRN2", target_bir_lowering=False, num_devices=1)
    dram = {n: nc.dram_tensor(f"in_{n}", v.shape, F32, kind="ExternalInput").ap() for n, v in arrays.items()}
    at, n = const_at["inv_count"]
    dram["inv_count"] = dram["consts"][:, at:at + n].rearrange("p (g t) -> p g t", g=len(PW))
    dram["table"] = nc.dram_tensor("coefficient_table", (NTB, P, NK * TB), F32, kind="Internal").ap()
    dram["gla_low"] = nc.dram_tensor("gla_low_copy", (P, T), F32, kind="Internal").ap()
    dram["scan"] = nc.dram_tensor("scan_vectors", (P, 5, 2 * RC, T), F32, kind="Internal").ap()
    out = nc.dram_tensor("out", (P, DC, T), F32, kind="ExternalOutput").ap()
    build(nc, dram, param_at, const_at, out)
    r = run_bass_kernel_spmd(nc, [{f"in_{n}": v for n, v in arrays.items()}], core_ids=[0])
    return r.results[0]["out"].transpose(1, 0, 2).reshape(D, T).T.reshape(1, T, D)
```
